# Optimizing a Trainium2 kernel written in Bass

```python
import math
import jax, jax.numpy as jnp
from jax import lax
import numpy as np

D_MODEL = 1024
BATCH = 1
SEQ = 256
DEPTH = 2

ATTN_HEADS = 16
ATTN_KV_HEADS = 4
ATTN_GROUP = ATTN_HEADS // ATTN_KV_HEADS
ATTN_HEAD_DIM = 64
ATTN_Q_DIM = ATTN_HEADS * ATTN_HEAD_DIM
ATTN_KV_DIM = ATTN_KV_HEADS * ATTN_HEAD_DIM
ATTN_IN_DIM = ATTN_Q_DIM + 2 * ATTN_KV_DIM
WINDOW = 128
ATTN_BLOCK = 128
ROPE_DIM = ATTN_HEAD_DIM // 4
ROPE_THETA = 500000.0

GDN_QK_HEADS = 8
GDN_V_HEADS = 16
GDN_HEAD_K = 128
GDN_HEAD_V = 128
GDN_CONV = 4
GDN_CHUNK = 64
GDN_KEY_DIM = GDN_QK_HEADS * GDN_HEAD_K
GDN_VAL_DIM = GDN_V_HEADS * GDN_HEAD_V
GDN_QKV_DIM = 2 * GDN_KEY_DIM + GDN_VAL_DIM
GDN_IN_DIM = GDN_QKV_DIM + GDN_VAL_DIM + 2 * GDN_V_HEADS

D_FF = 3 * D_MODEL
FFN_CONV = 3

N_ATTN_LAYERS = (DEPTH + 1) // 2
N_GDN_LAYERS = DEPTH // 2
EPS = 1e-6


def rms_norm(x, gain):
    xf = x.astype(jnp.float32)
    y = xf * lax.rsqrt(jnp.mean(xf * xf, axis=-1, keepdims=True) + EPS)
    return (y * gain.astype(jnp.float32)).astype(x.dtype)

def l2_norm(x):
    return x * lax.rsqrt(jnp.sum(x * x, axis=-1, keepdims=True) + EPS)

def causal_dwconv(x, w):
    k = w.shape[0]
    return lax.conv_general_dilated(
        x, w[:, None, :].astype(x.dtype), window_strides=(1,), padding=[(k - 1, 0)],
        dimension_numbers=("NWC", "WIO", "NWC"), feature_group_count=x.shape[-1])

def rope_tables(positions):
    inv_freq = ROPE_THETA ** (-jnp.arange(0, ROPE_DIM, 2, dtype=jnp.float32) / ROPE_DIM)
    ang = positions.astype(jnp.float32)[..., None] * inv_freq
    return jnp.cos(ang)[:, :, None, :], jnp.sin(ang)[:, :, None, :]

def partial_rope(x, cos, sin):
    cos = cos.astype(x.dtype)
    sin = sin.astype(x.dtype)
    half = ROPE_DIM // 2
    x1, x2, xp = x[..., :half], x[..., half:ROPE_DIM], x[..., ROPE_DIM:]
    return jnp.concatenate([x1 * cos - x2 * sin, x2 * cos + x1 * sin, xp], axis=-1)

def swa_sink_attention(u, w_in, q_gain, k_gain, sinks, w_out, cos, sin):
    B, S, _ = u.shape
    nb = S // ATTN_BLOCK
    blk, hkv, g, hd = ATTN_BLOCK, ATTN_KV_HEADS, ATTN_GROUP, ATTN_HEAD_DIM
    qkv = u @ w_in
    q = qkv[..., :ATTN_Q_DIM].reshape(B, S, ATTN_HEADS, hd)
    k = qkv[..., ATTN_Q_DIM:ATTN_Q_DIM + ATTN_KV_DIM].reshape(B, S, hkv, hd)
    v = qkv[..., ATTN_Q_DIM + ATTN_KV_DIM:].reshape(B, S, hkv, hd)
    q = partial_rope(rms_norm(q, q_gain), cos, sin)
    k = partial_rope(rms_norm(k, k_gain), cos, sin)
    qb = q.reshape(B, nb, blk, hkv, g, hd)

    def band(t):
        prev = jnp.pad(t, ((0, 0), (blk, 0), (0, 0), (0, 0)))[:, :S]
        return jnp.concatenate([prev.reshape(B, nb, blk, hkv, hd),
                                t.reshape(B, nb, blk, hkv, hd)], axis=2)

    kb, vb = band(k), band(v)
    scores = jnp.einsum("bnqhgd,bnkhd->bnhgqk", qb, kb,
                        preferred_element_type=jnp.float32) * (hd ** -0.5)
    dist = jnp.arange(blk)[:, None] + blk - jnp.arange(2 * blk)[None, :]
    in_window = (dist >= 0) & (dist < WINDOW)
    key_pos = jnp.arange(nb)[:, None] * blk - blk + jnp.arange(2 * blk)[None, :]
    mask = in_window[None] & (key_pos >= 0)[:, None, :]
    scores = jnp.where(mask[None, :, None, None], scores, jnp.finfo(jnp.float32).min)
    sink = jnp.broadcast_to(sinks.astype(jnp.float32).reshape(1, 1, hkv, g, 1, 1),
                            scores.shape[:-1] + (1,))
    probs = jax.nn.softmax(jnp.concatenate([scores, sink], axis=-1), axis=-1)[..., :-1]
    out = jnp.einsum("bnhgqk,bnkhd->bnqhgd", probs.astype(vb.dtype), vb)
    return out.reshape(B, S, ATTN_Q_DIM) @ w_out

def chunk_gated_delta_rule(q, k, v, g, beta):
    out_dtype = v.dtype
    B, S, H, DK = q.shape
    DV = v.shape[-1]
    C = GDN_CHUNK
    nc = S // C
    f32 = jnp.float32

    def chunks(t):
        t = t.astype(f32).reshape((B, nc, C, H) + t.shape[3:])
        return jnp.moveaxis(t, 3, 1)

    q, k, v, g, beta = chunks(q), chunks(k), chunks(v), chunks(g), chunks(beta)
    gc = jnp.cumsum(g, axis=-1)
    incl = jnp.tril(jnp.ones((C, C), dtype=bool))
    strict = jnp.tril(jnp.ones((C, C), dtype=bool), k=-1)
    decay = jnp.exp(jnp.where(incl, gc[..., :, None] - gc[..., None, :], -jnp.inf))
    kk = jnp.einsum("bhncd,bhnsd->bhncs", k, k)
    m = jnp.where(strict, beta[..., :, None] * kk * decay, 0.0)
    a = m + jnp.eye(C, dtype=f32)
    rhs = jnp.concatenate([v * beta[..., None], k * (beta * jnp.exp(gc))[..., None]], axis=-1)
    sol = lax.linalg.triangular_solve(a, rhs, left_side=True, lower=True, unit_diagonal=True)
    u, w = sol[..., :DV], sol[..., DV:]
    qk = jnp.where(incl, jnp.einsum("bhncd,bhnsd->bhncs", q, k) * decay, 0.0)
    q_dec = q * jnp.exp(gc)[..., None]
    k_dec = k * jnp.exp(gc[..., -1:] - gc)[..., None]
    g_last = jnp.exp(gc[..., -1])

    def step(state, inp):
        u_c, w_c, qk_c, qd_c, kd_c, gl_c = inp
        v_new = u_c - jnp.einsum("bhcd,bhde->bhce", w_c, state)
        o = jnp.einsum("bhcd,bhde->bhce", qd_c, state) + jnp.einsum("bhcs,bhse->bhce", qk_c, v_new)
        state = state * gl_c[..., None, None] + jnp.einsum("bhcd,bhce->bhde", kd_c, v_new)
        return state, o

    xs = tuple(jnp.moveaxis(t, 2, 0) for t in (u, w, qk, q_dec, k_dec, g_last))
    _, o = lax.scan(step, jnp.zeros((B, H, DK, DV), f32), xs)
    o = jnp.transpose(o, (1, 0, 3, 2, 4)).reshape(B, S, H, DV)
    return o.astype(out_dtype)

def gated_deltanet(u, w_in, conv_w, a_log, dt_bias, norm_gain, w_out):
    B, S, _ = u.shape
    proj = u @ w_in
    qkv = jax.nn.silu(causal_dwconv(proj[..., :GDN_QKV_DIM], conv_w))
    z = proj[..., GDN_QKV_DIM:GDN_QKV_DIM + GDN_VAL_DIM].reshape(B, S, GDN_V_HEADS, GDN_HEAD_V)
    b = proj[..., GDN_QKV_DIM + GDN_VAL_DIM:GDN_QKV_DIM + GDN_VAL_DIM + GDN_V_HEADS]
    a = proj[..., GDN_QKV_DIM + GDN_VAL_DIM + GDN_V_HEADS:]
    rep = GDN_V_HEADS // GDN_QK_HEADS
    q = qkv[..., :GDN_KEY_DIM].reshape(B, S, GDN_QK_HEADS, GDN_HEAD_K).astype(jnp.float32)
    k = qkv[..., GDN_KEY_DIM:2 * GDN_KEY_DIM].reshape(B, S, GDN_QK_HEADS, GDN_HEAD_K).astype(jnp.float32)
    v = qkv[..., 2 * GDN_KEY_DIM:].reshape(B, S, GDN_V_HEADS, GDN_HEAD_V)
    q = jnp.repeat(l2_norm(q) * (GDN_HEAD_K ** -0.5), rep, axis=2)
    k = jnp.repeat(l2_norm(k), rep, axis=2)
    beta = jax.nn.sigmoid(b.astype(jnp.float32))
    g = -jnp.exp(a_log.astype(jnp.float32)) * jax.nn.softplus(
        a.astype(jnp.float32) + dt_bias.astype(jnp.float32))
    o = chunk_gated_delta_rule(q, k, v, g, beta)
    o = rms_norm(o, norm_gain) * jax.nn.silu(z)
    return o.reshape(B, S, GDN_VAL_DIM) @ w_out

def conv_glu_ffn(u, w_up, conv_w, conv_b, w_down):
    gu = u @ w_up
    gate = causal_dwconv(gu[..., :D_FF], conv_w) + conv_b
    return (jax.nn.silu(gate) * gu[..., D_FF:]) @ w_down

def first_inputs(seed: int = 0) -> dict:
    key = jax.random.key(seed)
    ks = jax.random.split(key, 24)
    f32 = jnp.float32

    def nrm(k, shape, scale):
        return jax.random.normal(k, shape, f32) * scale

    x = nrm(ks[0], (BATCH, SEQ, D_MODEL), 1.0)
    start = jax.random.randint(ks[1], (BATCH, 1), 0, 4096, dtype=jnp.int32)
    positions = start + jnp.arange(SEQ, dtype=jnp.int32)[None, :]
    mixer_norm = 1.0 + nrm(ks[2], (DEPTH, D_MODEL), 0.05)
    ffn_norm = 1.0 + nrm(ks[3], (DEPTH, D_MODEL), 0.05)

    attn_w_in = nrm(ks[4], (N_ATTN_LAYERS, D_MODEL, ATTN_IN_DIM), D_MODEL ** -0.5)
    attn_q_gain = 1.0 + nrm(ks[5], (N_ATTN_LAYERS, ATTN_HEAD_DIM), 0.05)
    attn_k_gain = 1.0 + nrm(ks[6], (N_ATTN_LAYERS, ATTN_HEAD_DIM), 0.05)
    attn_sinks = nrm(ks[7], (N_ATTN_LAYERS, ATTN_HEADS), 1.0)
    attn_w_out = nrm(ks[8], (N_ATTN_LAYERS, ATTN_Q_DIM, D_MODEL), ATTN_Q_DIM ** -0.5)

    gdn_w_in = nrm(ks[9], (N_GDN_LAYERS, D_MODEL, GDN_IN_DIM), D_MODEL ** -0.5)
    gdn_conv = nrm(ks[10], (N_GDN_LAYERS, GDN_CONV, GDN_QKV_DIM), GDN_CONV ** -0.5)
    gdn_a_log = jnp.log(jax.random.uniform(ks[11], (N_GDN_LAYERS, GDN_V_HEADS), f32, 1.0, 16.0))
    dt = jnp.exp(jax.random.uniform(ks[12], (N_GDN_LAYERS, GDN_V_HEADS), f32,
                                    math.log(1e-3), math.log(1e-1)))
    gdn_dt_bias = dt + jnp.log(-jnp.expm1(-dt))
    gdn_norm = 1.0 + nrm(ks[13], (N_GDN_LAYERS, GDN_HEAD_V), 0.05)
    gdn_w_out = nrm(ks[14], (N_GDN_LAYERS, GDN_VAL_DIM, D_MODEL), GDN_VAL_DIM ** -0.5)

    ffn_w_up = nrm(ks[15], (DEPTH, D_MODEL, 2 * D_FF), D_MODEL ** -0.5)
    ffn_conv = nrm(ks[16], (DEPTH, FFN_CONV, D_FF), FFN_CONV ** -0.5)
    ffn_conv_b = nrm(ks[17], (DEPTH, D_FF), 0.02)
    ffn_w_down = nrm(ks[18], (DEPTH, D_FF, D_MODEL), D_FF ** -0.5)
    return {"x": x, "positions": positions, "mixer_norm": mixer_norm, "ffn_norm": ffn_norm,
            "attn_w_in": attn_w_in, "attn_q_gain": attn_q_gain, "attn_k_gain": attn_k_gain,
            "attn_sinks": attn_sinks, "attn_w_out": attn_w_out,
            "gdn_w_in": gdn_w_in, "gdn_conv": gdn_conv, "gdn_a_log": gdn_a_log,
            "gdn_dt_bias": gdn_dt_bias, "gdn_norm": gdn_norm, "gdn_w_out": gdn_w_out,
            "ffn_w_up": ffn_w_up, "ffn_conv": ffn_conv, "ffn_conv_b": ffn_conv_b,
            "ffn_w_down": ffn_w_down}

def first_block(x, positions, mixer_norm, ffn_norm, attn_w_in, attn_q_gain, attn_k_gain,
              attn_sinks, attn_w_out, gdn_w_in, gdn_conv, gdn_a_log, gdn_dt_bias, gdn_norm,
              gdn_w_out, ffn_w_up, ffn_conv, ffn_conv_b, ffn_w_down):
    cos, sin = rope_tables(positions)
    h = x
    for i in range(DEPTH):
        j = i // 2
        u = rms_norm(h, mixer_norm[i])
        if i % 2 == 0:
            h = h + swa_sink_attention(u, attn_w_in[j], attn_q_gain[j], attn_k_gain[j],
                                       attn_sinks[j], attn_w_out[j], cos, sin)
        else:
            h = h + gated_deltanet(u, gdn_w_in[j], gdn_conv[j], gdn_a_log[j], gdn_dt_bias[j],
                                   gdn_norm[j], gdn_w_out[j])
        u = rms_norm(h, ffn_norm[i])
        h = h + conv_glu_ffn(u, ffn_w_up[i], ffn_conv[i], ffn_conv_b[i], ffn_w_down[i])
    return h


N_EVEN = (DEPTH + 1) // 2
N_ODD = DEPTH // 2
N_SUBLAYERS = 3
D_FF_2 = 2816

A_WIDTH = D_MODEL // 2
A_GROUPS = 8
A_CONV = 31
B_WIDTH = D_MODEL // 2
B_CONV = 3
EVEN_IN = 2 * A_WIDTH + 3 * B_WIDTH
EVEN_MIX = A_WIDTH + B_WIDTH

POOL_WINDOWS = (2, 4, 8, 16)
C_GROUPS = len(POOL_WINDOWS)
C_WIDTH = D_MODEL // 2
C_GROUP_DIM = C_WIDTH // C_GROUPS
D_HEADS = 8
HEAD_DIM = 64
D_WIDTH = D_HEADS * HEAD_DIM
ODD_IN = C_WIDTH + 3 * D_WIDTH
ODD_MIX = C_WIDTH + D_WIDTH
MOBA_BLOCK = 256
MOBA_TOPK = 3
Q_CHUNK = 128


def rms_norm_2(x, g):
    xf = x.astype(jnp.float32)
    y = xf * lax.rsqrt(jnp.mean(xf * xf, axis=-1, keepdims=True) + EPS)
    return (y * g.astype(jnp.float32)).astype(x.dtype)

def modulate(h, shift, scale):
    return h * (1.0 + scale[:, None, :]) + shift[:, None, :]

def group_layer_norm(u, n_groups, g, b):
    bn, s, ch = u.shape
    uf = u.astype(jnp.float32).reshape(bn, s, n_groups, ch // n_groups)
    mu = jnp.mean(uf, axis=-1, keepdims=True)
    var = jnp.mean(jnp.square(uf - mu), axis=-1, keepdims=True)
    y = ((uf - mu) * lax.rsqrt(var + EPS)).reshape(bn, s, ch)
    return (y * g + b).astype(u.dtype)

def causal_depthwise_conv(u, w):
    k, ch = w.shape
    return lax.conv_general_dilated(
        u, w[:, None, :], window_strides=(1,), padding=[(k - 1, 0)],
        dimension_numbers=("NWC", "WIO", "NWC"), feature_group_count=ch)

def swiglu(h, w_gate, w_up, w_down):
    return (jax.nn.silu(h @ w_gate) * (h @ w_up)) @ w_down

def conv_mixers(h, w_in, conv_a_w, conv_a_b, ln_a_g, ln_a_b, conv_b_w, w_out):
    z = h @ w_in
    a_val, a_gate, b_gate, c_gate, b_val = jnp.split(
        z, [A_WIDTH, 2 * A_WIDTH, 2 * A_WIDTH + B_WIDTH, 2 * A_WIDTH + 2 * B_WIDTH], axis=-1)
    a = a_val * jax.nn.sigmoid(a_gate)
    a = causal_depthwise_conv(a, conv_a_w) + conv_a_b
    a = jax.nn.silu(group_layer_norm(a, A_GROUPS, ln_a_g, ln_a_b))
    bb = b_gate * causal_depthwise_conv(c_gate * b_val, conv_b_w)
    return jnp.concatenate([a, bb], axis=-1) @ w_out

def multiscale_pool(u, pool_w, pool_b, pool_scale):
    bn, s, _ = u.shape
    ug = u.reshape(bn, s, C_GROUPS, C_GROUP_DIM).astype(jnp.float32)
    cs0 = jnp.pad(jnp.cumsum(ug, axis=1), ((0, 0), (1, 0), (0, 0), (0, 0)))
    t1 = jnp.arange(1, s + 1, dtype=jnp.float32)
    means = []
    for g, w in enumerate(POOL_WINDOWS):
        upper = cs0[:, 1:, g]
        lower = jnp.pad(cs0[:, :s + 1 - w, g], ((0, 0), (w - 1, 0), (0, 0)))
        means.append((upper - lower) / jnp.minimum(t1, w)[None, :, None])
    pooled = (jnp.stack(means, axis=2) - ug).astype(u.dtype)
    mixed = jnp.einsum("bsgc,gcd->bsgd", pooled, pool_w) + pool_b
    return mixed.reshape(bn, s, C_WIDTH) * pool_scale

def moba_attention(q, k, v):
    bn, s, _ = q.shape
    s_pad = -(-s // MOBA_BLOCK) * MOBA_BLOCK
    nb = s_pad // MOBA_BLOCK
    topk = min(MOBA_TOPK, nb)

    def to_heads(t):
        return t.reshape(bn, s, D_HEADS, HEAD_DIM).transpose(0, 2, 1, 3)

    pad = ((0, 0), (0, 0), (0, s_pad - s), (0, 0))
    qh = to_heads(q) * (HEAD_DIM ** -0.5)
    kh = jnp.pad(to_heads(k), pad)
    vh = jnp.pad(to_heads(v), pad)
    k_blocks = kh.reshape(bn, D_HEADS, nb, MOBA_BLOCK, HEAD_DIM)
    v_blocks = vh.reshape(bn, D_HEADS, nb, MOBA_BLOCK, HEAD_DIM)
    k_mean = jnp.mean(k_blocks.astype(jnp.float32), axis=3)
    slopes = jnp.asarray(2.0 ** (-8.0 * np.arange(1, D_HEADS + 1) / D_HEADS), dtype=jnp.float32)
    b_idx = jnp.arange(bn)[:, None, None, None]
    h_idx = jnp.arange(D_HEADS)[None, :, None, None]
    offs = jnp.arange(MOBA_BLOCK)
    blk_ids = jnp.arange(nb)
    slot_ids = jnp.arange(topk)

    def chunk(ci):
        q0 = ci * Q_CHUNK
        own = q0 // MOBA_BLOCK
        qc = lax.dynamic_slice_in_dim(qh, q0, Q_CHUNK, axis=2)
        qpos = q0 + jnp.arange(Q_CHUNK)
        gate = jnp.einsum("bhqd,bhnd->bhqn", qc.astype(jnp.float32), k_mean)
        gate = jnp.where(blk_ids < own, gate, -jnp.inf)
        _, sel = lax.top_k(gate, topk)
        sel_valid = slot_ids < own
        k_sel = k_blocks[b_idx, h_idx, sel]
        v_sel = v_blocks[b_idx, h_idx, sel]
        s_sel = jnp.einsum("bhqd,bhqjkd->bhqjk", qc, k_sel).astype(jnp.float32)
        kpos_sel = sel[..., None] * MOBA_BLOCK + offs
        s_sel = s_sel - slopes[:, None, None, None] * (qpos[:, None, None] - kpos_sel)
        s_sel = jnp.where(sel_valid[:, None], s_sel, -jnp.inf)
        s_sel = s_sel.reshape(bn, D_HEADS, Q_CHUNK, topk * MOBA_BLOCK)
        k_own = lax.dynamic_slice_in_dim(kh, own * MOBA_BLOCK, MOBA_BLOCK, axis=2)
        v_own = lax.dynamic_slice_in_dim(vh, own * MOBA_BLOCK, MOBA_BLOCK, axis=2)
        dist = qpos[:, None] - (own * MOBA_BLOCK + offs)[None, :]
        s_own = jnp.einsum("bhqd,bhkd->bhqk", qc, k_own).astype(jnp.float32)
        s_own = jnp.where(dist >= 0, s_own - slopes[:, None, None] * dist, -jnp.inf)
        p = jax.nn.softmax(jnp.concatenate([s_sel, s_own], axis=-1), axis=-1).astype(v.dtype)
        p_sel, p_own = jnp.split(p, [topk * MOBA_BLOCK], axis=-1)
        p_sel = p_sel.reshape(bn, D_HEADS, Q_CHUNK, topk, MOBA_BLOCK)
        return (jnp.einsum("bhqjk,bhqjkd->bhqd", p_sel, v_sel)
                + jnp.einsum("bhqk,bhkd->bhqd", p_own, v_own))

    out = lax.map(chunk, jnp.arange(s // Q_CHUNK))
    return out.transpose(1, 0, 3, 2, 4).reshape(bn, s, D_WIDTH)

def pool_moba_mixers(h, w_in, pool_w, pool_b, pool_scale, w_out):
    z = h @ w_in
    u, q, k, v = jnp.split(z, [C_WIDTH, C_WIDTH + D_WIDTH, C_WIDTH + 2 * D_WIDTH], axis=-1)
    pooled = multiscale_pool(u, pool_w, pool_b, pool_scale)
    att = moba_attention(q, k, v)
    return jnp.concatenate([pooled, att], axis=-1) @ w_out

def second_inputs(seed: int = 0) -> dict:
    key = jax.random.key(seed)
    ks = jax.random.split(key, 24)
    f32 = jnp.float32

    def nrm(k, shape, scale):
        return jax.random.normal(k, shape, dtype=f32) * scale

    return {
        "x": nrm(ks[0], (BATCH, SEQ, D_MODEL), 1.0),
        "c": nrm(ks[1], (BATCH, D_MODEL), 1.0),
        "ada_w": nrm(ks[2], (DEPTH, D_MODEL, N_SUBLAYERS * 3 * D_MODEL), D_MODEL ** -0.5),
        "ada_b": nrm(ks[3], (DEPTH, N_SUBLAYERS * 3 * D_MODEL), 0.02),
        "ffn_norm": 1.0 + nrm(ks[4], (DEPTH, 2, D_MODEL), 0.05),
        "ffn_w_gate": nrm(ks[5], (DEPTH, 2, D_MODEL, D_FF_2), D_MODEL ** -0.5),
        "ffn_w_up": nrm(ks[6], (DEPTH, 2, D_MODEL, D_FF_2), D_MODEL ** -0.5),
        "ffn_w_down": nrm(ks[7], (DEPTH, 2, D_FF_2, D_MODEL), D_FF_2 ** -0.5),
        "mix_norm": 1.0 + nrm(ks[8], (DEPTH, D_MODEL), 0.05),
        "conv_w_in": nrm(ks[9], (N_EVEN, D_MODEL, EVEN_IN), D_MODEL ** -0.5),
        "conv_a_w": nrm(ks[10], (N_EVEN, A_CONV, A_WIDTH), A_CONV ** -0.5),
        "conv_a_b": nrm(ks[11], (N_EVEN, A_WIDTH), 0.02),
        "conv_a_ln_g": 1.0 + nrm(ks[12], (N_EVEN, A_WIDTH), 0.05),
        "conv_a_ln_b": nrm(ks[13], (N_EVEN, A_WIDTH), 0.02),
        "conv_b_w": nrm(ks[14], (N_EVEN, B_CONV, B_WIDTH), B_CONV ** -0.5),
        "conv_w_out": nrm(ks[15], (N_EVEN, EVEN_MIX, D_MODEL), EVEN_MIX ** -0.5),
        "pm_w_in": nrm(ks[16], (N_ODD, D_MODEL, ODD_IN), D_MODEL ** -0.5),
        "pool_w": nrm(ks[17], (N_ODD, C_GROUPS, C_GROUP_DIM, C_GROUP_DIM), C_GROUP_DIM ** -0.5),
        "pool_b": nrm(ks[18], (N_ODD, C_GROUPS, C_GROUP_DIM), 0.02),
        "pool_scale": 1.0 + nrm(ks[19], (N_ODD, C_WIDTH), 0.1),
        "pm_w_out": nrm(ks[20], (N_ODD, ODD_MIX, D_MODEL), ODD_MIX ** -0.5),
        "final_norm": 1.0 + nrm(ks[21], (D_MODEL,), 0.05),
    }

def second_block(x, c, ada_w, ada_b, ffn_norm, ffn_w_gate, ffn_w_up, ffn_w_down, mix_norm,
              conv_w_in, conv_a_w, conv_a_b, conv_a_ln_g, conv_a_ln_b, conv_b_w, conv_w_out,
              pm_w_in, pool_w, pool_b, pool_scale, pm_w_out, final_norm):
    bn = x.shape[0]
    cond = jax.nn.silu(c)
    for i in range(DEPTH):
        mod = (cond @ ada_w[i] + ada_b[i]).reshape(bn, N_SUBLAYERS, 3, D_MODEL)
        h = modulate(rms_norm_2(x, ffn_norm[i, 0]), mod[:, 0, 0], mod[:, 0, 1])
        x = x + 0.5 * mod[:, 0, 2][:, None, :] * swiglu(
            h, ffn_w_gate[i, 0], ffn_w_up[i, 0], ffn_w_down[i, 0])
        h = modulate(rms_norm_2(x, mix_norm[i]), mod[:, 1, 0], mod[:, 1, 1])
        if i % 2 == 0:
            e = i // 2
            y = conv_mixers(h, conv_w_in[e], conv_a_w[e], conv_a_b[e], conv_a_ln_g[e],
                            conv_a_ln_b[e], conv_b_w[e], conv_w_out[e])
        else:
            o = i // 2
            y = pool_moba_mixers(h, pm_w_in[o], pool_w[o], pool_b[o], pool_scale[o], pm_w_out[o])
        x = x + mod[:, 1, 2][:, None, :] * y
        h = modulate(rms_norm_2(x, ffn_norm[i, 1]), mod[:, 2, 0], mod[:, 2, 1])
        x = x + 0.5 * mod[:, 2, 2][:, None, :] * swiglu(
            h, ffn_w_gate[i, 1], ffn_w_up[i, 1], ffn_w_down[i, 1])
    return rms_norm_2(x, final_norm)


def setup_inputs(seed=0):
    out = dict(first_inputs(seed))
    for name, value in second_inputs(seed + 1).items():
        if name != "x":
            out[name + "_2"] = value
    return out


def reference(
    x, positions, mixer_norm, ffn_norm, attn_w_in, attn_q_gain, attn_k_gain, attn_sinks,
    attn_w_out, gdn_w_in, gdn_conv, gdn_a_log, gdn_dt_bias, gdn_norm, gdn_w_out, ffn_w_up,
    ffn_conv, ffn_conv_b, ffn_w_down, c_2, ada_w_2, ada_b_2, ffn_norm_2, ffn_w_gate_2,
    ffn_w_up_2, ffn_w_down_2, mix_norm_2, conv_w_in_2, conv_a_w_2, conv_a_b_2, conv_a_ln_g_2,
    conv_a_ln_b_2, conv_b_w_2, conv_w_out_2, pm_w_in_2, pool_w_2, pool_b_2, pool_scale_2,
    pm_w_out_2, final_norm_2,
):
    x = first_block(
        x, positions, mixer_norm, ffn_norm, attn_w_in, attn_q_gain, attn_k_gain, attn_sinks,
        attn_w_out, gdn_w_in, gdn_conv, gdn_a_log, gdn_dt_bias, gdn_norm, gdn_w_out, ffn_w_up,
        ffn_conv, ffn_conv_b, ffn_w_down,
    )
    return second_block(
        x, c_2, ada_w_2, ada_b_2, ffn_norm_2, ffn_w_gate_2, ffn_w_up_2, ffn_w_down_2,
        mix_norm_2, conv_w_in_2, conv_a_w_2, conv_a_b_2, conv_a_ln_g_2, conv_a_ln_b_2,
        conv_b_w_2, conv_w_out_2, pm_w_in_2, pool_w_2, pool_b_2, pool_scale_2, pm_w_out_2,
        final_norm_2,
    )


_drawn_inputs = setup_inputs


def setup_inputs(seed=0):
    import zlib

    import numpy as np

    out = dict(_drawn_inputs(seed))
    spreads = {}
    factors = {'attn_q_gain': 3.254,
     'attn_k_gain': 3.277,
     'ffn_conv_b': 3.048,
     'conv_a_b_2': 8.0,
     'conv_a_ln_g_2': 6.004,
     'conv_a_ln_b_2': 24.636,
     'pool_b_2': 8.0,
     'attn_sinks': 4.834,
     'ffn_norm_2': 2.809,
     'pool_scale_2': 3.851}
    for name, (base, spread) in spreads.items():
        noise = np.random.default_rng([zlib.crc32(name.encode()), seed]).standard_normal(out[name].shape)
        drawn = base * np.exp(spread * noise) if base else spread * noise
        out[name] = __import__('jax').numpy.asarray(drawn.astype(out[name].dtype))
    for name, factor in factors.items():
        out[name] = (out[name] * factor).astype(out[name].dtype)
    return out
```

```python
from contextlib import ExitStack

import concourse.bass as bass
import numpy as np
from concourse import mybir

F32 = mybir.dt.float32
I32 = mybir.dt.int32
ALU = mybir.AluOpType
ACT = mybir.ActivationFunctionType
AX_X = mybir.AxisListType.X

P = 128
D = 1024
T = 256
C = D // P
HD = 64
RING = 4
EPS = 1e-6
NEG = -3.0e38
FF1, FF2 = 3072 // P, 2816 // P
GH, GB = 16, 4
CH = 64
TAPS_A = 31
ROPE = HD // 4
MAGIC = 12582912.0
PIECE = 512
PIECES = 2 * 9 * D // PIECE

UNITS = [("attn_in", 12), ("attn_out", 8), ("ffn0", 3 * FF1), ("gdn_gates", 1), ("gdn_in", 48), ("gdn_out", 16),
         ("ffn1", 3 * FF1), ("ffn2", 3 * FF2), ("conv_in", 20), ("conv_out", 8), ("ffn3", 3 * FF2),
         ("ffn4", 3 * FF2), ("pm_in", 16), ("pm_out", 8), ("ffn5", 3 * FF2)]
FIRST_UNIT = {}
N_UNITS = 0
for _name, _n in UNITS:
    FIRST_UNIT[_name] = N_UNITS
    N_UNITS += _n

COLS = [("mixer_norm", 16), ("ffn_norm", 16), ("q_gain", 1), ("k_gain", 1), ("gdn_conv", 128), ("a_log", 1),
        ("dt_bias", 1), ("gdn_norm", 1), ("ffn_conv", 8 * FF1), ("cond", 8), ("ada_b", 144), ("ffn_norm_2", 32),
        ("mix_norm", 16), ("conv_a_w", 4 * TAPS_A), ("conv_a_b", 4), ("ln_g", 4), ("ln_b", 4), ("conv_b_w", 12),
        ("pool_b", 4), ("pool_scale", 4), ("final_norm", 8), ("inv_freq", 1), ("sinks", 16), ("eps", 1),
        ("half_pi", 1), ("one", 1), ("zero", 1)]
COL = {}
N_COLS = 0
for _name, _n in COLS:
    COL[_name] = N_COLS
    N_COLS += _n

CONSTS = [("ident", 128), ("ones", 128), ("block_ones", 128), ("rotate", 128), ("window_mask", 384),
          ("stack_ident", 64), ("level_lo", 64), ("level_up", 6 * 64), ("strict_lo_neg", 64), ("incl_up_neg", 64),
          ("strict_up", 64), ("reset", T), ("pool_inv", 4 * T)]
CONST = {}
N_CONST = 0
for _name, _n in CONSTS:
    CONST[_name] = (N_CONST, _n)
    N_CONST += _n


def attn_tile_heads(j):
    return (j, 4 + j) if j < 4 else (4 + j, 8 + j)



class Steps:

    def __init__(self, eng, sem):
        self.eng, self.sem, self.n, self.turns = eng, sem, 0, 0

    def mark(self, ins):
        ins.then_inc(self.sem, 1)
        self.n += 1
        return ins

    def wait(self, back=0):
        self.eng.wait_ge(self.sem, self.n - back + self.turns)

    def start_loop(self, turn, per):
        self.n0, self.per, self.turns = self.n, per, per * turn

    def end_loop(self, count):
        assert self.n - self.n0 == self.per, (self.n - self.n0, self.per)
        self.n, self.turns = self.n0 + self.per * count, 0


class Carver:

    def __init__(self, tile, size):
        self.tile, self.size, self.at = tile, size, 0

    def cut(self, *dims):
        n = int(np.prod(dims))
        assert self.at + n <= self.size, (self.at + n, self.size)
        ap = self.tile[:, self.at:self.at + n]
        self.at += n
        names = "abcd"[:len(dims)]
        if len(dims) > 1:
            ap = ap.rearrange(f"p ({' '.join(names)}) -> p {' '.join(names)}", **dict(zip(names, dims)))
        return ap


def build(nc, dram, out_dram):
    with ExitStack() as ctx:
        def sb(name, shape, dt=F32):
            return ctx.enter_context(nc.sbuf_tensor(name, shape, dt))

        def sem(name):
            return ctx.enter_context(nc.semaphore(name))

        ring = sb("weight_ring", [P, RING, C, P])
        h = sb("h", [P, C, T])
        u = sb("u", [P, C, T])
        mix = sb("mix", [P, 2 * C, T])
        cols = sb("cols", [P, N_COLS])
        consts = sb("consts", [P, N_CONST])
        squares = sb("squares", [P, C, T])
        scaled = sb("scaled", [P, C, T])
        root = sb("root", [P, T])
        rstd = sb("rstd", [P, T])
        mods = sb("mods", [P, 144])
        cond = sb("cond", [P, 8])
        gain = sb("gain", [P, 8])
        half_gate = sb("half_gate", [P, 8])
        positions = sb("positions", [P, T], I32)
        AR = 27 * 1024
        arena = sb("arena", [P, AR])
        ps = ctx.enter_context(nc.psum_tensor("ps", [P, 8, 512], F32))
        gates_dram = nc.dram_tensor("gates_scratch", (2, GH, T), F32, kind="Internal").ap()

        def col(name, k=0):
            at = COL[name] + k
            return cols[:, bass.ds(at, 1)]

        def const(name, k=None, n=None):
            at, size = CONST[name]
            if k is not None:
                at, size = at + k * n, n
            return consts[:, at:at + size]

        ident, ones = const("ident"), const("ones")

        raw_ready = [sem(f"raw_ready{s}") for s in range(RING)]
        unit_done = [sem(f"unit_done{s}") for s in range(RING)]
        small_loaded = sem("small_loaded")
        cond_ready = sem("cond_ready")
        h_loaded, h_ready = sem("h_loaded"), sem("h_ready")
        sq_ready, ss_ready, root_ready = sem("sq_ready"), sem("ss_ready"), sem("root_ready")
        scaled_ready, u_ready = sem("scaled_ready"), sem("u_ready")
        dve_steps, act_steps, pool_steps = sem("dve_steps"), sem("act_steps"), sem("pool_steps")
        out_done, out_ready = sem("out_done"), sem("out_ready")
        mix_ready = sem("mix_ready")
        cv0_ready, cv_ready = sem("conv_tap_ready"), sem("conv_ready")
        sg_ready, act_ready = sem("silu_ready"), sem("act_ready")
        ada_loaded = [sem("ada_loaded0"), sem("ada_loaded1")]
        ada_summed, ada_cols = sem("ada_summed"), sem("ada_cols")
        pjsq_ready, pjss_ready, pjroot_ready = sem("pjsq_ready"), sem("pjss_ready"), sem("pjroot_ready")
        qn_ready, rot_ready, rope_ready = sem("qn_ready"), sem("rot_ready"), sem("rope_ready")
        angle_ready, sine_ready = sem("angle_ready"), sem("sine_ready")
        v_copied = sem("v_copied")
        sc_ready, max_ready, exp_ready, p_ready = sem("scores_ready"), sem("max_ready"), sem("exp_ready"), sem("probs_ready")
        pt_ready, ptc_ready, pv_ready = sem("pt_ready"), sem("pt_copied"), sem("pv_ready")

        MODS = {}
        for n, (l, s) in enumerate([(0, 0), (0, 1), (0, 2), (1, 0), (1, 1), (1, 2)]):
            MODS[4 + n] = (l, s)

        def mod_col(l, s, which):
            return 72 * l + (3 * s + which) * 8

        NORM_AT = {0: ("mixer_norm", 0), 2: ("mixer_norm", 8), 1: ("ffn_norm", 0), 3: ("ffn_norm", 8),
                   4: ("ffn_norm_2", 0), 5: ("mix_norm", 0), 6: ("ffn_norm_2", 8),
                   7: ("ffn_norm_2", 16), 8: ("mix_norm", 8), 9: ("ffn_norm_2", 24), 10: ("final_norm", 0)}

        def take_unit(pe, first, j, turn_units=0, turn=None):
            n = first + j
            need = 16 * (n // RING + 1)
            if turn is not None:
                assert turn_units % RING == 0
                need = need + 16 * (turn_units // RING) * turn
            pe.wait_ge(raw_ready[n % RING], need)
            return n % RING

        def unit_products(eng, first, j, turn_units=0, turn=None):
            n = first + j
            need = n // RING + 1
            if turn is not None:
                need = need + turn_units // RING * turn
            eng.wait_ge(unit_done[n % RING], need)

        def norm_bank(k):
            return 0 if k in (1, 3, 6, 9) else 7

        def norm_act(act, k):
            for c in range(C):
                if k == 0:
                    act.wait_ge(h_loaded, 16)
                else:
                    act.wait_ge(h_ready, 8 * (k - 1) + c + 1)
                nc.scalar.activation(squares[:, c], h[:, c], ACT.Square).then_inc(sq_ready, 1)
            act.wait_ge(ss_ready, k + 1)
            nc.scalar.activation(root[:], ps[:, norm_bank(k), 0:T], ACT.Sqrt, bias=col("eps"), scale=1.0 / D).then_inc(root_ready, 1)
            if k in MODS:
                l, s = MODS[k]
                for c in range(C):
                    act.wait_ge(scaled_ready, 8 * (k - 4) + c + 1)
                    sh = mod_col(l, s, 0) + c
                    nc.scalar.activation(u[:, c], scaled[:, c], ACT.Identity, bias=mods[:, sh:sh + 1]).then_inc(u_ready, 1)

        def norm_pe(pe, k):
            for c in range(C):
                pe.wait_ge(sq_ready, 8 * k + c + 1)
                last = nc.tensor.matmul(ps[:, norm_bank(k), 0:T], ones, squares[:, c], start=(c == 0), stop=(c == C - 1))
            last.then_inc(ss_ready, 1)

        def norm_dve(dve, steps, k):
            if k in MODS:
                l, s = MODS[k]
                name, at = NORM_AT[k]
                dve.wait_ge(h_ready, 8 * k)
                sc, ga = mod_col(l, s, 1), mod_col(l, s, 2)
                a = COL[name] + at
                steps.mark(nc.vector.scalar_tensor_tensor(gain[:], mods[:, sc:sc + 8], 1.0, cols[:, a:a + 8], ALU.add, ALU.mult))
                steps.mark(nc.vector.tensor_scalar(half_gate[:], mods[:, ga:ga + 8], 1.0 if s == 1 else 0.5, None, ALU.mult))
            dve.wait_ge(root_ready, k + 1)
            steps.mark(nc.vector.reciprocal(rstd[:], root[:]))
            steps.wait()
            for c in range(C):
                if k in MODS:
                    nc.vector.scalar_tensor_tensor(scaled[:, c], h[:, c], gain[:, c:c + 1], rstd[:], ALU.mult, ALU.mult).then_inc(scaled_ready, 1)
                else:
                    name, at = NORM_AT[k]
                    nc.vector.scalar_tensor_tensor(u[:, c], h[:, c], col(name, at + c), rstd[:], ALU.mult, ALU.mult).then_inc(
                        out_ready if k == 10 else u_ready, 1)

        def u_count(k, c):
            return 8 * k + c + 1

        def residual_dve(dve, steps, k, gated, banks):
            for c in range(C):
                if banks == "lin":
                    name, per = LIN[k]
                    unit_products(dve, FIRST_UNIT[name], per * c + per - 1)
                    src = ps[:, c, 0:T]
                else:
                    src = ps[:, c // 2, (c % 2) * T:(c % 2 + 1) * T]
                g = half_gate[:, c:c + 1] if gated else 1.0
                nc.vector.scalar_tensor_tensor(h[:, c], src, g, h[:, c], ALU.mult, ALU.add).then_inc(h_ready, 1)

        LIN = {0: ("attn_out", 1), 2: ("gdn_out", 2), 5: ("conv_out", 1), 8: ("pm_out", 1)}
        MIX_COUNT = {0: 4, 2: 8, 5: 12, 8: 18}

        def lin_pe(pe, k, name, kc):
            pe.wait_ge(mix_ready, MIX_COUNT[k])
            per = kc // C
            for n in range(C):
                for b in range(per):
                    s = take_unit(pe, FIRST_UNIT[name], n * per + b)
                    for kk in range(C):
                        last = nc.tensor.matmul(ps[:, n, 0:T], ring[:, s, kk], mix[:, b * C + kk],
                                                start=(b == 0 and kk == 0), stop=(b == per - 1 and kk == C - 1))
                    last.then_inc(unit_done[s], 1)

        ffn = Carver(arena, AR)
        ada_ring = ffn.cut(2, C, PIECE)
        ada_acc = ffn.cut(10, PIECE)
        cvb = ffn.cut(4, T)
        sgb = ffn.cut(4, T)
        actb = ffn.cut(4, T)
        FFN = [(1, FF1, 1, [(5, 2)]), (3, FF1, 1, [(5, 2)]), (4, FF2, 2, [(5, 2)]), (6, FF2, 2, [(3, 2), (2, 0)]),
               (7, FF2, 2, [(5, 0)]), (9, FF2, 2, [(5, 0)])]
        F_BASE = [0, FF1, 2 * FF1, 2 * FF1 + FF2, 2 * FF1 + 2 * FF2, 2 * FF1 + 3 * FF2, 2 * FF1 + 4 * FF2]
        PIECE_BASE = [0, 10, 20, 30, 36, 36, 36]
        CREDIT = 4

        def gate_up(pe, q, first, f, turn_f=0, turn=None):
            n = F_BASE[q] + f
            need = n - 3 + CREDIT
            if turn is not None:
                need = need + turn_f * turn
            pe.wait_ge(act_ready, need)
            b = 4 + f % 4
            for half in range(2):
                s = take_unit(pe, first, half, 3 * turn_f, turn)
                for k in range(C):
                    last = nc.tensor.matmul(ps[:, b, half * T:(half + 1) * T], ring[:, s, k], u[:, k],
                                            start=(half == 0 and k == 0), stop=(k == C - 1), skip_group_check=True)
                last.then_inc(unit_done[s], 1)

        def down(pe, q, first, f, start, turn_f=0, turn=None):
            n = F_BASE[q] + f
            need = n + 1 + CREDIT
            if turn is not None:
                need = need + turn_f * turn
            pe.wait_ge(act_ready, need)
            s = take_unit(pe, first, 0, 3 * turn_f, turn)
            for c in range(C):
                last = nc.tensor.matmul(ps[:, c // 2, (c % 2) * T:(c % 2 + 1) * T], ring[:, s, c], actb[:, f % 4],
                                        start=(start and c % 2 == 0), stop=True, skip_group_check=True)
            last.then_inc(unit_done[s], 1)

        def ffn_pe(pe, q):
            k, nf, kind, loops = FFN[q]
            first = FIRST_UNIT[f"ffn{q}"]
            for c in range(C):
                pe.wait_ge(u_ready, u_count(k, c))
            gate_up(pe, q, first, 0)
            gate_up(pe, q, first + 2, 1)
            down(pe, q, first + 4, 0, True)
            at, f0 = first + 5, 2
            for turns, _ in loops:
                with pe.Fori(0, turns) as i:
                    for j in range(4):
                        gate_up(pe, q, at + 3 * j, f0 + j, 4, i)
                        down(pe, q, at + 3 * j + 2, f0 + j - 1, False, 4, i)
                at, f0 = at + 12 * turns, f0 + 4 * turns
            for f in range(f0, nf):
                gate_up(pe, q, at, f)
                down(pe, q, at + 2, f - 1, False)
                at += 3
            down(pe, q, at, nf - 1, False)
            n0, n1 = PIECE_BASE[q], PIECE_BASE[q + 1]
            if n1 > n0:
                pe.wait_ge(ada_summed, n1)
                for n in range(4 * (n1 - n0)):
                    last = nc.tensor.matmul(ps[:, 4, n:n + 1], ada_acc[:, n // 4, (n % 4) * P:(n % 4 + 1) * P],
                                            ones[:, 0:1], start=True, stop=True)
                last.then_inc(ada_cols, 1)

        def ffn_tile_act(act, q, f, turn=None):
            k, nf, kind, loops = FFN[q]
            n = F_BASE[q] + f + 1
            at = 0
            if turn is not None:
                n, at = n + 4 * turn, 16 * turn
            b, r = 4 + f % 4, f % 4
            up_unit = 1 if f == 0 else 3 * f
            unit_products(act, FIRST_UNIT[f"ffn{q}"], up_unit, 12, turn)
            if kind == 1:
                w = COL["ffn_conv"] + 4 * FF1 * q + 4 * f + at
                nc.scalar.activation(cvb[:, r], ps[:, b, 0:T], ACT.Identity, scale=cols[:, bass.ds(w + 2, 1)],
                                     bias=cols[:, bass.ds(w + 3, 1)]).then_inc(cv0_ready, 1)
                act.wait_ge(cv_ready, n)
                nc.scalar.activation(sgb[:, r], cvb[:, r], ACT.Silu).then_inc(sg_ready, 1)
            else:
                nc.scalar.activation(sgb[:, r], ps[:, b, 0:T], ACT.Silu).then_inc(sg_ready, 1)

        def ffn_tile_dve(dve, steps, q, f, turn=None):
            k, nf, kind, loops = FFN[q]
            n = F_BASE[q] + f + 1
            at = 0
            if turn is not None:
                n, at = n + 4 * turn, 16 * turn
            b, r = 4 + f % 4, f % 4
            if kind == 1:
                w = COL["ffn_conv"] + 4 * FF1 * q + 4 * f + at
                dve.wait_ge(cv0_ready, n)
                steps.mark(nc.vector.scalar_tensor_tensor(cvb[:, r, 1:T], ps[:, b, 0:T - 1], cols[:, bass.ds(w + 1, 1)],
                                                          cvb[:, r, 1:T], ALU.mult, ALU.add))
                steps.wait()
                nc.vector.scalar_tensor_tensor(cvb[:, r, 2:T], ps[:, b, 0:T - 2], cols[:, bass.ds(w, 1)],
                                               cvb[:, r, 2:T], ALU.mult, ALU.add).then_inc(cv_ready, 1)
            dve.wait_ge(sg_ready, n)
            nc.vector.tensor_tensor(actb[:, r], sgb[:, r], ps[:, b, T:2 * T], ALU.mult).then_inc(act_ready, 1)

        def ada_dve(dve, steps, q, piece, part, turn, per):
            slot = piece % 2
            base = PIECE_BASE[q]
            acc = ada_acc[:, bass.ds(piece - base + per * turn, 1), :].rearrange("p a b -> p (a b)")
            if part == 0:
                dve.wait_ge(ada_loaded[slot], 16 * (piece // 2 + 1) + 16 * (per // 2) * turn)
            for kb in range(4 * part, 4 * part + 4):
                src = ada_ring[:, slot, kb]
                if kb == 0:
                    steps.mark(nc.vector.tensor_scalar(acc, src, cond[:, 0:1], None, ALU.mult))
                else:
                    steps.wait()
                    ins = nc.vector.scalar_tensor_tensor(acc, src, cond[:, kb:kb + 1], acc, ALU.mult, ALU.add)
                    if kb == C - 1:
                        ins.then_inc(ada_summed, 1)
                    else:
                        steps.mark(ins)

        def ffn_act(act, q):
            k, nf, kind, loops = FFN[q]
            for f in range(2):
                ffn_tile_act(act, q, f)
            f0 = 2
            for turns, _ in loops:
                with act.Fori(0, turns) as i:
                    for j in range(4):
                        ffn_tile_act(act, q, f0 + j, i)
                f0 += 4 * turns
            for f in range(f0, nf):
                ffn_tile_act(act, q, f)

        def ffn_dve(dve, steps, q):
            k, nf, kind, loops = FFN[q]
            for f in range(2):
                ffn_tile_dve(dve, steps, q, f)
            f0, piece = 2, PIECE_BASE[q]
            for turns, pieces in loops:
                with dve.Fori(0, turns) as i:
                    steps.start_loop(i, (4 if kind == 1 else 0) + 7 * pieces)
                    for j in range(4):
                        ffn_tile_dve(dve, steps, q, f0 + j, i)
                        if pieces:
                            ada_dve(dve, steps, q, piece + j // 2, j % 2, i, pieces)
                    steps.end_loop(turns)
                f0, piece = f0 + 4 * turns, piece + pieces * turns
            for f in range(f0, nf):
                ffn_tile_dve(dve, steps, q, f)
            unit_products(dve, FIRST_UNIT[f"ffn{q}"], 3 * nf - 1)
            residual_dve(dve, steps, k, kind == 2, "acc")
            n0, n1 = PIECE_BASE[q], PIECE_BASE[q + 1]
            if n1 > n0:
                dve.wait_ge(ada_cols, q + 1)
                a = COL["ada_b"]
                steps.mark(nc.vector.tensor_tensor(mods[:, 4 * n0:4 * n1], ps[:, 4, 0:4 * (n1 - n0)],
                                                   cols[:, a + 4 * n0:a + 4 * n1], ALU.add))
                steps.wait()

        def ffn_pool(pool, q):
            k, nf, kind, loops = FFN[q]
            piece = PIECE_BASE[q]
            if PIECE_BASE[q + 1] == piece:
                return
            pool.wait_ge(h_ready, 8 * k)
            for turns, pieces in loops:
                if not pieces:
                    continue
                for s in range(2):
                    if piece + s >= 2:
                        pool.wait_ge(ada_summed, piece + s - 1)
                    pool.dma_start(ada_ring[:, s], dram["ada"][piece + s]).then_inc(ada_loaded[s], 16)
                with pool.Fori(1, turns) as i:
                    for s in range(2):
                        pool.wait_ge(ada_summed, piece + 2 * i + s - 1)
                        pool.dma_start(ada_ring[:, s], dram["ada"][piece + 2 * i + s]).then_inc(ada_loaded[s], 16)
                piece += pieces * turns

        at_ = Carver(arena, AR)
        qk = at_.cut(10, T)
        vtok = at_.cut(2, 512)
        sco = at_.cut(4, 384)
        prb = at_.cut(4, 384)
        prT = at_.cut(12, P)
        cosb, sinb = at_.cut(T), at_.cut(T)
        ang, turns_, resid, absr = at_.cut(T), at_.cut(T), at_.cut(T), at_.cut(T)
        pjr, pjs, pjroot, pjn = at_.cut(2, T), at_.cut(2, T), at_.cut(2, T), at_.cut(2, T)
        ropa, ropb = at_.cut(2, T), at_.cut(2, T)
        mx, mm, nm, sd, sm = at_.cut(4, 3), at_.cut(4, 2), at_.cut(4, 2), at_.cut(4, 2), at_.cut(4, 2)
        es, tot, rec = at_.cut(4, 2), at_.cut(4, 2), at_.cut(4, 2)
        alibi = at_.cut(8, 384)

        TWO_PI = 2 * np.pi
        C1 = 6.28125
        C2 = float(np.round((TWO_PI - C1) * 2**20) / 2**20)
        C3 = float(TWO_PI - C1 - C2)
        PI_IN = float(np.nextafter(np.float32(np.pi), np.float32(0)))

        def angles_dve(dve, steps):
            dve.wait_ge(small_loaded, 16 * N_SMALL)
            m, w = steps.mark, steps.wait
            m(nc.vector.tensor_scalar(ang, positions[:], col("inv_freq"), None, ALU.mult))
            w()
            m(nc.vector.tensor_scalar(turns_, ang, 1.0 / TWO_PI, None, ALU.mult))
            w()
            m(nc.vector.tensor_scalar(turns_, turns_, MAGIC, None, ALU.add))
            w()
            m(nc.vector.tensor_scalar(turns_, turns_, -MAGIC, None, ALU.add))
            w()
            for c_ in (C1, C2, C3):
                m(nc.vector.scalar_tensor_tensor(ang, turns_, -c_, ang, ALU.mult, ALU.add))
                w()
            m(nc.vector.tensor_scalar(resid, ang, PI_IN, -PI_IN, ALU.min, ALU.max))
            w()
            m(nc.vector.tensor_scalar(absr, resid, -1.0, None, ALU.mult))
            w()
            nc.vector.tensor_tensor(absr, absr, resid, ALU.max).then_inc(angle_ready, 1)

        def angles_act(act):
            act.wait_ge(angle_ready, 1)
            nc.scalar.activation(sinb, resid, ACT.Sin)
            nc.scalar.activation(cosb, absr, ACT.Sin, scale=-1.0, bias=col("half_pi")).then_inc(sine_ready, 1)

        def attn_in_pe(pe):
            first = FIRST_UNIT["attn_in"]
            for t in range(12):
                if t < 10:
                    if t == 0:
                        for c in range(C):
                            pe.wait_ge(u_ready, u_count(0, c))
                    if t >= 2:
                        pe.wait_ge(pjsq_ready, t - 1)
                    s = take_unit(pe, first, t)
                    for k in range(C):
                        last = nc.tensor.matmul(ps[:, t % 2, 0:T], ring[:, s, k], u[:, k], start=(k == 0), stop=(k == C - 1))
                    last.then_inc(unit_done[s], 1)
                if 0 <= t - 1 < 10:
                    a = t - 1
                    pe.wait_ge(pjsq_ready, a + 1)
                    if a >= 2:
                        pe.wait_ge(pjroot_ready, a - 1)
                    nc.tensor.matmul(ps[:, 2 + a % 2, 0:T], const("block_ones"), pjs[:, a % 2], start=True, stop=True).then_inc(pjss_ready, 1)
                if 0 <= t - 2 < 10:
                    a = t - 2
                    pe.wait_ge(qn_ready, a + 1)
                    if a >= 2:
                        pe.wait_ge(rope_ready, a - 1)
                    nc.tensor.matmul(ps[:, 4 + a % 2, 0:T], const("rotate"), pjn[:, a % 2], start=True, stop=True).then_inc(rot_ready, 1)
            for n in range(2):
                s = take_unit(pe, first, 10 + n)
                for tb in range(2):
                    for k in range(C):
                        last = nc.tensor.matmul(ps[:, 6, tb * 256 + n * P:tb * 256 + (n + 1) * P], u[:, k, tb * P:(tb + 1) * P],
                                                ring[:, s, k], start=(n == 0 and tb == 0 and k == 0), stop=(k == C - 1),
                                                skip_group_check=True)
                last.then_inc(unit_done[s], 1)

        def attn_in_act(act):
            for t in range(11):
                if t < 10:
                    unit_products(act, FIRST_UNIT["attn_in"], t)
                    if t >= 2:
                        act.wait_ge(qn_ready, t - 1)
                    nc.scalar.activation(pjr[:, t % 2], ps[:, t % 2, 0:T], ACT.Copy)
                    nc.scalar.activation(pjs[:, t % 2], ps[:, t % 2, 0:T], ACT.Square).then_inc(pjsq_ready, 1)
                if t >= 1:
                    a = t - 1
                    act.wait_ge(pjss_ready, a + 1)
                    nc.scalar.activation(pjroot[:, a % 2], ps[:, 2 + a % 2, 0:T], ACT.Sqrt, bias=col("eps"), scale=1.0 / HD).then_inc(pjroot_ready, 1)
            for t in (10, 11):
                unit_products(act, FIRST_UNIT["attn_in"], t)
            nc.scalar.activation(vtok[:, :, 0:256], ps[:, 6, :].rearrange("p (a b) -> p a b", a=2), ACT.Copy).then_inc(v_copied, 1)

        def attn_in_dve(dve, steps):
            m, w = steps.mark, steps.wait
            dve.wait_ge(sine_ready, 1)
            for t in range(11):
                if t < 10:
                    r = t % 2
                    dve.wait_ge(pjroot_ready, t + 1)
                    m(nc.vector.reciprocal(pjroot[:, r], pjroot[:, r]))
                    if t >= 2:
                        dve.wait_ge(rot_ready, t - 1)
                    w()
                    nc.vector.scalar_tensor_tensor(pjn[:, r], pjr[:, r], col("k_gain" if t < 2 else "q_gain"), pjroot[:, r],
                                                   ALU.mult, ALU.mult).then_inc(qn_ready, 1)
                if t >= 1:
                    a, r = t - 1, (t - 1) % 2
                    dve.wait_ge(rot_ready, a + 1)
                    dve.wait_ge(qn_ready, a + 1)
                    m(nc.vector.tensor_tensor(ropa[:, r], pjn[:, r], cosb, ALU.mult))
                    m(nc.vector.tensor_tensor(ropb[:, r], ps[:, 4 + r, 0:T], sinb, ALU.mult))
                    w()
                    nc.vector.tensor_tensor(qk[:, a], ropa[:, r], ropb[:, r], ALU.add).then_inc(rope_ready, 1)

        BATCHES = [4, 2]

        def head_of(which, b, j):
            jt, half = 2 * b + j // 2, j % 2
            if which == 0:
                g = 2 * (jt // 4) + half
                return 2 + jt, half, jt // 4, 64 * g, jt
            return jt, half, 4 + jt, 64 * (2 * jt + half), 4 + jt

        def core_pe(pe, which):
            if which == 0:
                pe.wait_ge(rope_ready, 10)
            else:
                pe.wait_ge(qk1_ready, 8)
            base = 4 * which
            for b in range(BATCHES[which]):
                n = base + b
                if b:
                    pe.wait_ge(max_ready, n)
                for j in range(4):
                    qt, half, kt, vc, oc = head_of(which, b, j)
                    rows = slice(64 * half, 64 * half + 64)
                    nc.tensor.matmul(ps[:, j, 0:P], qk[rows, qt, 0:P], qk[rows, kt, 0:P], start=True, stop=True)
                    last = nc.tensor.matmul(ps[:, j, P:384], qk[rows, qt, P:T], qk[rows, kt, 0:T], start=True, stop=True)
                last.then_inc(sc_ready, 1)
                pe.wait_ge(p_ready, n + 1)
                if b:
                    pe.wait_ge(ptc_ready, n)
                for j in range(4):
                    for t in range(3):
                        x = 3 * j + t
                        last = nc.tensor.transpose(ps[:, 4 + x // 4, (x % 4) * P:(x % 4 + 1) * P], prb[:, j, t * P:(t + 1) * P], ident)
                last.then_inc(pt_ready, 1)
                pe.wait_ge(ptc_ready, n + 1)
                pe.wait_ge(v_copied, which + 1)
                if b:
                    pe.wait_ge(mix_ready, CORE_MIX[which] + b)
                for j in range(4):
                    qt, half, kt, vc, oc = head_of(which, b, j)
                    at = (j // 2) * T
                    o = ps[64 * half:64 * half + 64, 7]
                    nc.tensor.matmul(o[:, at:at + P], vtok[:, 0, vc:vc + 64], prT[:, 3 * j], start=True, stop=True)
                    nc.tensor.matmul(o[:, at + P:at + T], vtok[:, 0, vc:vc + 64], prT[:, 3 * j + 1], start=True, stop=False)
                    last = nc.tensor.matmul(o[:, at + P:at + T], vtok[:, 1, vc:vc + 64], prT[:, 3 * j + 2], start=False, stop=True)
                last.then_inc(pv_ready, 1)

        CORE_MIX = [0, 16]

        def core_act(act, which):
            base = 4 * which
            for b in range(BATCHES[which]):
                n = base + b
                act.wait_ge(max_ready, n + 1)
                if b:
                    act.wait_ge(pt_ready, n)
                for j in range(4):
                    nc.scalar.activation(prb[:, j, 0:P], sco[:, j, 0:P], ACT.Exp, bias=nm[:, j, 0:1], accum_out=sm[:, j, 0:1])
                    last = nc.scalar.activation(prb[:, j, P:384], sco[:, j, P:384], ACT.Exp, bias=nm[:, j, 1:2], accum_out=sm[:, j, 1:2])
                if which == 0:
                    last = nc.scalar.activation(es, sd, ACT.Exp)
                last.then_inc(exp_ready, 1)
                act.wait_ge(pt_ready, n + 1)
                if b:
                    act.wait_ge(pv_ready, n)
                for x in range(3):
                    last = nc.scalar.activation(prT[:, 4 * x:4 * x + 4].rearrange("p a b -> p (a b)"), ps[:, 4 + x, :], ACT.Copy)
                last.then_inc(ptc_ready, 1)
                act.wait_ge(pv_ready, n + 1)
                oc = head_of(which, b, 0)[4]
                nc.scalar.activation(mix[:, oc:oc + 2].rearrange("p a b -> p (a b)"), ps[:, 7, :], ACT.Copy).then_inc(mix_ready, 1)

        def core_dve(dve, steps, which):
            m, w = steps.mark, steps.wait
            base = 4 * which
            for b in range(BATCHES[which]):
                n = base + b
                dve.wait_ge(sc_ready, n + 1)
                if b:
                    dve.wait_ge(exp_ready, n)
                for j in range(4):
                    bias = const("window_mask") if which == 0 else alibi[:, 4 * b + j]
                    m(nc.vector.scalar_tensor_tensor(sco[:, j], ps[:, j, 0:384], HD ** -0.5, bias, ALU.mult, ALU.add))
                w()
                m(nc.vector.tensor_reduce(mx.rearrange("p a b -> p (a b)"), sco.rearrange("p j (t k) -> p (j t) k", t=3), AX_X, ALU.max))
                w()
                m(nc.vector.tensor_copy(mm[:, :, 0], mx[:, :, 0]))
                m(nc.vector.tensor_tensor(mm[:, :, 1], mx[:, :, 1], mx[:, :, 2], ALU.max))
                w()
                if which == 0:
                    sk = cols[:, COL["sinks"] + 4 * b:COL["sinks"] + 4 * b + 4].unsqueeze(2).to_broadcast([P, 4, 2])
                    m(nc.vector.tensor_tensor(mm, mm, sk, ALU.max))
                    w()
                    m(nc.vector.tensor_tensor(sd, sk, mm, ALU.subtract))
                ins = nc.vector.tensor_scalar(nm, mm, -1.0, None, ALU.mult)
                m(ins)
                w()
                m2 = nc.vector.tensor_copy(mx[:, :, 0], nm[:, :, 0])
                m2.then_inc(max_ready, 1)
                dve.wait_ge(exp_ready, n + 1)
                if which == 0:
                    m(nc.vector.tensor_tensor(tot, sm, es, ALU.add))
                    w()
                    m(nc.vector.reciprocal(rec, tot))
                else:
                    m(nc.vector.reciprocal(rec, sm))
                w()
                for j in range(4):
                    m(nc.vector.tensor_scalar(prb[:, j, 0:P], prb[:, j, 0:P], rec[:, j, 0:1], None, ALU.mult))
                    m(nc.vector.tensor_scalar(prb[:, j, P:384], prb[:, j, P:384], rec[:, j, 1:2], None, ALU.mult))
                w()
                nc.vector.tensor_copy(mx[:, :, 1], rec[:, :, 0]).then_inc(p_ready, 1)

        qk1_ready = sem("moba_qk_ready")

        g_gates, g_rows_out, g_rows, g_cols, g_colsx = (sem(n) for n in (
            "gates_ready", "gates_stored", "gate_rows_loaded", "gate_cols_ready", "gate_cols_exp"))
        g_soft, g_texp, g_tabs = sem("softplus_ready"), sem("table_arg_ready"), sem("tables_exp")
        g_tap, g_conv, g_silu, g_z = sem("g_tap"), sem("g_conv"), sem("g_silu"), sem("g_z")
        g_sq, g_ss, g_root, g_qkn = sem("g_squares"), sem("g_sums"), sem("g_root"), sem("g_qk_normed")
        g_vt, g_vb, g_kt, g_kk, g_ktok, g_kb, g_kd = (sem(n) for n in (
            "g_v_turned", "g_v_scaled", "g_k_turned", "g_kk", "g_k_copied", "g_k_scaled", "g_k_decayed"))
        g_egr_in, g_egr, g_mt, g_qkm, g_bt, g_x, g_p, g_pc, g_dx = (sem(n) for n in (
            "g_rows_loaded", "g_rows_exp", "g_mt", "g_qk_masked", "g_level_masked", "g_inverse", "g_bx", "g_bx_copied", "g_xbx"))
        g_uw, g_u, g_wt, g_qd, g_s = (sem(n) for n in ("g_uw", "g_u_copied", "g_w_copied", "g_q_decayed", "g_state"))
        pe_waited = sem("pe_waited")
        g_ws, g_vn, g_op, g_kv, g_o = (sem(n) for n in ("g_ws", "g_v_new", "g_out", "g_kv", "g_out_copied"))

        gd = Carver(arena, AR)
        m_tab, mt_tab, qk_tab = gd.cut(GH, 2, CH), gd.cut(GH, 2, CH), gd.cut(GH, 2, CH)
        cbuf, qkv, zs, egr = gd.cut(8, T), gd.cut(8, T), gd.cut(4, T), gd.cut(4, T)
        gsq_at = gd.at
        gsq, grt = gd.cut(4, T), gd.cut(4, T)
        kb, kd, vb = gd.cut(4, 2, P), gd.cut(4, 2, P), gd.cut(4, 2, P)
        m_, mt_, qk_ = gd.cut(4, 2, CH), gd.cut(4, 2, CH), gd.cut(4, 2, CH)
        bt, x_, xt_, p1, ktok = gd.cut(5, 8, CH), gd.cut(8, CH), gd.cut(8, CH), gd.cut(8, CH), gd.cut(4, P)
        qd, state, vnew, ot = gd.cut(4, T), gd.cut(4, P), gd.cut(4, P), gd.cut(4, T)
        uu = cbuf[:, 0:4].rearrange("p a (b c) -> p (a b) c", b=2)
        wt = cbuf[:, 4:8]
        bcol, gcol, ecol, kbcol, nea = gd.cut(2, GH), gd.cut(2, GH), gd.cut(2, GH), gd.cut(2, GH), gd.cut(1)
        gates, xa, ta, tb_ = ot[:, 0], ot[:, 1], ot[:, 2], ot[:, 3]
        g_row = qkv.rearrange("p a b -> p (a b)").rearrange("p (h t s) -> p h t s", h=GH, t=2)
        b_row = arena[:, gsq_at:gsq_at + 2 * 4 * T].rearrange("p (h t s) -> p h t s", h=GH, t=2)
        N_TURNS = GH // GB

        def gdn_gates_pe(pe):
            first = FIRST_UNIT["gdn_gates"]
            for c in range(C):
                pe.wait_ge(u_ready, u_count(2, c))
            s = take_unit(pe, first, 0)
            for k in range(C):
                last = nc.tensor.matmul(ps[:, 0, 0:T], ring[:, s, k], u[:, k], start=(k == 0), stop=(k == C - 1))
            last.then_inc(unit_done[s], 1)
            pe.wait_ge(g_gates, 1)
            for t in range(2):
                last = nc.tensor.matmul(ps[:, 7, 64 * t:64 * t + 48], gates[0:48, t * P:(t + 1) * P], ident[0:48, 0:48],
                                        start=True, stop=True)
            last.then_inc(g_cols, 1)

        def gdn_gates_act(act, steps):
            m, w = steps.mark, steps.wait
            unit_products(act, FIRST_UNIT["gdn_gates"], 0)
            act.wait_ge(g_soft, 1)
            m(nc.scalar.activation(gates[0:16], ps[0:16, 0, 0:T], ACT.Sigmoid))
            a = slice(32, 48)
            m(nc.scalar.activation(xa[a], ps[a, 0, 0:T], ACT.Identity, bias=cols[a, COL["dt_bias"]:COL["dt_bias"] + 1]))
            w()
            m(nc.scalar.activation(ta[a], xa[a], ACT.Abs))
            w()
            m(nc.scalar.activation(ta[a], ta[a], ACT.Exp, scale=-1.0))
            m(nc.scalar.activation(nea[a], cols[a, COL["a_log"]:COL["a_log"] + 1], ACT.Exp))
            w()
            nc.scalar.activation(ta[a], ta[a], ACT.Ln, bias=cols[a, COL["one"]:COL["one"] + 1]).then_inc(g_soft, 1)
            act.wait_ge(g_colsx, 1)
            nc.scalar.activation(ecol, gcol, ACT.Exp).then_inc(g_colsx, 1)
            act.wait_ge(g_texp, 2)
            nc.scalar.activation(qk_tab, qk_tab, ACT.Exp).then_inc(g_tabs, 1)
            nc.scalar.activation(m_tab, m_tab, ACT.Exp).then_inc(g_tabs, 1)

        def gdn_gates_dve(dve, steps):
            m, w = steps.mark, steps.wait
            a = slice(32, 48)
            nc.vector.memset(gates[0:64], 0.0).then_inc(g_soft, 1)
            dve.wait_ge(g_soft, 2)
            m(nc.vector.tensor_scalar(tb_[a], xa[a], 0.0, None, ALU.max))
            m(nc.vector.tensor_scalar(nea[a], nea[a], -1.0, None, ALU.mult))
            w()
            m(nc.vector.tensor_tensor(tb_[a], tb_[a], ta[a], ALU.add))
            w()
            m(nc.vector.tensor_scalar(tb_[a], tb_[a], nea[a], None, ALU.mult))
            w()
            at, _ = CONST["reset"]
            nc.vector.tensor_tensor_scan(gates[a], consts[a, at:at + T], tb_[a], 0.0, ALU.mult, ALU.add).then_inc(g_gates, 1)
            dve.wait_ge(g_cols, 1)
            cols_ = ps[:, 7, 0:2 * 64].rearrange("p (t n) -> p t n", t=2)
            m(nc.vector.tensor_copy(bcol, cols_[:, :, 0:16]))
            nc.vector.tensor_copy(gcol, cols_[:, :, 32:48]).then_inc(g_colsx, 1)
            dve.wait_ge(g_colsx, 2)
            m(nc.vector.tensor_tensor(kbcol, bcol, ecol, ALU.mult))
            dve.wait_ge(g_rows, 64)
            gc4 = gcol.rearrange("p t h -> p h t").unsqueeze(3).to_broadcast([P, GH, 2, CH])
            bc4 = bcol.rearrange("p t h -> p h t").unsqueeze(3).to_broadcast([P, GH, 2, CH])
            flat = lambda x: x.rearrange("p h t s -> p (h t) s")
            each = lambda name: const(name).unsqueeze(1).to_broadcast([P, GH * 2, CH])
            m(nc.vector.tensor_tensor(mt_tab, g_row, gc4, ALU.subtract))
            w()
            nc.vector.tensor_tensor(flat(qk_tab), flat(mt_tab), each("incl_up_neg"), ALU.add).then_inc(g_texp, 1)
            nc.vector.scalar_tensor_tensor(flat(m_tab), flat(mt_tab), -1.0, each("strict_lo_neg"), ALU.mult, ALU.add).then_inc(g_texp, 1)
            dve.wait_ge(g_tabs, 1)
            m(nc.vector.tensor_tensor(mt_tab, qk_tab, b_row, ALU.mult))
            w()
            m(nc.vector.tensor_tensor(flat(mt_tab), flat(mt_tab), each("strict_up"), ALU.mult))
            dve.wait_ge(g_tabs, 2)
            m(nc.vector.tensor_tensor(m_tab, m_tab, bc4, ALU.mult))
            w()

        def gdn_gates_pool(pool):
            pool.wait_ge(g_gates, 1)
            pool.dma_start(gates_dram[0], gates[0:16]).then_inc(g_rows_out, 16)
            pool.dma_start(gates_dram[1], gates[32:48]).then_inc(g_rows_out, 16)
            pool.wait_ge(g_rows_out, 32)
            for n, dst in ((0, b_row), (1, g_row)):
                for half in range(2):
                    src = gates_dram[n].rearrange("h (t f s) -> f h t s", t=2, f=2)[half].partition_broadcast(64)
                    pool.dma_start(dst[64 * half:64 * half + 64], src).then_inc(g_rows, 16)

        def gdn_turn_pool(pool, i):
            pool.wait_ge(g_s, 5 * i + 1)
            pool.dma_start(egr, gates_dram[1][bass.ds(4 * i, 4), :].partition_broadcast(P)).then_inc(g_egr_in, 16)
            pool.wait_ge(g_mt, i + 1)
            for lv in range(1, 6):
                up = const("level_up", lv, CH).unsqueeze(1).to_broadcast([P, 8, CH])
                nc.gpsimd.tensor_tensor(bt[:, lv - 1], mt_.rearrange("p h t s -> p (h t) s"), up, ALU.mult).then_inc(g_bt, 1)

        def small_tiles(pe):
            pe.sem_inc(pe_waited, 1)

        def gdn_turn_pe(pe, i):
            first = FIRST_UNIT["gdn_in"]
            for j in range(12):
                if j >= 4:
                    pe.wait_ge(g_conv, 8 * i + j - 3)
                s = take_unit(pe, first, j, 12, i)
                for k in range(C):
                    last = nc.tensor.matmul(ps[:, j % 4, 0:T], ring[:, s, k], u[:, k], start=(k == 0), stop=(k == C - 1))
                last.then_inc(unit_done[s], 1)
            pe.wait_ge(g_silu, 8 * i + 8)
            for n in range(4):
                for t in range(2):
                    x = 2 * n + t
                    last = nc.tensor.transpose(ps[:, 6 + x // 4, (x % 4) * P:(x % 4 + 1) * P], qkv[:, 4 + n, t * P:(t + 1) * P], ident)
            last.then_inc(g_vt, 1)
            pe.wait_ge(g_sq, 2 * i + 1)
            for n in range(2):
                last = nc.tensor.matmul(ps[:, 4 + n], ones, gsq[:, 2 * n:2 * n + 2], start=True, stop=True)
            last.then_inc(g_ss, 1)
            pe.wait_ge(g_qkn, i + 1)
            for n in range(2):
                for t in range(2):
                    last = nc.tensor.transpose(ps[:, 4, (2 * n + t) * P:(2 * n + t + 1) * P], qkv[:, 2 + n, t * P:(t + 1) * P], ident)
            last.then_inc(g_kt, 1)
            for q in range(2):
                for n in range(2):
                    for c in range(4):
                        tk = slice(c * CH, (c + 1) * CH)
                        at = 256 * q + 128 * n + 64 * (c // 2)
                        rhs = qkv[:, 2 + n, tk] if q == 0 else qkv[:, n, tk]
                        last = nc.tensor.matmul(ps[64 * (c % 2):64 * (c % 2) + 64, 5, at:at + 64], qkv[:, 2 + n, tk], rhs, start=True, stop=True)
            last.then_inc(g_kk, 1)
            for lv in range(1, 6):
                pe.wait_ge(g_x, 6 * i + lv)
                pe.wait_ge(g_bt, 5 * i + lv)
                if lv == 1:
                    pe.wait_ge(g_ktok, i + 1)
                small_tiles(pe)
                for n in range(8):
                    for f in range(2):
                        r = slice(64 * f, 64 * f + 64)
                        last = nc.tensor.matmul(ps[r, 4, 64 * n:64 * n + 64], bt[r, lv - 1, n], x_[r, n], start=True, stop=True)
                last.then_inc(g_p, 1)
                pe.wait_ge(g_pc, 5 * i + lv)
                small_tiles(pe)
                for which in range(2):
                    if which == 0 and lv == 5:
                        continue
                    for n in range(8):
                        for f in range(2):
                            r = slice(64 * f, 64 * f + 64)
                            o = ps[r, 5 + which, 64 * n:64 * n + 64]
                            if which == 0:
                                last = nc.tensor.matmul(o, xt_[r, n], p1[r, n], start=True, stop=True)
                            else:
                                last = nc.tensor.matmul(o, p1[r, n], xt_[r, n], start=True, stop=True)
                last.then_inc(g_dx, 1)
            pe.wait_ge(g_x, 6 * i + 6)
            pe.wait_ge(g_vb, i + 1)
            pe.wait_ge(g_kb, i + 1)
            small_tiles(pe)
            for n in range(8):
                for f in range(2):
                    r = slice(64 * f, 64 * f + 64)
                    nc.tensor.matmul(ps[r, 4 + n // 4, (n % 4) * P:(n % 4 + 1) * P], xt_[r, n], vb[r, n // 2, n % 2], start=True, stop=True)
                    last = nc.tensor.matmul(ps[:, 6 + f, 64 * n:64 * n + 64], kb[r, n // 2, n % 2], xt_[r, n], start=True, stop=True)
            last.then_inc(g_uw, 1)
            pe.wait_ge(g_u, i + 1)
            pe.wait_ge(g_wt, i + 1)
            pe.wait_ge(g_qd, i + 1)
            for c in range(4):
                f, t = c % 2, c // 2
                r, tk = slice(64 * f, 64 * f + 64), slice(c * CH, (c + 1) * CH)
                pe.wait_ge(g_s, 5 * i + c + 1)
                for n in range(4):
                    last = nc.tensor.matmul(ps[r, 4, n * P:(n + 1) * P], wt[:, n, tk], state[:, n], start=True, stop=True)
                last.then_inc(g_ws, 1)
                if c:
                    pe.wait_ge(g_o, 4 * i + c)
                for n in range(4):
                    nc.tensor.matmul(ps[:, 5, n * CH:(n + 1) * CH], state[:, n], qd[:, n, tk], start=(n == 0), stop=False, skip_group_check=True)
                pe.wait_ge(g_vn, 4 * i + c + 1)
                for n in range(4):
                    last = nc.tensor.matmul(ps[:, 6, n * P:(n + 1) * P], kd[r, n, t], vnew[r, n], start=True, stop=True)
                last.then_inc(g_kv, 1)
                for n in range(4):
                    last = nc.tensor.matmul(ps[:, 5, n * CH:(n + 1) * CH], vnew[r, n], qk_[r, n, t], start=False, stop=True, skip_group_check=True)
                last.then_inc(g_op, 1)
            pe.wait_ge(g_sq, 2 * i + 2)
            pe.wait_ge(g_s, 5 * i + 5)
            for n in range(2):
                last = nc.tensor.matmul(ps[:, 6 + n], ones, gsq[:, 2 * n:2 * n + 2], start=True, stop=True)
            last.then_inc(g_ss, 1)

        def gdn_turn_act(act, steps, i):
            m, w = steps.mark, steps.wait
            first = FIRST_UNIT["gdn_in"]
            wc = COL["gdn_conv"]
            for j in range(9):
                if j < 8:
                    unit_products(act, first, j, 12, i)
                    nc.scalar.activation(cbuf[:, j], ps[:, j % 4, 0:T], ACT.Identity,
                                         scale=cols[:, bass.ds(wc + 4 * j + 3 + 32 * i, 1)]).then_inc(g_tap, 1)
                if j:
                    act.wait_ge(g_conv, 8 * i + j)
                    nc.scalar.activation(qkv[:, j - 1], cbuf[:, j - 1], ACT.Silu).then_inc(g_silu, 1)
            for j in range(4):
                unit_products(act, first, 8 + j, 12, i)
                m(nc.scalar.activation(zs[:, j], ps[:, j, 0:T], ACT.Silu))
            act.wait_ge(g_silu, 8 * i + 4)
            nc.scalar.activation(gsq, qkv[:, 0:4], ACT.Square).then_inc(g_sq, 1)
            act.wait_ge(g_vt, i + 1)
            for n in range(4):
                for t in range(2):
                    x = 2 * n + t
                    last = nc.scalar.activation(vb[:, n, t], ps[:, 6 + x // 4, (x % 4) * P:(x % 4 + 1) * P], ACT.Copy,
                                                scale=bcol[:, t, bass.ds(4 * i + n, 1)])
            last.then_inc(g_vb, 1)
            act.wait_ge(g_ss, 2 * i + 1)
            nc.scalar.activation(grt.rearrange("p a b -> p (a b)"), ps[:, 4:6].rearrange("p a b -> p (a b)"), ACT.Sqrt, bias=col("eps")).then_inc(g_root, 1)
            act.wait_ge(g_egr_in, 16 * i + 16)
            nc.scalar.activation(egr, egr, ACT.Exp).then_inc(g_egr, 1)
            act.wait_ge(g_kt, i + 1)
            nc.scalar.activation(ktok.rearrange("p a b -> p (a b)"), ps[:, 4], ACT.Copy).then_inc(g_ktok, 1)
            act.wait_ge(g_ktok, i + 1)
            for n in range(4):
                for t in range(2):
                    last = nc.scalar.activation(kb[:, n, t], ktok[:, 2 * (n // 2) + t], ACT.Copy, scale=kbcol[:, t, bass.ds(4 * i + n, 1)])
            last.then_inc(g_kb, 1)
            for lv in range(1, 6):
                act.wait_ge(g_p, 5 * i + lv)
                nc.scalar.activation(p1.rearrange("p a b -> p (a b)"), ps[:, 4], ACT.Copy).then_inc(g_pc, 1)
            act.wait_ge(g_uw, i + 1)
            nc.scalar.activation(uu.rearrange("p a b -> p (a b)"), ps[:, 4:6].rearrange("p a b -> p (a b)"), ACT.Copy).then_inc(g_u, 1)
            for c in range(4):
                act.wait_ge(g_op, 4 * i + c + 1)
                nc.scalar.activation(ot[:, :, c * CH:(c + 1) * CH], ps[:, 5, 0:256].rearrange("p (a b) -> p a b", a=4), ACT.Copy).then_inc(g_o, 1)
            act.wait_ge(g_o, 4 * i + 4)
            nc.scalar.activation(gsq, ot, ACT.Square).then_inc(g_sq, 1)
            act.wait_ge(g_ss, 2 * i + 2)
            nc.scalar.activation(grt.rearrange("p a b -> p (a b)"), ps[:, 6:8].rearrange("p a b -> p (a b)"), ACT.Sqrt, bias=col("eps"),
                                 scale=1.0 / P).then_inc(g_root, 1)

        def gdn_turn_dve(dve, steps, i):
            m, w = steps.mark, steps.wait
            wc = COL["gdn_conv"]
            nc.vector.memset(state, 0.0).then_inc(g_s, 1)
            for j in range(8):
                dve.wait_ge(g_tap, 8 * i + j + 1)
                for tap in range(3):
                    d = 3 - tap
                    ins = nc.vector.scalar_tensor_tensor(cbuf[:, j, d:T], ps[:, j % 4, 0:T - d],
                                                         cols[:, bass.ds(wc + 4 * j + tap + 32 * i, 1)], cbuf[:, j, d:T], ALU.mult, ALU.add)
                    if tap < 2:
                        m(ins)
                        w()
                    else:
                        ins.then_inc(g_conv, 1)
            dve.wait_ge(g_root, 2 * i + 1)
            m(nc.vector.reciprocal(grt, grt))
            w()
            m(nc.vector.scalar_tensor_tensor(qkv[:, 0:2], qkv[:, 0:2], P ** -0.5, grt[:, 0:2], ALU.mult, ALU.mult))
            w()
            nc.vector.tensor_tensor(qkv[:, 2:4], qkv[:, 2:4], grt[:, 2:4], ALU.mult).then_inc(g_qkn, 1)
            dve.wait_ge(g_kk, i + 1)
            for q, (dst, tab) in enumerate(((m_, m_tab), (mt_, mt_tab), (qk_, qk_tab))):
                for n in range(2):
                    at = 128 * n + (256 if q == 2 else 0)
                    kk = ps[:, 5, at:at + 128].unsqueeze(1).to_broadcast([P, 2, 128])
                    ins = nc.vector.tensor_tensor(dst[:, 2 * n:2 * n + 2].rearrange("p a b c -> p a (b c)"), kk,
                                                  tab[:, bass.ds(4 * i + 2 * n, 2)].rearrange("p a b c -> p a (b c)"), ALU.mult)
                    if q == 1 and n == 1:
                        ins.then_inc(g_mt, 1)
                    elif q == 2 and n == 1:
                        ins.then_inc(g_qkm, 1)
                    else:
                        m(ins)
            w()
            dve.wait_ge(g_mt, i + 1)
            eye = const("stack_ident").unsqueeze(1).to_broadcast([P, 8, CH])
            lo = const("level_lo").unsqueeze(1).to_broadcast([P, 8, CH])
            up = const("level_up", 0, CH).unsqueeze(1).to_broadcast([P, 8, CH])
            m(nc.vector.tensor_tensor(x_, m_.rearrange("p a b c -> p (a b) c"), lo, ALU.mult))
            m(nc.vector.tensor_tensor(xt_, mt_.rearrange("p a b c -> p (a b) c"), up, ALU.mult))
            w()
            m(nc.vector.tensor_tensor(x_, eye, x_, ALU.subtract))
            nc.vector.tensor_tensor(xt_, eye, xt_, ALU.subtract).then_inc(g_x, 1)
            dve.wait_ge(g_ktok, i + 1)
            for n in range(4):
                for t in range(2):
                    dcol = qk_tab[:, bass.ds(4 * i + n, 1), t, CH - 1]
                    ins = nc.vector.tensor_scalar(kd[:, n, t], ktok[:, 2 * (n // 2) + t], dcol, None, ALU.mult)
                    m(ins)
            dve.wait_ge(g_egr, i + 1)
            for n in range(2):
                ins = nc.vector.tensor_tensor(qd[:, 2 * n:2 * n + 2], qkv[:, n].unsqueeze(1).to_broadcast([P, 2, T]), egr[:, 2 * n:2 * n + 2], ALU.mult)
                if n == 0:
                    m(ins)
                else:
                    ins.then_inc(g_qd, 1)
            for lv in range(1, 6):
                dve.wait_ge(g_dx, 5 * i + lv)
                flat = lambda x: x.rearrange("p a b -> p (a b)")
                if lv < 5:
                    m(nc.vector.tensor_tensor(flat(x_), flat(x_), ps[:, 5], ALU.subtract))
                nc.vector.tensor_tensor(flat(xt_), flat(xt_), ps[:, 6], ALU.subtract).then_inc(g_x, 1)
            dve.wait_ge(g_uw, i + 1)
            nc.vector.tensor_copy(wt.rearrange("p h (t f s) -> p (h t) f s", t=2, f=2),
                                  ps[:, 6:8].rearrange("p f (n s) -> p n f s", n=8)).then_inc(g_wt, 1)
            dve.wait_ge(g_u, i + 1)
            for c in range(4):
                f, t = c % 2, c // 2
                r = slice(64 * f, 64 * f + 64)
                dve.wait_ge(g_ws, 4 * i + c + 1)
                ut = uu[r].rearrange("p (a b) c -> p a b c", b=2)[:, :, t]
                nc.vector.tensor_tensor(vnew[r], ut, ps[r, 4].rearrange("p (a b) -> p a b", a=4), ALU.subtract).then_inc(g_vn, 1)
                dve.wait_ge(g_kv, 4 * i + c + 1)
                for n in range(4):
                    ins = nc.vector.scalar_tensor_tensor(state[:, n], state[:, n], egr[:, n, c * CH + CH - 1:c * CH + CH],
                                                         ps[:, 6, n * P:(n + 1) * P], ALU.mult, ALU.add)
                    if n < 3:
                        m(ins)
                ins.then_inc(g_s, 1)
            dve.wait_ge(g_root, 2 * i + 2)
            m(nc.vector.reciprocal(grt, grt))
            w()
            m(nc.vector.scalar_tensor_tensor(ot, ot, col("gdn_norm"), grt, ALU.mult, ALU.mult))
            w()
            nc.vector.tensor_tensor(mix[:, bass.ds(4 * i, 4)], ot, zs, ALU.mult).then_inc(mix_ready, 1)

        def gdn_pe(pe):
            gdn_gates_pe(pe)
            with pe.Fori(0, N_TURNS) as i:
                gdn_turn_pe(pe, i)

        def gdn_act(act, steps):
            gdn_gates_act(act, steps)
            with act.Fori(0, N_TURNS) as i:
                steps.start_loop(i, 4)
                gdn_turn_act(act, steps, i)
                steps.end_loop(N_TURNS)

        def gdn_dve(dve, steps):
            gdn_gates_dve(dve, steps)
            with dve.Fori(0, N_TURNS) as i:
                steps.start_loop(i, 16 + 2 + 4 + 3 + 8 + 1 + 4 + 12 + 2)
                gdn_turn_dve(dve, steps, i)
                steps.end_loop(N_TURNS)

        def gdn_pool(pool):
            gdn_gates_pool(pool)
            with pool.Fori(0, N_TURNS) as i:
                gdn_turn_pool(pool, i)

        cm = Carver(arena, AR)
        PAD_A = TAPS_A - 1
        a_pad, a_acc, a_x, a_sq, a_rt = cm.cut(4, PAD_A + T), cm.cut(4, T), cm.cut(4, T), cm.cut(4, T), cm.cut(4, T)
        b_pad, b_acc, gate_t, cg_t = cm.cut(4, 2 + T), cm.cut(4, T), cm.cut(4, T), cm.cut(4, T)
        a_sig, b_cg, a_prod, b_prod = sem("a_sigmoid"), sem("b_c_gate"), sem("a_product"), sem("b_product")
        b_done, a_conv, a_biased, a_mean = sem("b_done"), sem("a_convolved"), sem("a_biased"), sem("a_mean")
        a_centred, a_sqd, a_var, a_root, a_norm = (sem(n) for n in ("a_centred", "a_squared", "a_var", "a_root", "a_normed"))

        def conv_pe(pe):
            first = FIRST_UNIT["conv_in"]
            for c in range(C):
                pe.wait_ge(u_ready, u_count(5, c))
            for n in range(20):
                b = n % 8
                if n >= 16:
                    pe.wait_ge(b_done, (n - 16) // 3 + 1)
                elif n >= 8:
                    pe.wait_ge(a_prod, (n - 8) // 2 + 1)
                s = take_unit(pe, first, n)
                for k in range(C):
                    last = nc.tensor.matmul(ps[:, b, 0:T], ring[:, s, k], u[:, k], start=(k == 0), stop=(k == C - 1))
                last.then_inc(unit_done[s], 1)
            flat = lambda x, n: x[:, 2 * n:2 * n + 2].rearrange("p a b -> p (a b)")
            pe.wait_ge(a_biased, 1)
            pe.wait_ge(b_done, 4)
            for n in range(2):
                last = nc.tensor.matmul(ps[:, n], const("block_ones"), flat(a_x, n), start=True, stop=True)
            last.then_inc(a_mean, 1)
            pe.wait_ge(a_sqd, 1)
            for n in range(2):
                last = nc.tensor.matmul(ps[:, 2 + n], const("block_ones"), flat(a_sq, n), start=True, stop=True)
            last.then_inc(a_var, 1)

        def conv_act(act):
            first = FIRST_UNIT["conv_in"]
            for j in range(4):
                unit_products(act, first, 2 * j + 1)
                nc.scalar.activation(gate_t[:, j], ps[:, 2 * j + 1, 0:T], ACT.Sigmoid).then_inc(a_sig, 1)
            for j in range(4):
                unit_products(act, first, 8 + 3 * j)
                nc.scalar.activation(cg_t[:, j], ps[:, (8 + 3 * j) % 8, 0:T], ACT.Copy).then_inc(b_cg, 1)
            act.wait_ge(a_conv, 1)
            for j in range(4):
                last = nc.scalar.activation(a_x[:, j], a_acc[:, j], ACT.Identity, bias=col("conv_a_b", j))
            last.then_inc(a_biased, 1)
            act.wait_ge(a_centred, 1)
            nc.scalar.activation(a_sq, a_x, ACT.Square).then_inc(a_sqd, 1)
            act.wait_ge(a_var, 1)
            nc.scalar.activation(a_rt.rearrange("p a b -> p (a b)"), ps[:, 2:4].rearrange("p a b -> p (a b)"), ACT.Sqrt, bias=col("eps"),
                                 scale=1.0 / 64).then_inc(a_root, 1)
            act.wait_ge(a_norm, 1)
            for j in range(4):
                nc.scalar.activation(mix[:, j], a_x[:, j], ACT.Silu, bias=col("ln_b", j)).then_inc(mix_ready, 1)

        def conv_dve(dve, steps):
            m, w = steps.mark, steps.wait
            first = FIRST_UNIT["conv_in"]
            m(nc.vector.memset(a_pad, 0.0))
            m(nc.vector.memset(b_pad, 0.0))
            w()
            for j in range(4):
                dve.wait_ge(a_sig, j + 1)
                nc.vector.tensor_tensor(a_pad[:, j, PAD_A:PAD_A + T], ps[:, 2 * j, 0:T], gate_t[:, j], ALU.mult).then_inc(a_prod, 1)
            dve.wait_ge(a_prod, 4)
            wa = COL["conv_a_w"]
            for j in range(4):
                m(nc.vector.tensor_scalar(a_acc[:, j], a_pad[:, j, 0:T], col("conv_a_w", j), None, ALU.mult))

            def a_taps(turns):
                with dve.Fori(0, turns) as i:
                    steps.start_loop(i, 12)
                    for q in range(3):
                        for j in range(4):
                            steps.wait(3)
                            m(nc.vector.scalar_tensor_tensor(a_acc[:, j], a_pad[:, j, bass.ds(1 + q + 3 * i, T)],
                                                             cols[:, bass.ds(wa + 4 * (1 + q) + j + 12 * i, 1)], a_acc[:, j], ALU.mult, ALU.add))
                    steps.end_loop(turns)

            a_taps((TAPS_A - 1) // 3)
            w()
            nc.vector.tensor_copy(a_rt[:, 0, 0:1], a_acc[:, 3, T - 1:T]).then_inc(a_conv, 1)
            for j in range(4):
                n = 8 + 3 * j
                dve.wait_ge(b_cg, j + 1)
                unit_products(dve, first, n + 1)
                unit_products(dve, first, n + 2)
                m(nc.vector.tensor_tensor(b_pad[:, j, 2:2 + T], ps[:, (n + 1) % 8, 0:T], cg_t[:, j], ALU.mult))
                w()
                m(nc.vector.tensor_scalar(b_acc[:, j], b_pad[:, j, 0:T], col("conv_b_w", 3 * j), None, ALU.mult))
                for q in (1, 2):
                    w()
                    m(nc.vector.scalar_tensor_tensor(b_acc[:, j], b_pad[:, j, q:q + T], col("conv_b_w", 3 * j + q), b_acc[:, j], ALU.mult, ALU.add))
                w()
                m(nc.vector.tensor_tensor(mix[:, 4 + j], b_acc[:, j], ps[:, (n + 2) % 8, 0:T], ALU.mult))
                w()
                nc.vector.tensor_copy(b_acc[:, j, 0:1], b_acc[:, j, 1:2]).then_inc(b_done, 1)
            dve.wait_ge(a_mean, 1)
            flat2 = lambda x: x.rearrange("p a b -> p (a b)")
            nc.vector.scalar_tensor_tensor(flat2(a_x), flat2(ps[:, 0:2]), -1.0 / 64, flat2(a_x), ALU.mult, ALU.add).then_inc(a_centred, 1)
            dve.wait_ge(a_root, 1)
            m(nc.vector.reciprocal(a_rt, a_rt))
            w()
            for j in range(4):
                ins = nc.vector.scalar_tensor_tensor(a_x[:, j], a_x[:, j], col("ln_g", j), a_rt[:, j], ALU.mult, ALU.mult)
            ins.then_inc(a_norm, 1)

        PADP = 16
        px, pb1, pb2 = at_.cut(4, PADP + T), at_.cut(4, PADP + T), at_.cut(4, PADP + T)
        pooled = at_.cut(4, T)
        pool_w = at_.cut(4, P)
        moba_loaded, p_copied, p_pooled, p_mixed = sem("moba_loaded"), sem("p_copied"), sem("p_pooled"), sem("p_mixed")

        def moba_pe(pe):
            first = FIRST_UNIT["pm_in"]
            for c in range(C):
                pe.wait_ge(u_ready, u_count(8, c))
            for n in range(12):
                if n >= 8:
                    pe.wait_ge(p_copied, n - 7)
                s = take_unit(pe, first, n)
                for k in range(C):
                    last = nc.tensor.matmul(ps[:, n % 8, 0:T], ring[:, s, k], u[:, k], start=(k == 0), stop=(k == C - 1))
                last.then_inc(unit_done[s], 1)
            pe.wait_ge(qk1_ready, 4)
            for n in range(4):
                s = take_unit(pe, first, 12 + n)
                for tb in range(2):
                    for k in range(C):
                        last = nc.tensor.matmul(ps[:, 4 + tb, n * P:(n + 1) * P], u[:, k, tb * P:(tb + 1) * P], ring[:, s, k],
                                                start=(n == 0 and k == 0), stop=(k == C - 1), skip_group_check=True)
                last.then_inc(unit_done[s], 1)
            pe.wait_ge(p_pooled, 1)
            pe.wait_ge(moba_loaded, 32)
            for g in range(4):
                last = nc.tensor.matmul(ps[:, 6 + g // 2, (g % 2) * T:(g % 2 + 1) * T], pool_w[:, g], pooled[:, g], start=True, stop=True)
            last.then_inc(p_mixed, 1)
            pe.wait_ge(mix_ready, 16)

        def moba_act(act):
            first = FIRST_UNIT["pm_in"]
            for n in range(12):
                unit_products(act, first, n)
                if n < 4:
                    nc.scalar.activation(px[:, n, PADP:PADP + T], ps[:, n, 0:T], ACT.Copy).then_inc(p_copied, 1)
                else:
                    nc.scalar.activation(qk[:, n - 4], ps[:, n % 8, 0:T], ACT.Copy).then_inc(qk1_ready, 1)
            for n in range(4):
                unit_products(act, first, 12 + n)
            nc.scalar.activation(vtok, ps[:, 4:6], ACT.Copy).then_inc(v_copied, 1)

        def moba_dve(dve, steps):
            m, w = steps.mark, steps.wait
            for b in (px, pb1, pb2):
                m(nc.vector.memset(b[:, :, 0:PADP], 0.0))
            w()
            dve.wait_ge(p_copied, 4)
            src = px
            for lv in range(4):
                dst, d = (pb1, pb2)[lv % 2], 1 << lv
                m(nc.vector.tensor_tensor(dst[:, lv:, PADP:], src[:, lv:, PADP:], src[:, lv:, PADP - d:PADP + T - d], ALU.add))
                w()
                src = dst
            inv = const("pool_inv").rearrange("p (g t) -> p g t", g=4)
            for g in range(4):
                m(nc.vector.tensor_tensor(pooled[:, g], (pb1, pb2)[g % 2][:, g, PADP:], inv[:, g], ALU.mult))
            w()
            nc.vector.tensor_tensor(pooled, pooled, px[:, :, PADP:], ALU.subtract).then_inc(p_pooled, 1)
            dve.wait_ge(p_mixed, 1)
            for g in range(4):
                nc.vector.tensor_scalar(mix[:, g], ps[:, 6 + g // 2, (g % 2) * T:(g % 2 + 1) * T], col("pool_b", g), col("pool_scale", g),
                                        ALU.add, ALU.mult).then_inc(mix_ready, 1)
            dve.wait_ge(moba_loaded, 32)

        def moba_pool(pool):
            pool.wait_ge(h_ready, 8 * 8)
            pool.dma_start(alibi, dram["alibi"]).then_inc(moba_loaded, 16)
            pool.dma_start(pool_w, dram["pool_w"]).then_inc(moba_loaded, 16)


        def pe_program(pe):
            pe.wait_ge(small_loaded, 16 * N_SMALL)
            norm_pe(pe, 0)
            attn_in_pe(pe)
            core_pe(pe, 0)
            lin_pe(pe, 0, "attn_out", C)
            norm_pe(pe, 1)
            ffn_pe(pe, 0)
            norm_pe(pe, 2)
            gdn_pe(pe)
            lin_pe(pe, 2, "gdn_out", 2 * C)
            norm_pe(pe, 3)
            ffn_pe(pe, 1)
            norm_pe(pe, 4)
            ffn_pe(pe, 2)
            norm_pe(pe, 5)
            conv_pe(pe)
            lin_pe(pe, 5, "conv_out", C)
            norm_pe(pe, 6)
            ffn_pe(pe, 3)
            norm_pe(pe, 7)
            ffn_pe(pe, 4)
            norm_pe(pe, 8)
            moba_pe(pe)
            core_pe(pe, 1)
            lin_pe(pe, 8, "pm_out", C)
            norm_pe(pe, 9)
            ffn_pe(pe, 5)
            norm_pe(pe, 10)

        def act_program(act):
            steps = Steps(act, act_steps)
            act.wait_ge(small_loaded, 16 * N_SMALL)
            nc.scalar.activation(cond[:], cols[:, COL["cond"]:COL["cond"] + 8], ACT.Silu).then_inc(cond_ready, 1)
            norm_act(act, 0)
            angles_act(act)
            attn_in_act(act)
            core_act(act, 0)
            norm_act(act, 1)
            ffn_act(act, 0)
            norm_act(act, 2)
            gdn_act(act, steps)
            norm_act(act, 3)
            ffn_act(act, 1)
            norm_act(act, 4)
            ffn_act(act, 2)
            norm_act(act, 5)
            conv_act(act)
            norm_act(act, 6)
            ffn_act(act, 3)
            norm_act(act, 7)
            ffn_act(act, 4)
            norm_act(act, 8)
            moba_act(act)
            core_act(act, 1)
            norm_act(act, 9)
            ffn_act(act, 5)
            norm_act(act, 10)

        def dve_program(dve):
            steps = Steps(dve, dve_steps)
            nc.vector.memset(cvb[:, 0, 0:1], 0.0).then_inc(act_ready, CREDIT)
            angles_dve(dve, steps)
            norm_dve(dve, steps, 0)
            attn_in_dve(dve, steps)
            core_dve(dve, steps, 0)
            residual_dve(dve, steps, 0, False, "lin")
            norm_dve(dve, steps, 1)
            dve.wait_ge(cond_ready, 1)
            ffn_dve(dve, steps, 0)
            norm_dve(dve, steps, 2)
            gdn_dve(dve, steps)
            residual_dve(dve, steps, 2, False, "lin")
            norm_dve(dve, steps, 3)
            ffn_dve(dve, steps, 1)
            norm_dve(dve, steps, 4)
            ffn_dve(dve, steps, 2)
            norm_dve(dve, steps, 5)
            conv_dve(dve, steps)
            residual_dve(dve, steps, 5, True, "lin")
            norm_dve(dve, steps, 6)
            ffn_dve(dve, steps, 3)
            norm_dve(dve, steps, 7)
            ffn_dve(dve, steps, 4)
            norm_dve(dve, steps, 8)
            moba_dve(dve, steps)
            core_dve(dve, steps, 1)
            residual_dve(dve, steps, 8, True, "lin")
            norm_dve(dve, steps, 9)
            ffn_dve(dve, steps, 5)
            norm_dve(dve, steps, 10)

        def pool_program(pool):
            ffn_pool(pool, 0)
            gdn_pool(pool)
            for q in (1, 2, 3):
                ffn_pool(pool, q)
            moba_pool(pool)

        SMALL = [(cols[:], dram["cols"]), (consts[:], dram["consts"]), (positions[:], dram["positions"])]
        N_SMALL = len(SMALL)
        block = ctx.enter_context(nc.Block())

        @block.sync
        def _(sp):
            for dst, src in SMALL:
                sp.dma_start(dst, src).then_inc(small_loaded, 16)
            sp.dma_start(h[:], dram["x"]).then_inc(h_loaded, 16)
            for s in range(RING):
                sp.dma_start(ring[:, s], dram["w"][s]).then_inc(raw_ready[s], 16)
            with sp.Fori(1, N_UNITS // RING) as i:
                for s in range(RING):
                    sp.wait_ge(unit_done[s], i)
                    sp.dma_start(ring[:, s], dram["w"][RING * i + s]).then_inc(raw_ready[s], 16)
            for s in range(N_UNITS % RING):
                sp.wait_ge(unit_done[s], N_UNITS // RING)
                sp.dma_start(ring[:, s], dram["w"][N_UNITS - N_UNITS % RING + s]).then_inc(raw_ready[s], 16)
            sp.wait_ge(out_ready, 8)
            sp.dma_start(out_dram, u[:]).then_inc(out_done, 16)
            sp.wait_ge(out_done, 16)

        @block.gpsimd
        def _(pool):
            pool_program(pool)

        @block.tensor
        def _(pe):
            pe_program(pe)

        @block.scalar
        def _(act):
            act_program(act)

        @block.vector
        def _(dve):
            dve_program(dve)


def columns(a):
    a = np.ascontiguousarray(a).reshape(-1, P)
    return a.T


def by_output(w):
    k, n = w.shape
    return w.reshape(k // D, C, P, n // P, P).transpose(3, 0, 2, 1, 4).reshape(-1, P, D)


def by_row(w):
    return w.reshape(-1, P, D)


def ffn_units(gate, up, down):
    g, u, d = by_output(gate), by_output(up), by_row(down)
    nf = d.shape[0]
    order = [g[0], u[0]]
    for f in range(1, nf):
        order += [g[f], u[f], d[f - 1]]
    return order + [d[nf - 1]]


def weight_stream(x):
    heads = np.array([attn_tile_heads(j) for j in range(C)]).reshape(-1)
    q_cols = (heads[:, None] * HD + np.arange(HD)).reshape(-1)
    w = x["attn_w_in"][0]
    units = list(by_output(w[:, D:D + 256])) + list(by_output(w[:, :D][:, q_cols])) + list(by_output(w[:, D + 256:]))
    units += list(by_output(x["attn_w_out"][0][q_cols]))
    up = x["ffn_w_up"][0]
    units += ffn_units(up[:, :3072], up[:, 3072:], x["ffn_w_down"][0])
    w = x["gdn_w_in"][0]
    gates = np.zeros((D, P), w.dtype)
    gates[:, 0:16] = w[:, 6144:6160]
    gates[:, 32:48] = w[:, 6160:6176]
    units += list(by_output(gates))
    tiles = by_output(w[:, :6144])
    for i in range(GH // GB):
        units += [tiles[t] for t in gdn_turn_tiles(i)] + [tiles[32 + 4 * i + j] for j in range(4)]
    units += list(by_output(x["gdn_w_out"][0]))
    up = x["ffn_w_up"][1]
    units += ffn_units(up[:, :3072], up[:, 3072:], x["ffn_w_down"][1])
    f2 = lambda l, s: ffn_units(x["ffn_w_gate_2"][l, s], x["ffn_w_up_2"][l, s], x["ffn_w_down_2"][l, s])
    units += f2(0, 0)
    t = by_output(x["conv_w_in_2"][0])
    units += [t[n] for j in range(4) for n in (j, 4 + j)] + [t[n] for j in range(4) for n in (12 + j, 16 + j, 8 + j)]
    units += list(by_output(x["conv_w_out_2"][0]))
    units += f2(0, 1) + f2(1, 0)
    units += list(by_output(x["pm_w_in_2"][0])) + list(by_output(x["pm_w_out_2"][0]))
    units += f2(1, 1)
    assert len(units) == N_UNITS
    return np.stack(units).reshape(N_UNITS, P, C, P)


def gdn_turn_tiles(i):
    return [2 * i, 2 * i + 1, 8 + 2 * i, 9 + 2 * i] + [16 + 4 * i + j for j in range(4)]


def packed_columns(x):
    out = np.zeros((P, N_COLS), np.float32)

    def put(name, a):
        out[:, COL[name]:COL[name] + a.shape[1]] = a

    put("mixer_norm", columns(x["mixer_norm"]))
    put("ffn_norm", columns(x["ffn_norm"]))
    put("q_gain", np.tile(x["attn_q_gain"][0], 2)[:, None])
    put("k_gain", np.tile(x["attn_k_gain"][0], 2)[:, None])
    taps = x["gdn_conv"][0].reshape(4, 32, P)
    order = [t for i in range(GH // GB) for t in gdn_turn_tiles(i)]
    put("gdn_conv", taps[:, order].transpose(2, 1, 0).reshape(P, 128))
    out[32:48, COL["a_log"]] = x["gdn_a_log"][0]
    out[32:48, COL["dt_bias"]] = x["gdn_dt_bias"][0]
    put("gdn_norm", x["gdn_norm"][0][:, None])
    fc = np.concatenate([x["ffn_conv"], x["ffn_conv_b"][:, None]], axis=1).reshape(2, 4, FF1, P)
    put("ffn_conv", fc.transpose(3, 0, 2, 1).reshape(P, -1))
    put("cond", columns(x["c_2"]))
    put("ada_b", columns(x["ada_b_2"]))
    put("ffn_norm_2", columns(x["ffn_norm_2"]))
    put("mix_norm", columns(x["mix_norm_2"]))
    put("conv_a_w", x["conv_a_w_2"][0].reshape(TAPS_A, 4, P).transpose(2, 0, 1).reshape(P, -1))
    put("conv_a_b", columns(x["conv_a_b_2"]))
    put("ln_g", columns(x["conv_a_ln_g_2"]))
    put("ln_b", columns(x["conv_a_ln_b_2"]))
    put("conv_b_w", x["conv_b_w_2"][0].reshape(3, 4, P).transpose(2, 1, 0).reshape(P, -1))
    put("pool_b", x["pool_b_2"][0].T)
    put("pool_scale", columns(x["pool_scale_2"]))
    put("final_norm", columns(x["final_norm_2"]))
    half = ROPE // 2
    freq = (np.float32(500000.0) ** (-np.arange(0, ROPE, 2, dtype=np.float32) / np.float32(ROPE))).astype(np.float32)
    for b in range(2):
        out[64 * b:64 * b + half, COL["inv_freq"]] = freq
        out[64 * b + half:64 * b + ROPE, COL["inv_freq"]] = freq
    sinks = x["attn_sinks"][0]
    put("sinks", np.broadcast_to(sinks[[hd for j in range(C) for hd in attn_tile_heads(j)]], (P, 16)))
    out[:, COL["eps"]] = EPS
    out[:, COL["half_pi"]] = np.pi / 2
    out[:, COL["one"]] = 1.0
    return out


def constant_matrices():
    out = np.zeros((P, N_CONST), np.float32)

    def put(name, a):
        out[:, CONST[name][0]:CONST[name][0] + a.shape[1]] = a

    i, j = np.arange(P)[:, None], np.arange(P)[None, :]
    put("ident", (i == j) * 1.0)
    put("ones", np.ones((P, P)))
    put("block_ones", (i // 64 == j // 64) * 1.0)
    rot = np.zeros((P, P))
    half = ROPE // 2
    for b in (0, 64):
        for m in range(half):
            rot[b + m + half, b + m] = -1.0
            rot[b + m, b + m + half] = 1.0
    put("rotate", rot)
    q = np.arange(P)[:, None]
    k = np.arange(T)[None, :]
    dist1 = P + q - k
    mask = np.concatenate([np.where(k[:, :P] <= q, 0.0, NEG), np.where((dist1 >= 0) & (dist1 < 128), 0.0, NEG)], axis=1)
    put("window_mask", mask)
    p, s = np.arange(P)[:, None] % 64, np.arange(64)[None, :]
    put("stack_ident", (p == s) * 1.0)
    put("level_lo", ((p // 2 == s // 2) & (p > s)) * 1.0)
    for lv in range(6):
        z = 2 ** lv
        a = CONST["level_up"][0] + 64 * lv
        out[:, a:a + 64] = (p // (2 * z) == s // (2 * z)) & (p // z % 2 == 0) & (s // z % 2 == 1)
    put("strict_lo_neg", np.where(s < p, 0.0, NEG))
    put("incl_up_neg", np.where(s >= p, 0.0, NEG))
    put("strict_up", (s > p) * 1.0)
    put("reset", np.broadcast_to((np.arange(T) % CH != 0) * 1.0, (P, T)))
    inv = np.stack([1.0 / np.minimum(np.arange(1, T + 1), w) for w in (2, 4, 8, 16)]).reshape(1, -1)
    put("pool_inv", np.broadcast_to(inv, (P, 4 * T)))
    return out


def alibi_matrices():
    q, k = np.arange(P)[:, None], np.arange(T)[None, :]
    slopes = 2.0 ** -(np.arange(8) + 1.0)
    out = np.zeros((P, 8, 384), np.float32)
    for n, slope in enumerate(slopes):
        d0, d1 = q - k[:, :P], P + q - k
        out[:, n, :P] = np.where(d0 >= 0, -slope * d0, NEG)
        out[:, n, P:] = np.where(d1 >= 0, -slope * d1, NEG)
    return out


def kernel(**inputs):
    import concourse.bacc as bacc
    from concourse.bass_utils import run_bass_kernel_spmd

    x = {k: np.asarray(v) for k, v in inputs.items()}
    ada = x["ada_w_2"].reshape(2, C, P, 18, PIECE).transpose(0, 3, 2, 1, 4).reshape(PIECES, P, C, PIECE)
    arrays = {
        "x": np.ascontiguousarray(x["x"][0].T.reshape(C, P, T).transpose(1, 0, 2)),
        "w": weight_stream(x),
        "ada": np.ascontiguousarray(ada),
        "cols": packed_columns(x),
        "consts": constant_matrices(),
        "alibi": alibi_matrices(),
        "pool_w": np.ascontiguousarray(x["pool_w_2"][0].transpose(1, 0, 2)),
        "positions": np.ascontiguousarray(np.broadcast_to(x["positions"], (P, T))),
    }
    nc = bacc.Bacc("TRN2", target_bir_lowering=False, num_devices=1)
    dram = {name: nc.dram_tensor(f"in_{name}", a.shape, mybir.dt.from_np(a.dtype), kind="ExternalInput").ap()
            for name, a in arrays.items()}
    out = nc.dram_tensor("out", (P, C, T), F32, kind="ExternalOutput").ap()
    build(nc, dram, out)
    r = run_bass_kernel_spmd(nc, [{f"in_{name}": a for name, a in arrays.items()}], core_ids=[0])
    got = r.results[0]["out"]
    return got.transpose(1, 0, 2).reshape(D, T).T.reshape(1, T, D)
```

```python
from contextlib import ExitStack

import concourse.bass as bass
import numpy as np
from concourse import mybir

F32 = mybir.dt.float32
FR = mybir.dt.float32r
I32 = mybir.dt.int32
ALU = mybir.AluOpType
ACT = mybir.ActivationFunctionType
AX_X = mybir.AxisListType.X

P = 128
D = 1024
T = 256
C = D // P
HD = 64
RING = 4
SPLIT = 3
EPS = 1e-6
NEG = -3.0e38
FF1, FF2 = 3072 // P, 2816 // P
GH, GB = 16, 4
CH = 64
TAPS_A = 31
ROPE = HD // 4
MAGIC = 12582912.0
PIECE = 512
PIECES = 2 * 9 * D // PIECE

UNITS = [("attn_in", 12), ("attn_out", 8), ("ffn0", 3 * FF1), ("gdn_gates", 1), ("gdn_in", 48), ("gdn_out", 16),
         ("ffn1", 3 * FF1), ("ffn2", 3 * FF2), ("conv_in", 20), ("conv_out", 8), ("ffn3", 3 * FF2),
         ("ffn4", 3 * FF2), ("pm_in", 16), ("pm_out", 8), ("ffn5", 3 * FF2)]
FIRST_UNIT = {}
N_UNITS = 0
for _name, _n in UNITS:
    FIRST_UNIT[_name] = N_UNITS
    N_UNITS += _n

COLS = [("mixer_norm", 16), ("ffn_norm", 16), ("q_gain", 1), ("k_gain", 1), ("gdn_conv", 128), ("a_log", 1),
        ("dt_bias", 1), ("gdn_norm", 1), ("ffn_conv", 8 * FF1), ("cond", 8), ("ada_b", 144), ("ffn_norm_2", 32),
        ("mix_norm", 16), ("conv_a_w", 4 * TAPS_A), ("conv_a_b", 4), ("ln_g", 4), ("ln_b", 4), ("conv_b_w", 12),
        ("pool_b", 4), ("pool_scale", 4), ("final_norm", 8), ("inv_freq", 1), ("sinks", 16), ("eps", 1),
        ("half_pi", 1), ("one", 1), ("zero", 1)]
COL = {}
N_COLS = 0
for _name, _n in COLS:
    COL[_name] = N_COLS
    N_COLS += _n

CONSTS = [("ident", 128), ("ones", 128), ("block_ones", 128), ("rotate", 128), ("window_mask", 384),
          ("stack_ident", 64), ("level_lo", 64), ("level_up", 6 * 64), ("strict_lo_neg", 64), ("incl_up_neg", 64),
          ("strict_up", 64), ("reset", T), ("pool_inv", 4 * T)]
CONST = {}
N_CONST = 0
for _name, _n in CONSTS:
    CONST[_name] = (N_CONST, _n)
    N_CONST += _n


def attn_tile_heads(j):
    return (j, 4 + j) if j < 4 else (4 + j, 8 + j)



class Steps:

    def __init__(self, eng, sem):
        self.eng, self.sem, self.n, self.turns = eng, sem, 0, 0

    def mark(self, ins):
        ins.then_inc(self.sem, 1)
        self.n += 1
        return ins

    def wait(self, back=0):
        self.eng.wait_ge(self.sem, self.n - back + self.turns)

    def start_loop(self, turn, per):
        self.n0, self.per, self.turns = self.n, per, per * turn

    def end_loop(self, count):
        assert self.n - self.n0 == self.per, (self.n - self.n0, self.per)
        self.n, self.turns = self.n0 + self.per * count, 0


class Carver:

    def __init__(self, tile, size):
        self.tile, self.size, self.at = tile, size, 0

    def cut(self, *dims):
        n = int(np.prod(dims))
        assert self.at + n <= self.size, (self.at + n, self.size)
        ap = self.tile[:, self.at:self.at + n]
        self.at += n
        names = "abcd"[:len(dims)]
        if len(dims) > 1:
            ap = ap.rearrange(f"p ({' '.join(names)}) -> p {' '.join(names)}", **dict(zip(names, dims)))
        return ap


def build(nc, dram, out_dram):
    with ExitStack() as ctx:
        def sb(name, shape, dt=F32):
            return ctx.enter_context(nc.sbuf_tensor(name, shape, dt))

        def sem(name):
            return ctx.enter_context(nc.semaphore(name))

        ring = sb("weight_ring", [P, RING, C, P])
        h = sb("h", [P, C, T])
        u = sb("u", [P, C, T])
        mix = sb("mix", [P, 2 * C, T])
        cols = sb("cols", [P, N_COLS])
        consts = sb("consts", [P, N_CONST])
        squares = sb("squares", [P, C, T])
        scaled = sb("scaled", [P, C, T])
        root = sb("root", [P, T])
        rstd = sb("rstd", [P, T])
        mods = sb("mods", [P, 144])
        cond = sb("cond", [P, 8])
        gain = sb("gain", [P, 8])
        half_gate = sb("half_gate", [P, 8])
        positions = sb("positions", [P, T], I32)
        AR = 20 * 1024 + 256
        arena = sb("arena", [P, AR])
        with nc.sbuf_tensor("gdn_tiles", [P, 10 * 1024], F32) as gdn_tiles:
            pass
        w_hi, w_lo = sb("weights_hi", [P, SPLIT, C, P], FR), sb("weights_lo", [P, SPLIT, C, P], FR)
        u_hi, u_lo = sb("u_hi", [P, C, T], FR), sb("u_lo", [P, C, T], FR)
        act_hi, act_lo = sb("act_hi", [P, 2, T], FR), sb("act_lo", [P, 2, T], FR)
        ps = ctx.enter_context(nc.psum_tensor("ps", [P, 8, 512], F32))
        gates_dram = nc.dram_tensor("gates_scratch", (2, GH, T), F32, kind="Internal").ap()

        def col(name, k=0):
            at = COL[name] + k
            return cols[:, bass.ds(at, 1)]

        def const(name, k=None, n=None):
            at, size = CONST[name]
            if k is not None:
                at, size = at + k * n, n
            return consts[:, at:at + size]

        ident, ones = const("ident"), const("ones")

        raw_ready = [sem(f"raw_ready{s}") for s in range(RING)]
        unit_done = [sem(f"unit_done{s}") for s in range(RING)]
        small_loaded = sem("small_loaded")
        cond_ready = sem("cond_ready")
        h_loaded, h_ready = sem("h_loaded"), sem("h_ready")
        sq_ready, ss_ready, root_ready = sem("sq_ready"), sem("ss_ready"), sem("root_ready")
        scaled_ready, u_ready = sem("scaled_ready"), sem("u_ready")
        dve_steps, act_steps, pool_steps = sem("dve_steps"), sem("act_steps"), sem("pool_steps")
        out_done, out_ready = sem("out_done"), sem("out_ready")
        mix_ready = sem("mix_ready")
        cv0_ready, cv_ready = sem("conv_tap_ready"), sem("conv_ready")
        sg_ready, act_ready = sem("silu_ready"), sem("act_ready")
        hi_ready, split_done = sem("hi_ready"), [sem(f"split_done{s}") for s in range(RING)]
        u_hi_ready, u_lo_ready = sem("u_hi_ready"), sem("u_lo_ready")
        act_hi_ready, act_lo_ready = sem("act_hi_ready"), sem("act_lo_ready")
        ada_loaded = [sem("ada_loaded0"), sem("ada_loaded1")]
        ada_summed, ada_cols = sem("ada_summed"), sem("ada_cols")
        pjsq_ready, pjss_ready, pjroot_ready = sem("pjsq_ready"), sem("pjss_ready"), sem("pjroot_ready")
        qn_ready, rot_ready, rope_ready = sem("qn_ready"), sem("rot_ready"), sem("rope_ready")
        angle_ready, sine_ready = sem("angle_ready"), sem("sine_ready")
        v_copied = sem("v_copied")
        sc_ready, max_ready, exp_ready, p_ready = sem("scores_ready"), sem("max_ready"), sem("exp_ready"), sem("probs_ready")
        pt_ready, ptc_ready, pv_ready = sem("pt_ready"), sem("pt_copied"), sem("pv_ready")

        MODS = {}
        for n, (l, s) in enumerate([(0, 0), (0, 1), (0, 2), (1, 0), (1, 1), (1, 2)]):
            MODS[4 + n] = (l, s)

        def mod_col(l, s, which):
            return 72 * l + (3 * s + which) * 8

        NORM_AT = {0: ("mixer_norm", 0), 2: ("mixer_norm", 8), 1: ("ffn_norm", 0), 3: ("ffn_norm", 8),
                   4: ("ffn_norm_2", 0), 5: ("mix_norm", 0), 6: ("ffn_norm_2", 8),
                   7: ("ffn_norm_2", 16), 8: ("mix_norm", 8), 9: ("ffn_norm_2", 24), 10: ("final_norm", 0)}

        def take_unit(pe, first, j, turn_units=0, turn=None):
            n = first + j
            need = 16 * (n // RING + 1)
            if turn is not None:
                assert turn_units % RING == 0
                need = need + 16 * (turn_units // RING) * turn
            pe.wait_ge(raw_ready[n % RING], need)
            return n % RING

        def unit_products(eng, first, j, turn_units=0, turn=None):
            n = first + j
            need = n // RING + 1
            if turn is not None:
                need = need + turn_units // RING * turn
            eng.wait_ge(unit_done[n % RING], need)

        def norm_bank(k):
            return 0 if k in (1, 3, 6, 9) else 7

        def norm_act(act, k):
            for c in range(C):
                if k == 0:
                    act.wait_ge(h_loaded, 16)
                else:
                    act.wait_ge(h_ready, 8 * (k - 1) + c + 1)
                nc.scalar.activation(squares[:, c], h[:, c], ACT.Square).then_inc(sq_ready, 1)
            act.wait_ge(ss_ready, k + 1)
            nc.scalar.activation(root[:], ps[:, norm_bank(k), 0:T], ACT.Sqrt, bias=col("eps"), scale=1.0 / D).then_inc(root_ready, 1)
            if k in MODS:
                l, s = MODS[k]
                for c in range(C):
                    act.wait_ge(scaled_ready, 8 * (k - 4) + c + 1)
                    sh = mod_col(l, s, 0) + c
                    nc.scalar.activation(u[:, c], scaled[:, c], ACT.Identity, bias=mods[:, sh:sh + 1]).then_inc(u_ready, 1)

        def norm_pe(pe, k):
            for c in range(C):
                pe.wait_ge(sq_ready, 8 * k + c + 1)
                last = nc.tensor.matmul(ps[:, norm_bank(k), 0:T], ones, squares[:, c], start=(c == 0), stop=(c == C - 1))
            last.then_inc(ss_ready, 1)

        def norm_dve(dve, steps, k):
            if k in MODS:
                l, s = MODS[k]
                name, at = NORM_AT[k]
                dve.wait_ge(h_ready, 8 * k)
                sc, ga = mod_col(l, s, 1), mod_col(l, s, 2)
                a = COL[name] + at
                steps.mark(nc.vector.scalar_tensor_tensor(gain[:], mods[:, sc:sc + 8], 1.0, cols[:, a:a + 8], ALU.add, ALU.mult))
                steps.mark(nc.vector.tensor_scalar(half_gate[:], mods[:, ga:ga + 8], 1.0 if s == 1 else 0.5, None, ALU.mult))
            dve.wait_ge(root_ready, k + 1)
            steps.mark(nc.vector.reciprocal(rstd[:], root[:]))
            steps.wait()
            for c in range(C):
                if k in MODS:
                    nc.vector.scalar_tensor_tensor(scaled[:, c], h[:, c], gain[:, c:c + 1], rstd[:], ALU.mult, ALU.mult).then_inc(scaled_ready, 1)
                else:
                    name, at = NORM_AT[k]
                    nc.vector.scalar_tensor_tensor(u[:, c], h[:, c], col(name, at + c), rstd[:], ALU.mult, ALU.mult).then_inc(
                        out_ready if k == 10 else u_ready, 1)

        def u_count(k, c):
            return 8 * k + c + 1

        def residual_dve(dve, steps, k, gated, banks, next_ffn=None):
            for c in range(C):
                if next_ffn is not None and c == C - 2:
                    split_first_dve(dve, next_ffn, (0, 1))
                if banks == "lin":
                    name, per = LIN[k]
                    unit_products(dve, FIRST_UNIT[name], per * c + per - 1)
                    src = ps[:, c, 0:T]
                else:
                    src = ps[:, c // 2, (c % 2) * T:(c % 2 + 1) * T]
                g = half_gate[:, c:c + 1] if gated else 1.0
                nc.vector.scalar_tensor_tensor(h[:, c], src, g, h[:, c], ALU.mult, ALU.add).then_inc(h_ready, 1)
            if next_ffn is not None:
                split_first_dve(dve, next_ffn, (2,))

        LIN = {0: ("attn_out", 1), 2: ("gdn_out", 2), 5: ("conv_out", 1), 8: ("pm_out", 1)}
        MIX_COUNT = {0: 4, 2: 8, 5: 12, 8: 18}

        def lin_pe(pe, k, name, kc):
            pe.wait_ge(mix_ready, MIX_COUNT[k])
            per = kc // C
            for n in range(C):
                for b in range(per):
                    s = take_unit(pe, FIRST_UNIT[name], n * per + b)
                    for kk in range(C):
                        last = nc.tensor.matmul(ps[:, n, 0:T], ring[:, s, kk], mix[:, b * C + kk],
                                                start=(b == 0 and kk == 0), stop=(b == per - 1 and kk == C - 1))
                    last.then_inc(unit_done[s], 1)

        ffn = Carver(arena, AR)
        ada_ring = ffn.cut(2, C, PIECE)
        ada_acc = ffn.cut(10, PIECE)
        cvb = ffn.cut(4, T)
        sgb = ffn.cut(4, T)
        actb = ffn.cut(4, T)
        FFN = [(1, FF1, 1, [(5, 2)]), (3, FF1, 1, [(5, 2)]), (4, FF2, 2, [(4, 2)]), (6, FF2, 2, [(4, 2)]),
               (7, FF2, 2, [(4, 0)]), (9, FF2, 2, [(4, 0)])]
        F_BASE = [0, FF1, 2 * FF1, 2 * FF1 + FF2, 2 * FF1 + 2 * FF2, 2 * FF1 + 3 * FF2, 2 * FF1 + 4 * FF2]
        PIECE_BASE = [0, 10, 20, 28, 36, 36, 36]
        CREDIT = 4

        def gate_at(f):
            return 3 * f - 1 if f else 0

        def up_at(f):
            return 3 * f if f else 1

        def down_at(q, f):
            return 3 * f + 4 if f < FFN[q][1] - 1 else 3 * f + 2

        def ffn_unit_done(eng, q, j, turn=None):
            unit_products(eng, FIRST_UNIT[f"ffn{q}"], j, 12, turn)

        def split_count(q, j):
            s = (FIRST_UNIT[f"ffn{q}"] + j) % RING
            return sum((FIRST_UNIT[f"ffn{p_}"] + i) % RING == s for p_ in range(q + 1)
                       for i in range(3 * FFN[p_][1] if p_ < q else j + 1))

        def split_wait(eng, q, j, turn=None):
            need = split_count(q, j)
            if turn is not None:
                need = need + 12 // RING * turn
            eng.wait_ge(split_done[(FIRST_UNIT[f"ffn{q}"] + j) % RING], need)
            return j % SPLIT

        def split_hi(act, q, j, turn=None):
            n = FIRST_UNIT[f"ffn{q}"] + j
            take_unit(act, FIRST_UNIT[f"ffn{q}"], j, 12, turn)
            if j >= SPLIT:
                ffn_unit_done(act, q, j - SPLIT, turn)
            elif q:
                ffn_unit_done(act, q - 1, 3 * FFN[q - 1][1] - SPLIT + j)
            nc.scalar.activation(w_hi[:, j % SPLIT], ring[:, n % RING], ACT.Copy).then_inc(hi_ready, 1)

        def split_lo(eng, vec, q, j, turn=None):
            n = FIRST_UNIT[f"ffn{q}"] + j
            need = 3 * F_BASE[q] + j + 1
            if turn is not None:
                need = need + 12 * turn
            eng.wait_ge(hi_ready, need)
            vec.tensor_tensor(w_lo[:, j % SPLIT], ring[:, n % RING], w_hi[:, j % SPLIT].bitcast(F32), ALU.subtract).then_inc(
                split_done[n % RING], 1)

        def split_first_act(act, q):
            for j in range(SPLIT):
                split_hi(act, q, j)

        def split_first_dve(dve, q, js):
            for j in js:
                split_lo(dve, nc.vector, q, j)

        def split_u_act(act, q):
            k = FFN[q][0]
            for c in range(C):
                act.wait_ge(u_ready, u_count(k, c))
                nc.scalar.activation(u_hi[:, c], u[:, c], ACT.Copy).then_inc(u_hi_ready, 1)

        def split_u_dve(dve, q):
            for c in range(C):
                dve.wait_ge(u_hi_ready, 8 * q + c + 1)
                nc.vector.tensor_tensor(u_lo[:, c], u[:, c], u_hi[:, c].bitcast(F32), ALU.subtract).then_inc(u_lo_ready, 1)

        def split_product(out, hi, lo, x_hi, x_lo, start, stop):
            nc.tensor.matmul(out, hi, x_hi, start=start, stop=False, skip_group_check=True)
            nc.tensor.matmul(out, hi, x_lo, start=False, stop=False, skip_group_check=True)
            return nc.tensor.matmul(out, lo, x_hi, start=False, stop=stop, skip_group_check=True)

        def gate_up(pe, q, f, turn=None):
            need = F_BASE[q] + f - 3 + CREDIT
            if turn is not None:
                need = need + 4 * turn
            pe.wait_ge(act_ready, need)
            b = 4 + f % 4
            for half in range(2):
                j = up_at(f) if half else gate_at(f)
                s = split_wait(pe, q, j, turn)
                for k in range(C):
                    if f == 0 and half == 0:
                        pe.wait_ge(u_lo_ready, 8 * q + k + 1)
                    last = split_product(ps[:, b, half * T:(half + 1) * T], w_hi[:, s, k], w_lo[:, s, k], u_hi[:, k], u_lo[:, k],
                                         half == 0 and k == 0, k == C - 1)
                last.then_inc(unit_done[(FIRST_UNIT[f"ffn{q}"] + j) % RING], 1)

        def down(pe, q, f, start, turn=None):
            need = F_BASE[q] + f + 1
            if turn is not None:
                need = need + 4 * turn
            pe.wait_ge(act_lo_ready, need)
            j = down_at(q, f)
            s = split_wait(pe, q, j, turn)
            for c in range(C):
                last = split_product(ps[:, c // 2, (c % 2) * T:(c % 2 + 1) * T], w_hi[:, s, c], w_lo[:, s, c],
                                     act_hi[:, f % 2], act_lo[:, f % 2], start and c % 2 == 0, True)
            last.then_inc(unit_done[(FIRST_UNIT[f"ffn{q}"] + j) % RING], 1)

        def ffn_pe(pe, q):
            k, nf, kind, loops = FFN[q]
            gate_up(pe, q, 0)
            gate_up(pe, q, 1)
            down(pe, q, 0, True)
            f0 = 2
            for turns, _ in loops:
                with pe.Fori(0, turns) as i:
                    for j in range(4):
                        gate_up(pe, q, f0 + j, i)
                        down(pe, q, f0 + j - 1, False, i)
                f0 += 4 * turns
            for f in range(f0, nf):
                gate_up(pe, q, f)
                down(pe, q, f - 1, False)
            down(pe, q, nf - 1, False)
            n0, n1 = PIECE_BASE[q], PIECE_BASE[q + 1]
            if n1 > n0:
                pe.wait_ge(ada_summed, n1)
                for n in range(4 * (n1 - n0)):
                    last = nc.tensor.matmul(ps[:, 4, n:n + 1], ada_acc[:, n // 4, (n % 4) * P:(n % 4 + 1) * P],
                                            ones[:, 0:1], start=True, stop=True)
                last.then_inc(ada_cols, 1)

        def ffn_tile_act(act, q, f, turn=None):
            k, nf, kind, loops = FFN[q]
            n = F_BASE[q] + f + 1
            at = 0
            if turn is not None:
                n, at = n + 4 * turn, 16 * turn
            b, r = 4 + f % 4, f % 4
            ffn_unit_done(act, q, up_at(f), turn)
            if kind == 1:
                w = COL["ffn_conv"] + 4 * FF1 * q + 4 * f + at
                nc.scalar.activation(cvb[:, r], ps[:, b, 0:T], ACT.Identity, scale=cols[:, bass.ds(w + 2, 1)],
                                     bias=cols[:, bass.ds(w + 3, 1)]).then_inc(cv0_ready, 1)
                if f < nf - 1:
                    split_hi(act, q, 3 * f + 3, turn)
                act.wait_ge(cv_ready, n)
                nc.scalar.activation(sgb[:, r], cvb[:, r], ACT.Silu).then_inc(sg_ready, 1)
            else:
                nc.scalar.activation(sgb[:, r], ps[:, b, 0:T], ACT.Silu).then_inc(sg_ready, 1)
                if f < nf - 1:
                    split_hi(act, q, 3 * f + 3, turn)
            if f < nf - 1:
                split_hi(act, q, 3 * f + 4, turn)
            act.wait_ge(act_ready, n + CREDIT)
            nc.scalar.activation(act_hi[:, f % 2], actb[:, r], ACT.Copy).then_inc(act_hi_ready, 1)
            if f < nf - 1:
                split_hi(act, q, 3 * f + 5, turn)

        def ffn_tile_dve(dve, steps, q, f, turn=None, ada=None):
            k, nf, kind, loops = FFN[q]
            n = F_BASE[q] + f + 1
            at = 0
            if turn is not None:
                n, at = n + 4 * turn, 16 * turn
            b, r = 4 + f % 4, f % 4
            if kind == 1:
                w = COL["ffn_conv"] + 4 * FF1 * q + 4 * f + at
                dve.wait_ge(cv0_ready, n)
                steps.mark(nc.vector.scalar_tensor_tensor(cvb[:, r, 1:T], ps[:, b, 0:T - 1], cols[:, bass.ds(w + 1, 1)],
                                                          cvb[:, r, 1:T], ALU.mult, ALU.add))
                steps.wait()
                nc.vector.scalar_tensor_tensor(cvb[:, r, 2:T], ps[:, b, 0:T - 2], cols[:, bass.ds(w, 1)],
                                               cvb[:, r, 2:T], ALU.mult, ALU.add).then_inc(cv_ready, 1)
                if f < nf - 1:
                    split_lo(dve, nc.vector, q, 3 * f + 3, turn)
            dve.wait_ge(sg_ready, n)
            nc.vector.tensor_tensor(actb[:, r], sgb[:, r], ps[:, b, T:2 * T], ALU.mult).then_inc(act_ready, 1)
            if kind == 2 and f < nf - 1:
                split_lo(dve, nc.vector, q, 3 * f + 3, turn)
            if ada:
                ada()
            dve.wait_ge(act_hi_ready, n)
            nc.vector.tensor_tensor(act_lo[:, f % 2], actb[:, r], act_hi[:, f % 2].bitcast(F32), ALU.subtract).then_inc(act_lo_ready, 1)
            if f < nf - 1:
                split_lo(dve, nc.vector, q, 3 * f + 5, turn)

        def ada_dve(dve, steps, q, piece, part, turn, per):
            slot = piece % 2
            base = PIECE_BASE[q]
            acc = ada_acc[:, bass.ds(piece - base + per * turn, 1), :].rearrange("p a b -> p (a b)")
            if part == 0:
                dve.wait_ge(ada_loaded[slot], 16 * (piece // 2 + 1) + 16 * (per // 2) * turn)
            for kb in range(4 * part, 4 * part + 4):
                src = ada_ring[:, slot, kb]
                if kb == 0:
                    steps.mark(nc.vector.tensor_scalar(acc, src, cond[:, 0:1], None, ALU.mult))
                else:
                    steps.wait()
                    ins = nc.vector.scalar_tensor_tensor(acc, src, cond[:, kb:kb + 1], acc, ALU.mult, ALU.add)
                    if kb == C - 1:
                        ins.then_inc(ada_summed, 1)
                    else:
                        steps.mark(ins)

        def ffn_act(act, q):
            k, nf, kind, loops = FFN[q]
            for f in range(2):
                ffn_tile_act(act, q, f)
            f0 = 2
            for turns, _ in loops:
                with act.Fori(0, turns) as i:
                    for j in range(4):
                        ffn_tile_act(act, q, f0 + j, i)
                f0 += 4 * turns
            for f in range(f0, nf):
                ffn_tile_act(act, q, f)

        def ffn_dve(dve, steps, q, next_ffn=None):
            k, nf, kind, loops = FFN[q]
            for f in range(2):
                ffn_tile_dve(dve, steps, q, f)
            f0, piece = 2, PIECE_BASE[q]
            for turns, pieces in loops:
                with dve.Fori(0, turns) as i:
                    steps.start_loop(i, (4 if kind == 1 else 0) + 7 * pieces)
                    for j in range(4):
                        part = (lambda: ada_dve(dve, steps, q, piece + j // 2, j % 2, i, pieces)) if pieces else None
                        ffn_tile_dve(dve, steps, q, f0 + j, i, part)
                    steps.end_loop(turns)
                f0, piece = f0 + 4 * turns, piece + pieces * turns
            for f in range(f0, nf):
                ffn_tile_dve(dve, steps, q, f)
            unit_products(dve, FIRST_UNIT[f"ffn{q}"], 3 * nf - 1)
            residual_dve(dve, steps, k, kind == 2, "acc", next_ffn)
            n0, n1 = PIECE_BASE[q], PIECE_BASE[q + 1]
            if n1 > n0:
                dve.wait_ge(ada_cols, q + 1)
                a = COL["ada_b"]
                steps.mark(nc.vector.tensor_tensor(mods[:, 4 * n0:4 * n1], ps[:, 4, 0:4 * (n1 - n0)],
                                                   cols[:, a + 4 * n0:a + 4 * n1], ALU.add))
                steps.wait()

        def ffn_pool(pool, q):
            k, nf, kind, loops = FFN[q]
            piece = PIECE_BASE[q]
            has_ada = PIECE_BASE[q + 1] > piece

            def load(slot, n, need):
                if need is not None:
                    pool.wait_ge(ada_summed, need)
                pool.dma_start(ada_ring[:, slot], dram["ada"][n]).then_inc(ada_loaded[slot], 16)

            if has_ada:
                pool.wait_ge(h_ready, 8 * k)
                for s in range(2):
                    load(s, piece + s, piece + s - 1 if piece else None)
            for f in range(2):
                split_lo(pool, nc.gpsimd, q, 3 * f + 4)
            f0 = 2
            for turns, pieces in loops:
                with pool.Fori(0, turns - 1 if pieces else turns) as i:
                    for j in range(4):
                        split_lo(pool, nc.gpsimd, q, 3 * (f0 + j) + 4, i)
                        if pieces and j % 2:
                            load(j // 2, bass_piece(piece, j // 2, i), piece + 2 * i + j // 2 + 1)
                f0 += 4 * turns
                if pieces:
                    for f in range(f0 - 4, f0):
                        split_lo(pool, nc.gpsimd, q, 3 * f + 4)
                piece += pieces * turns
            for f in range(f0, nf - 1):
                split_lo(pool, nc.gpsimd, q, 3 * f + 4)

        def bass_piece(piece, slot, i):
            return piece + slot + 2 + 2 * i

        at_ = Carver(arena, AR)
        qk = at_.cut(10, T)
        vtok = at_.cut(2, 512)
        sco = at_.cut(4, 384)
        prb = at_.cut(4, 384)
        prT = at_.cut(12, P)
        cosb, sinb = at_.cut(T), at_.cut(T)
        ang, turns_, resid, absr = at_.cut(T), at_.cut(T), at_.cut(T), at_.cut(T)
        reuse_at = at_.at
        pjr, pjs, pjroot, pjn = at_.cut(2, T), at_.cut(2, T), at_.cut(2, T), at_.cut(2, T)
        ropa, ropb = at_.cut(2, T), at_.cut(2, T)
        mx, mm, nm, sd, sm = at_.cut(4, 3), at_.cut(4, 2), at_.cut(4, 2), at_.cut(4, 2), at_.cut(4, 2)
        es, tot, rec = at_.cut(4, 2), at_.cut(4, 2), at_.cut(4, 2)
        alibi = at_.cut(8, 384)

        TWO_PI = 2 * np.pi
        C1 = 6.28125
        C2 = float(np.round((TWO_PI - C1) * 2**20) / 2**20)
        C3 = float(TWO_PI - C1 - C2)
        PI_IN = float(np.nextafter(np.float32(np.pi), np.float32(0)))

        def angles_dve(dve, steps):
            dve.wait_ge(small_loaded, 16 * N_SMALL)
            m, w = steps.mark, steps.wait
            m(nc.vector.tensor_scalar(ang, positions[:], col("inv_freq"), None, ALU.mult))
            w()
            m(nc.vector.tensor_scalar(turns_, ang, 1.0 / TWO_PI, None, ALU.mult))
            w()
            m(nc.vector.tensor_scalar(turns_, turns_, MAGIC, None, ALU.add))
            w()
            m(nc.vector.tensor_scalar(turns_, turns_, -MAGIC, None, ALU.add))
            w()
            for c_ in (C1, C2, C3):
                m(nc.vector.scalar_tensor_tensor(ang, turns_, -c_, ang, ALU.mult, ALU.add))
                w()
            m(nc.vector.tensor_scalar(resid, ang, PI_IN, -PI_IN, ALU.min, ALU.max))
            w()
            m(nc.vector.tensor_scalar(absr, resid, -1.0, None, ALU.mult))
            w()
            nc.vector.tensor_tensor(absr, absr, resid, ALU.max).then_inc(angle_ready, 1)

        def angles_act(act):
            act.wait_ge(angle_ready, 1)
            nc.scalar.activation(sinb, resid, ACT.Sin)
            nc.scalar.activation(cosb, absr, ACT.Sin, scale=-1.0, bias=col("half_pi")).then_inc(sine_ready, 1)

        def attn_in_pe(pe):
            first = FIRST_UNIT["attn_in"]
            for t in range(12):
                if t < 10:
                    if t == 0:
                        for c in range(C):
                            pe.wait_ge(u_ready, u_count(0, c))
                    if t >= 2:
                        pe.wait_ge(pjsq_ready, t - 1)
                    s = take_unit(pe, first, t)
                    for k in range(C):
                        last = nc.tensor.matmul(ps[:, t % 2, 0:T], ring[:, s, k], u[:, k], start=(k == 0), stop=(k == C - 1))
                    last.then_inc(unit_done[s], 1)
                if 0 <= t - 1 < 10:
                    a = t - 1
                    pe.wait_ge(pjsq_ready, a + 1)
                    if a >= 2:
                        pe.wait_ge(pjroot_ready, a - 1)
                    nc.tensor.matmul(ps[:, 2 + a % 2, 0:T], const("block_ones"), pjs[:, a % 2], start=True, stop=True).then_inc(pjss_ready, 1)
                if 0 <= t - 2 < 10:
                    a = t - 2
                    pe.wait_ge(qn_ready, a + 1)
                    if a >= 2:
                        pe.wait_ge(rope_ready, a - 1)
                    nc.tensor.matmul(ps[:, 4 + a % 2, 0:T], const("rotate"), pjn[:, a % 2], start=True, stop=True).then_inc(rot_ready, 1)
            for n in range(2):
                s = take_unit(pe, first, 10 + n)
                for tb in range(2):
                    for k in range(C):
                        last = nc.tensor.matmul(ps[:, 6, tb * 256 + n * P:tb * 256 + (n + 1) * P], u[:, k, tb * P:(tb + 1) * P],
                                                ring[:, s, k], start=(n == 0 and tb == 0 and k == 0), stop=(k == C - 1),
                                                skip_group_check=True)
                last.then_inc(unit_done[s], 1)

        def attn_in_act(act):
            for t in range(11):
                if t < 10:
                    unit_products(act, FIRST_UNIT["attn_in"], t)
                    if t >= 2:
                        act.wait_ge(qn_ready, t - 1)
                    nc.scalar.activation(pjr[:, t % 2], ps[:, t % 2, 0:T], ACT.Copy)
                    nc.scalar.activation(pjs[:, t % 2], ps[:, t % 2, 0:T], ACT.Square).then_inc(pjsq_ready, 1)
                if t >= 1:
                    a = t - 1
                    act.wait_ge(pjss_ready, a + 1)
                    nc.scalar.activation(pjroot[:, a % 2], ps[:, 2 + a % 2, 0:T], ACT.Sqrt, bias=col("eps"), scale=1.0 / HD).then_inc(pjroot_ready, 1)
            for t in (10, 11):
                unit_products(act, FIRST_UNIT["attn_in"], t)
            nc.scalar.activation(vtok[:, :, 0:256], ps[:, 6, :].rearrange("p (a b) -> p a b", a=2), ACT.Copy).then_inc(v_copied, 1)

        def attn_in_dve(dve, steps):
            m, w = steps.mark, steps.wait
            dve.wait_ge(sine_ready, 1)
            for t in range(11):
                if t < 10:
                    r = t % 2
                    dve.wait_ge(pjroot_ready, t + 1)
                    m(nc.vector.reciprocal(pjroot[:, r], pjroot[:, r]))
                    if t >= 2:
                        dve.wait_ge(rot_ready, t - 1)
                    w()
                    nc.vector.scalar_tensor_tensor(pjn[:, r], pjr[:, r], col("k_gain" if t < 2 else "q_gain"), pjroot[:, r],
                                                   ALU.mult, ALU.mult).then_inc(qn_ready, 1)
                if t >= 1:
                    a, r = t - 1, (t - 1) % 2
                    dve.wait_ge(rot_ready, a + 1)
                    dve.wait_ge(qn_ready, a + 1)
                    m(nc.vector.tensor_tensor(ropa[:, r], pjn[:, r], cosb, ALU.mult))
                    m(nc.vector.tensor_tensor(ropb[:, r], ps[:, 4 + r, 0:T], sinb, ALU.mult))
                    w()
                    nc.vector.tensor_tensor(qk[:, a], ropa[:, r], ropb[:, r], ALU.add).then_inc(rope_ready, 1)

        BATCHES = [4, 2]

        def head_of(which, b, j):
            jt, half = 2 * b + j // 2, j % 2
            if which == 0:
                g = 2 * (jt // 4) + half
                return 2 + jt, half, jt // 4, 64 * g, jt
            return jt, half, 4 + jt, 64 * (2 * jt + half), 4 + jt

        def core_pe(pe, which):
            if which == 0:
                pe.wait_ge(rope_ready, 10)
            else:
                pe.wait_ge(qk1_ready, 8)
            base = 4 * which
            for b in range(BATCHES[which]):
                n = base + b
                if b:
                    pe.wait_ge(max_ready, n)
                for j in range(4):
                    qt, half, kt, vc, oc = head_of(which, b, j)
                    rows = slice(64 * half, 64 * half + 64)
                    nc.tensor.matmul(ps[:, j, 0:P], qk[rows, qt, 0:P], qk[rows, kt, 0:P], start=True, stop=True)
                    last = nc.tensor.matmul(ps[:, j, P:384], qk[rows, qt, P:T], qk[rows, kt, 0:T], start=True, stop=True)
                last.then_inc(sc_ready, 1)
                pe.wait_ge(p_ready, n + 1)
                if b:
                    pe.wait_ge(ptc_ready, n)
                for j in range(4):
                    for t in range(3):
                        x = 3 * j + t
                        last = nc.tensor.transpose(ps[:, 4 + x // 4, (x % 4) * P:(x % 4 + 1) * P], prb[:, j, t * P:(t + 1) * P], ident)
                last.then_inc(pt_ready, 1)
                pe.wait_ge(ptc_ready, n + 1)
                pe.wait_ge(v_copied, which + 1)
                if b:
                    pe.wait_ge(mix_ready, CORE_MIX[which] + b)
                for j in range(4):
                    qt, half, kt, vc, oc = head_of(which, b, j)
                    at = (j // 2) * T
                    o = ps[64 * half:64 * half + 64, 7]
                    nc.tensor.matmul(o[:, at:at + P], vtok[:, 0, vc:vc + 64], prT[:, 3 * j], start=True, stop=True)
                    nc.tensor.matmul(o[:, at + P:at + T], vtok[:, 0, vc:vc + 64], prT[:, 3 * j + 1], start=True, stop=False)
                    last = nc.tensor.matmul(o[:, at + P:at + T], vtok[:, 1, vc:vc + 64], prT[:, 3 * j + 2], start=False, stop=True)
                last.then_inc(pv_ready, 1)

        CORE_MIX = [0, 16]

        def core_act(act, which):
            base = 4 * which
            for b in range(BATCHES[which]):
                n = base + b
                act.wait_ge(max_ready, n + 1)
                if b:
                    act.wait_ge(pt_ready, n)
                for j in range(4):
                    nc.scalar.activation(prb[:, j, 0:P], sco[:, j, 0:P], ACT.Exp, bias=nm[:, j, 0:1], accum_out=sm[:, j, 0:1])
                    last = nc.scalar.activation(prb[:, j, P:384], sco[:, j, P:384], ACT.Exp, bias=nm[:, j, 1:2], accum_out=sm[:, j, 1:2])
                if which == 0:
                    last = nc.scalar.activation(es, sd, ACT.Exp)
                last.then_inc(exp_ready, 1)
                act.wait_ge(pt_ready, n + 1)
                if b:
                    act.wait_ge(pv_ready, n)
                for x in range(3):
                    last = nc.scalar.activation(prT[:, 4 * x:4 * x + 4].rearrange("p a b -> p (a b)"), ps[:, 4 + x, :], ACT.Copy)
                last.then_inc(ptc_ready, 1)
                act.wait_ge(pv_ready, n + 1)
                oc = head_of(which, b, 0)[4]
                nc.scalar.activation(mix[:, oc:oc + 2].rearrange("p a b -> p (a b)"), ps[:, 7, :], ACT.Copy).then_inc(mix_ready, 1)

        def core_dve(dve, steps, which):
            m, w = steps.mark, steps.wait
            base = 4 * which
            for b in range(BATCHES[which]):
                n = base + b
                dve.wait_ge(sc_ready, n + 1)
                if b:
                    dve.wait_ge(exp_ready, n)
                for j in range(4):
                    bias = const("window_mask") if which == 0 else alibi[:, 4 * b + j]
                    m(nc.vector.scalar_tensor_tensor(sco[:, j], ps[:, j, 0:384], HD ** -0.5, bias, ALU.mult, ALU.add))
                w()
                m(nc.vector.tensor_reduce(mx.rearrange("p a b -> p (a b)"), sco.rearrange("p j (t k) -> p (j t) k", t=3), AX_X, ALU.max))
                w()
                m(nc.vector.tensor_copy(mm[:, :, 0], mx[:, :, 0]))
                m(nc.vector.tensor_tensor(mm[:, :, 1], mx[:, :, 1], mx[:, :, 2], ALU.max))
                w()
                if which == 0:
                    sk = cols[:, COL["sinks"] + 4 * b:COL["sinks"] + 4 * b + 4].unsqueeze(2).to_broadcast([P, 4, 2])
                    m(nc.vector.tensor_tensor(mm, mm, sk, ALU.max))
                    w()
                    m(nc.vector.tensor_tensor(sd, sk, mm, ALU.subtract))
                ins = nc.vector.tensor_scalar(nm, mm, -1.0, None, ALU.mult)
                m(ins)
                w()
                m2 = nc.vector.tensor_copy(mx[:, :, 0], nm[:, :, 0])
                m2.then_inc(max_ready, 1)
                dve.wait_ge(exp_ready, n + 1)
                if which == 0:
                    m(nc.vector.tensor_tensor(tot, sm, es, ALU.add))
                    w()
                    m(nc.vector.reciprocal(rec, tot))
                else:
                    m(nc.vector.reciprocal(rec, sm))
                w()
                for j in range(4):
                    m(nc.vector.tensor_scalar(prb[:, j, 0:P], prb[:, j, 0:P], rec[:, j, 0:1], None, ALU.mult))
                    m(nc.vector.tensor_scalar(prb[:, j, P:384], prb[:, j, P:384], rec[:, j, 1:2], None, ALU.mult))
                w()
                nc.vector.tensor_copy(mx[:, :, 1], rec[:, :, 0]).then_inc(p_ready, 1)

        qk1_ready = sem("moba_qk_ready")

        g_gates, g_rows_out, g_rows, g_cols, g_colsx = (sem(n) for n in (
            "gates_ready", "gates_stored", "gate_rows_loaded", "gate_cols_ready", "gate_cols_exp"))
        g_soft, g_texp, g_tabs = sem("softplus_ready"), sem("table_arg_ready"), sem("tables_exp")
        g_tap, g_conv, g_silu, g_z = sem("g_tap"), sem("g_conv"), sem("g_silu"), sem("g_z")
        g_sq, g_ss, g_root, g_qkn = sem("g_squares"), sem("g_sums"), sem("g_root"), sem("g_qk_normed")
        g_vt, g_vb, g_kt, g_kk, g_ktok, g_kb, g_kd = (sem(n) for n in (
            "g_v_turned", "g_v_scaled", "g_k_turned", "g_kk", "g_k_copied", "g_k_scaled", "g_k_decayed"))
        g_egr_in, g_egr, g_mt, g_qkm, g_bt, g_x, g_p, g_pc, g_dx = (sem(n) for n in (
            "g_rows_loaded", "g_rows_exp", "g_mt", "g_qk_masked", "g_level_masked", "g_inverse", "g_bx", "g_bx_copied", "g_xbx"))
        g_uw, g_u, g_wt, g_qd, g_s = (sem(n) for n in ("g_uw", "g_u_copied", "g_w_copied", "g_q_decayed", "g_state"))
        pe_waited = sem("pe_waited")
        g_zc, g_ln = sem("g_z_copied"), sem("g_ln")
        g_ws, g_vn, g_op, g_kv, g_o = (sem(n) for n in ("g_ws", "g_v_new", "g_out", "g_kv", "g_out_copied"))

        gd, gx = Carver(arena, AR), Carver(gdn_tiles, 10 * 1024)
        cbuf = squares[:]
        m_tab = scaled[:].rearrange("p a b -> p (a b)").rearrange("p (h t s) -> p h t s", h=GH, t=2)
        mt_tab, qk_tab = gd.cut(GH, 2, CH), gd.cut(GH, 2, CH)
        qkv, zs, egr = gd.cut(8, T), gd.cut(4, T), gd.cut(4, T)
        kb_at = gd.at
        kb, kd, vb = gd.cut(4, 2, P), gd.cut(4, 2, P), gd.cut(4, 2, P)
        m_, mt_, qk_ = gd.cut(4, 2, CH), gd.cut(4, 2, CH), gd.cut(4, 2, CH)
        bt, x_, xt_ = gd.cut(5, 8, CH), gd.cut(8, CH), gd.cut(8, CH)
        p1, vnew = gd.cut(8, CH), gd.cut(4, P)
        ktok, qd, state, ot = gd.cut(4, P), gd.cut(4, T), gd.cut(4, P), gd.cut(4, T)
        uu, wt = gx.cut(8, P), gx.cut(4, T)
        qkn, zs_now, gsq, grt = gx.cut(4, T), gx.cut(4, T), gx.cut(4, T), gx.cut(4, T)
        bcol, gcol, ecol, kbcol, nea = gd.cut(2, GH), gd.cut(2, GH), gd.cut(2, GH), gd.cut(2, GH), gd.cut(1)
        gates, xa, ta, tb_ = ot[:, 0], ot[:, 1], ot[:, 2], ot[:, 3]
        g_row = qkv.rearrange("p a b -> p (a b)").rearrange("p (h t s) -> p h t s", h=GH, t=2)
        b_row = arena[:, kb_at:kb_at + 2 * 4 * T].rearrange("p (h t s) -> p h t s", h=GH, t=2)
        N_TURNS = GH // GB

        def gdn_gates_pe(pe):
            first = FIRST_UNIT["gdn_gates"]
            for c in range(C):
                pe.wait_ge(u_ready, u_count(2, c))
            s = take_unit(pe, first, 0)
            for k in range(C):
                last = nc.tensor.matmul(ps[:, 0, 0:T], ring[:, s, k], u[:, k], start=(k == 0), stop=(k == C - 1))
            last.then_inc(unit_done[s], 1)
            pe.wait_ge(g_gates, 1)
            for t in range(2):
                last = nc.tensor.matmul(ps[:, 7, 64 * t:64 * t + 48], gates[0:48, t * P:(t + 1) * P], ident[0:48, 0:48],
                                        start=True, stop=True)
            last.then_inc(g_cols, 1)

        def gdn_gates_act(act, steps):
            m, w = steps.mark, steps.wait
            unit_products(act, FIRST_UNIT["gdn_gates"], 0)
            act.wait_ge(g_soft, 1)
            m(nc.scalar.activation(gates[0:16], ps[0:16, 0, 0:T], ACT.Sigmoid))
            a = slice(32, 48)
            m(nc.scalar.activation(xa[a], ps[a, 0, 0:T], ACT.Identity, bias=cols[a, COL["dt_bias"]:COL["dt_bias"] + 1]))
            w()
            m(nc.scalar.activation(ta[a], xa[a], ACT.Abs))
            w()
            m(nc.scalar.activation(ta[a], ta[a], ACT.Exp, scale=-1.0))
            m(nc.scalar.activation(nea[a], cols[a, COL["a_log"]:COL["a_log"] + 1], ACT.Exp))
            w()
            nc.scalar.activation(ta[a], ta[a], ACT.Ln, bias=cols[a, COL["one"]:COL["one"] + 1]).then_inc(g_soft, 1)
            act.wait_ge(g_colsx, 1)
            nc.scalar.activation(ecol, gcol, ACT.Exp).then_inc(g_colsx, 1)
            act.wait_ge(g_texp, 2)
            nc.scalar.activation(qk_tab, qk_tab, ACT.Exp).then_inc(g_tabs, 1)
            nc.scalar.activation(m_tab, m_tab, ACT.Exp).then_inc(g_tabs, 1)

        def gdn_gates_dve(dve, steps):
            m, w = steps.mark, steps.wait
            a = slice(32, 48)
            nc.vector.memset(gates[0:64], 0.0).then_inc(g_soft, 1)
            dve.wait_ge(g_soft, 2)
            m(nc.vector.tensor_scalar(tb_[a], xa[a], 0.0, None, ALU.max))
            m(nc.vector.tensor_scalar(nea[a], nea[a], -1.0, None, ALU.mult))
            w()
            m(nc.vector.tensor_tensor(tb_[a], tb_[a], ta[a], ALU.add))
            w()
            m(nc.vector.tensor_scalar(tb_[a], tb_[a], nea[a], None, ALU.mult))
            w()
            at, _ = CONST["reset"]
            nc.vector.tensor_tensor_scan(gates[a], consts[a, at:at + T], tb_[a], 0.0, ALU.mult, ALU.add).then_inc(g_gates, 1)
            dve.wait_ge(g_cols, 1)
            cols_ = ps[:, 7, 0:2 * 64].rearrange("p (t n) -> p t n", t=2)
            m(nc.vector.tensor_copy(bcol, cols_[:, :, 0:16]))
            nc.vector.tensor_copy(gcol, cols_[:, :, 32:48]).then_inc(g_colsx, 1)
            dve.wait_ge(g_colsx, 2)
            m(nc.vector.tensor_tensor(kbcol, bcol, ecol, ALU.mult))
            dve.wait_ge(g_rows, 64)
            gc4 = gcol.rearrange("p t h -> p h t").unsqueeze(3).to_broadcast([P, GH, 2, CH])
            bc4 = bcol.rearrange("p t h -> p h t").unsqueeze(3).to_broadcast([P, GH, 2, CH])
            flat = lambda x: x.rearrange("p h t s -> p (h t) s")
            each = lambda name: const(name).unsqueeze(1).to_broadcast([P, GH * 2, CH])
            m(nc.vector.tensor_tensor(mt_tab, g_row, gc4, ALU.subtract))
            w()
            nc.vector.tensor_tensor(flat(qk_tab), flat(mt_tab), each("incl_up_neg"), ALU.add).then_inc(g_texp, 1)
            nc.vector.scalar_tensor_tensor(flat(m_tab), flat(mt_tab), -1.0, each("strict_lo_neg"), ALU.mult, ALU.add).then_inc(g_texp, 1)
            dve.wait_ge(g_tabs, 1)
            m(nc.vector.tensor_tensor(mt_tab, qk_tab, b_row, ALU.mult))
            w()
            m(nc.vector.tensor_tensor(flat(mt_tab), flat(mt_tab), each("strict_up"), ALU.mult))
            dve.wait_ge(g_tabs, 2)
            m(nc.vector.tensor_tensor(m_tab, m_tab, bc4, ALU.mult))
            w()

        def gdn_gates_pool(pool):
            pool.wait_ge(g_gates, 1)
            pool.dma_start(gates_dram[0], gates[0:16]).then_inc(g_rows_out, 16)
            pool.dma_start(gates_dram[1], gates[32:48]).then_inc(g_rows_out, 16)
            pool.wait_ge(g_rows_out, 32)
            for n, dst in ((0, b_row), (1, g_row)):
                for half in range(2):
                    src = gates_dram[n].rearrange("h (t f s) -> f h t s", t=2, f=2)[half].partition_broadcast(64)
                    pool.dma_start(dst[64 * half:64 * half + 64], src).then_inc(g_rows, 16)

        def gdn_turn_pool(pool, i):
            pool.wait_ge(g_z, 4 * i + 4)
            pool.wait_ge(mix_ready, 4 + i)
            gain_ = col("gdn_norm").unsqueeze(2).to_broadcast([P, 4, T])
            nc.gpsimd.tensor_tensor(zs_now, zs, gain_, ALU.mult).then_inc(g_zc, 1)
            pool.wait_ge(g_s, 5 * i + 1)
            pool.dma_start(egr, gates_dram[1][bass.ds(4 * i, 4), :].partition_broadcast(P)).then_inc(g_egr_in, 16)
            pool.wait_ge(g_mt, i + 1)
            for lv in range(1, 6):
                up = const("level_up", lv, CH).unsqueeze(1).to_broadcast([P, 8, CH])
                nc.gpsimd.tensor_tensor(bt[:, lv - 1], mt_.rearrange("p h t s -> p (h t) s"), up, ALU.mult).then_inc(g_bt, 1)

        def small_tiles(pe):
            pe.sem_inc(pe_waited, 1)

        def gdn_unit_pe(pe, j, i=None):
            first, ahead = FIRST_UNIT["gdn_in"], 0 if i is None else 1
            if j >= 4:
                pe.wait_ge(g_conv, 8 * ahead + j - 3 + (8 * i if ahead else 0))
            elif ahead:
                pe.wait_ge(g_z, 4 * i + j + 1)
            s = take_unit(pe, first + 12 * ahead, j, 12, i)
            for k in range(C):
                last = nc.tensor.matmul(ps[:, j % 4, 0:T], ring[:, s, k], u[:, k], start=(k == 0), stop=(k == C - 1))
            last.then_inc(unit_done[s], 1)

        def gdn_turn_pe(pe, i, more):
            def projections(*tiles):
                if more:
                    for j in tiles:
                        gdn_unit_pe(pe, j, i)

            pe.wait_ge(g_silu, 8 * i + 8)
            for n in range(4):
                for t in range(2):
                    x = 2 * n + t
                    last = nc.tensor.transpose(ps[:, 6 + x // 4, (x % 4) * P:(x % 4 + 1) * P], qkv[:, 4 + n, t * P:(t + 1) * P], ident)
            last.then_inc(g_vt, 1)
            pe.wait_ge(g_sq, 2 * i + 1)
            for n in range(2):
                last = nc.tensor.matmul(ps[:, 4 + n], ones, gsq[:, 2 * n:2 * n + 2], start=True, stop=True)
            last.then_inc(g_ss, 1)
            projections(0)
            pe.wait_ge(g_qkn, i + 1)
            for n in range(2):
                for t in range(2):
                    last = nc.tensor.transpose(ps[:, 4, (2 * n + t) * P:(2 * n + t + 1) * P], qkn[:, 2 + n, t * P:(t + 1) * P], ident)
            last.then_inc(g_kt, 1)
            for q in range(2):
                for n in range(2):
                    for c in range(4):
                        tk = slice(c * CH, (c + 1) * CH)
                        at = 256 * q + 128 * n + 64 * (c // 2)
                        rhs = qkn[:, 2 + n, tk] if q == 0 else qkn[:, n, tk]
                        last = nc.tensor.matmul(ps[64 * (c % 2):64 * (c % 2) + 64, 5, at:at + 64], qkn[:, 2 + n, tk], rhs, start=True, stop=True)
            last.then_inc(g_kk, 1)
            projections(1, 2)
            for lv in range(1, 6):
                pe.wait_ge(g_x, 6 * i + lv)
                pe.wait_ge(g_bt, 5 * i + lv)
                if lv == 1:
                    pe.wait_ge(g_ktok, i + 1)
                small_tiles(pe)
                for n in range(8):
                    for f in range(2):
                        r = slice(64 * f, 64 * f + 64)
                        last = nc.tensor.matmul(ps[r, 4, 64 * n:64 * n + 64], bt[r, lv - 1, n], x_[r, n], start=True, stop=True)
                last.then_inc(g_p, 1)
                pe.wait_ge(g_pc, 5 * i + lv)
                small_tiles(pe)
                for which in range(2):
                    if which == 0 and lv == 5:
                        continue
                    for n in range(8):
                        for f in range(2):
                            r = slice(64 * f, 64 * f + 64)
                            o = ps[r, 5 + which, 64 * n:64 * n + 64]
                            if which == 0:
                                last = nc.tensor.matmul(o, xt_[r, n], p1[r, n], start=True, stop=True)
                            else:
                                last = nc.tensor.matmul(o, p1[r, n], xt_[r, n], start=True, stop=True)
                last.then_inc(g_dx, 1)
                projections(2 + lv)
            pe.wait_ge(g_x, 6 * i + 6)
            pe.wait_ge(g_vb, i + 1)
            pe.wait_ge(g_kb, i + 1)
            small_tiles(pe)
            for n in range(8):
                for f in range(2):
                    r = slice(64 * f, 64 * f + 64)
                    nc.tensor.matmul(ps[r, 4 + n // 4, (n % 4) * P:(n % 4 + 1) * P], xt_[r, n], vb[r, n // 2, n % 2], start=True, stop=True)
                    last = nc.tensor.matmul(ps[:, 6 + f, 64 * n:64 * n + 64], kb[r, n // 2, n % 2], xt_[r, n], start=True, stop=True)
            last.then_inc(g_uw, 1)
            projections(8)
            pe.wait_ge(g_u, i + 1)
            pe.wait_ge(g_wt, i + 1)
            pe.wait_ge(g_qd, i + 1)
            for c in range(4):
                f, t = c % 2, c // 2
                r, tk = slice(64 * f, 64 * f + 64), slice(c * CH, (c + 1) * CH)
                pe.wait_ge(g_s, 5 * i + c + 1)
                for n in range(4):
                    last = nc.tensor.matmul(ps[r, 4, n * P:(n + 1) * P], wt[:, n, tk], state[:, n], start=True, stop=True)
                last.then_inc(g_ws, 1)
                if c:
                    pe.wait_ge(g_o, 4 * i + c)
                for n in range(4):
                    nc.tensor.matmul(ps[:, 5, n * CH:(n + 1) * CH], state[:, n], qd[:, n, tk], start=(n == 0), stop=False, skip_group_check=True)
                pe.wait_ge(g_vn, 4 * i + c + 1)
                for n in range(4):
                    last = nc.tensor.matmul(ps[:, 6, n * P:(n + 1) * P], kd[r, n, t], vnew[r, n], start=True, stop=True)
                last.then_inc(g_kv, 1)
                for n in range(4):
                    last = nc.tensor.matmul(ps[:, 5, n * CH:(n + 1) * CH], vnew[r, n], qk_[r, n, t], start=False, stop=True, skip_group_check=True)
                last.then_inc(g_op, 1)
                if c < 3:
                    projections(9 + c)
            pe.wait_ge(g_sq, 2 * i + 2)
            pe.wait_ge(g_s, 5 * i + 5)
            for n in range(2):
                last = nc.tensor.matmul(ps[:, 4 + n], ones, gsq[:, 2 * n:2 * n + 2], start=True, stop=True)
            last.then_inc(g_ss, 1)

        def gdn_tile_act(act, j, i=None):
            first, ahead = FIRST_UNIT["gdn_in"], 0 if i is None else 1
            turns = 0 if i is None else i
            wc = COL["gdn_conv"] + 32 * ahead
            unit_products(act, first + 12 * ahead, j, 12, i)
            if j < 8:
                nc.scalar.activation(cbuf[:, j], ps[:, j % 4, 0:T], ACT.Identity,
                                     scale=cols[:, bass.ds(wc + 4 * j + 3 + 32 * turns, 1)]).then_inc(g_tap, 1)
            if 1 <= j <= 8:
                act.wait_ge(g_conv, 8 * (turns + ahead) + j)
                if ahead and j == 1:
                    act.wait_ge(g_qkn, turns + 1)
                nc.scalar.activation(qkv[:, j - 1], cbuf[:, j - 1], ACT.Silu).then_inc(g_silu, 1)
            if j >= 8:
                if ahead and j == 8:
                    act.wait_ge(g_zc, turns + 1)
                nc.scalar.activation(zs[:, j - 8], ps[:, j % 4, 0:T], ACT.Silu).then_inc(g_z, 1)

        def gdn_turn_act(act, steps, i, more):
            def projections(*tiles):
                if more:
                    for j in tiles:
                        gdn_tile_act(act, j, i)

            act.wait_ge(g_silu, 8 * i + 4)
            nc.scalar.activation(gsq, qkv[:, 0:4], ACT.Square).then_inc(g_sq, 1)
            act.wait_ge(g_ss, 2 * i + 1)
            act.wait_ge(mix_ready, 4 + i)
            nc.scalar.activation(grt.rearrange("p a b -> p (a b)"), ps[:, 4:6].rearrange("p a b -> p (a b)"), ACT.Ln,
                                 bias=col("eps")).then_inc(g_ln, 1)
            act.wait_ge(g_ln, 2 * i + 1)
            nc.scalar.activation(grt, grt, ACT.Exp, scale=-0.5).then_inc(g_root, 1)
            act.wait_ge(g_vt, i + 1)
            for n in range(4):
                for t in range(2):
                    x = 2 * n + t
                    last = nc.scalar.activation(vb[:, n, t], ps[:, 6 + x // 4, (x % 4) * P:(x % 4 + 1) * P], ACT.Copy,
                                                scale=bcol[:, t, bass.ds(4 * i + n, 1)])
            last.then_inc(g_vb, 1)
            act.wait_ge(g_egr_in, 16 * i + 16)
            nc.scalar.activation(egr, egr, ACT.Exp).then_inc(g_egr, 1)
            projections(0)
            act.wait_ge(g_kt, i + 1)
            nc.scalar.activation(ktok.rearrange("p a b -> p (a b)"), ps[:, 4], ACT.Copy).then_inc(g_ktok, 1)
            act.wait_ge(g_ktok, i + 1)
            for n in range(4):
                for t in range(2):
                    last = nc.scalar.activation(kb[:, n, t], ktok[:, 2 * (n // 2) + t], ACT.Copy, scale=kbcol[:, t, bass.ds(4 * i + n, 1)])
            last.then_inc(g_kb, 1)
            projections(1, 2)
            for lv in range(1, 6):
                act.wait_ge(g_p, 5 * i + lv)
                nc.scalar.activation(p1.rearrange("p a b -> p (a b)"), ps[:, 4], ACT.Copy).then_inc(g_pc, 1)
                projections(2 + lv)
            act.wait_ge(g_uw, i + 1)
            nc.scalar.activation(uu.rearrange("p a b -> p (a b)"), ps[:, 4:6].rearrange("p a b -> p (a b)"), ACT.Copy).then_inc(g_u, 1)
            projections(8)
            for c in range(4):
                act.wait_ge(g_op, 4 * i + c + 1)
                nc.scalar.activation(ot[:, :, c * CH:(c + 1) * CH], ps[:, 5, 0:256].rearrange("p (a b) -> p a b", a=4), ACT.Copy).then_inc(g_o, 1)
                if c < 3:
                    projections(9 + c)
            act.wait_ge(g_o, 4 * i + 4)
            nc.scalar.activation(gsq, ot, ACT.Square).then_inc(g_sq, 1)
            act.wait_ge(g_ss, 2 * i + 2)
            act.wait_ge(g_qkn, i + 1)
            nc.scalar.activation(grt.rearrange("p a b -> p (a b)"), ps[:, 4:6].rearrange("p a b -> p (a b)"), ACT.Ln, bias=col("eps"),
                                 scale=1.0 / P).then_inc(g_ln, 1)
            act.wait_ge(g_ln, 2 * i + 2)
            nc.scalar.activation(grt, grt, ACT.Exp, scale=-0.5).then_inc(g_root, 1)

        def gdn_tile_dve(dve, steps, j, i=None):
            ahead, turns = 0 if i is None else 1, 0 if i is None else i
            wc = COL["gdn_conv"] + 32 * ahead
            dve.wait_ge(g_tap, 8 * (turns + ahead) + j + 1)
            for tap in range(3):
                d = 3 - tap
                ins = nc.vector.scalar_tensor_tensor(cbuf[:, j, d:T], ps[:, j % 4, 0:T - d],
                                                     cols[:, bass.ds(wc + 4 * j + tap + 32 * turns, 1)], cbuf[:, j, d:T], ALU.mult, ALU.add)
                if tap < 2:
                    steps.mark(ins)
                    steps.wait()
                else:
                    ins.then_inc(g_conv, 1)

        def gdn_turn_dve(dve, steps, i, more):
            m, w = steps.mark, steps.wait

            def projections(*tiles):
                if more:
                    for j in tiles:
                        gdn_tile_dve(dve, steps, j, i)

            nc.vector.memset(state, 0.0).then_inc(g_s, 1)
            dve.wait_ge(g_root, 2 * i + 1)
            m(nc.vector.scalar_tensor_tensor(qkn[:, 0:2], qkv[:, 0:2], P ** -0.5, grt[:, 0:2], ALU.mult, ALU.mult))
            w()
            nc.vector.tensor_tensor(qkn[:, 2:4], qkv[:, 2:4], grt[:, 2:4], ALU.mult).then_inc(g_qkn, 1)
            projections(0)
            dve.wait_ge(g_kk, i + 1)
            for q, (dst, tab) in enumerate(((m_, m_tab), (mt_, mt_tab), (qk_, qk_tab))):
                for n in range(2):
                    at = 128 * n + (256 if q == 2 else 0)
                    kk = ps[:, 5, at:at + 128].unsqueeze(1).to_broadcast([P, 2, 128])
                    ins = nc.vector.tensor_tensor(dst[:, 2 * n:2 * n + 2].rearrange("p a b c -> p a (b c)"), kk,
                                                  tab[:, bass.ds(4 * i + 2 * n, 2)].rearrange("p a b c -> p a (b c)"), ALU.mult)
                    if q == 1 and n == 1:
                        ins.then_inc(g_mt, 1)
                    elif q == 2 and n == 1:
                        ins.then_inc(g_qkm, 1)
                    else:
                        m(ins)
            w()
            dve.wait_ge(g_mt, i + 1)
            eye = const("stack_ident").unsqueeze(1).to_broadcast([P, 8, CH])
            lo = const("level_lo").unsqueeze(1).to_broadcast([P, 8, CH])
            up = const("level_up", 0, CH).unsqueeze(1).to_broadcast([P, 8, CH])
            m(nc.vector.tensor_tensor(x_, m_.rearrange("p a b c -> p (a b) c"), lo, ALU.mult))
            m(nc.vector.tensor_tensor(xt_, mt_.rearrange("p a b c -> p (a b) c"), up, ALU.mult))
            w()
            m(nc.vector.tensor_tensor(x_, eye, x_, ALU.subtract))
            nc.vector.tensor_tensor(xt_, eye, xt_, ALU.subtract).then_inc(g_x, 1)
            dve.wait_ge(g_ktok, i + 1)
            for n in range(4):
                for t in range(2):
                    dcol = qk_tab[:, bass.ds(4 * i + n, 1), t, CH - 1]
                    ins = nc.vector.tensor_scalar(kd[:, n, t], ktok[:, 2 * (n // 2) + t], dcol, None, ALU.mult)
                    m(ins)
            dve.wait_ge(g_egr, i + 1)
            for n in range(2):
                ins = nc.vector.tensor_tensor(qd[:, 2 * n:2 * n + 2], qkn[:, n].unsqueeze(1).to_broadcast([P, 2, T]), egr[:, 2 * n:2 * n + 2], ALU.mult)
                if n == 0:
                    m(ins)
                else:
                    ins.then_inc(g_qd, 1)
            projections(1, 2)
            for lv in range(1, 6):
                dve.wait_ge(g_dx, 5 * i + lv)
                flat = lambda x: x.rearrange("p a b -> p (a b)")
                if lv < 5:
                    m(nc.vector.tensor_tensor(flat(x_), flat(x_), ps[:, 5], ALU.subtract))
                nc.vector.tensor_tensor(flat(xt_), flat(xt_), ps[:, 6], ALU.subtract).then_inc(g_x, 1)
                projections(2 + lv)
            dve.wait_ge(g_uw, i + 1)
            nc.vector.tensor_copy(wt.rearrange("p h (t f s) -> p (h t) f s", t=2, f=2),
                                  ps[:, 6:8].rearrange("p f (n s) -> p n f s", n=8)).then_inc(g_wt, 1)
            dve.wait_ge(g_u, i + 1)
            for c in range(4):
                f, t = c % 2, c // 2
                r = slice(64 * f, 64 * f + 64)
                dve.wait_ge(g_ws, 4 * i + c + 1)
                ut = uu[r].rearrange("p (a b) c -> p a b c", b=2)[:, :, t]
                nc.vector.tensor_tensor(vnew[r], ut, ps[r, 4].rearrange("p (a b) -> p a b", a=4), ALU.subtract).then_inc(g_vn, 1)
                dve.wait_ge(g_kv, 4 * i + c + 1)
                for n in range(4):
                    ins = nc.vector.scalar_tensor_tensor(state[:, n], state[:, n], egr[:, n, c * CH + CH - 1:c * CH + CH],
                                                         ps[:, 6, n * P:(n + 1) * P], ALU.mult, ALU.add)
                    if n < 3:
                        m(ins)
                ins.then_inc(g_s, 1)
            dve.wait_ge(g_root, 2 * i + 2)
            m(nc.vector.tensor_tensor(ot, ot, grt, ALU.mult))
            w()
            dve.wait_ge(g_zc, i + 1)
            nc.vector.tensor_tensor(mix[:, bass.ds(4 * i, 4)], ot, zs_now, ALU.mult).then_inc(mix_ready, 1)

        def gdn_pe(pe):
            gdn_gates_pe(pe)
            for j in range(12):
                gdn_unit_pe(pe, j)
            with pe.Fori(0, N_TURNS - 1) as i:
                gdn_turn_pe(pe, i, True)
            gdn_turn_pe(pe, N_TURNS - 1, False)

        def gdn_act(act, steps):
            gdn_gates_act(act, steps)
            for j in range(12):
                gdn_tile_act(act, j)
            with act.Fori(0, N_TURNS - 1) as i:
                gdn_turn_act(act, steps, i, True)
            gdn_turn_act(act, steps, N_TURNS - 1, False)

        def gdn_dve(dve, steps):
            gdn_gates_dve(dve, steps)
            for j in range(8):
                gdn_tile_dve(dve, steps, j)
            with dve.Fori(0, N_TURNS - 1) as i:
                steps.start_loop(i, 16 + 1 + 4 + 3 + 8 + 1 + 4 + 12 + 1)
                gdn_turn_dve(dve, steps, i, True)
                steps.end_loop(N_TURNS - 1)
            gdn_turn_dve(dve, steps, N_TURNS - 1, False)

        def gdn_pool(pool):
            gdn_gates_pool(pool)
            with pool.Fori(0, N_TURNS) as i:
                gdn_turn_pool(pool, i)

        cm = Carver(arena, AR)
        PAD_A = TAPS_A - 1
        a_pad, a_acc, a_x, a_sq, a_rt = cm.cut(4, PAD_A + T), cm.cut(4, T), cm.cut(4, T), cm.cut(4, T), cm.cut(4, T)
        b_pad, b_acc, gate_t, cg_t = cm.cut(4, 2 + T), cm.cut(4, T), cm.cut(4, T), cm.cut(4, T)
        a_sig, b_cg, a_prod, b_prod = sem("a_sigmoid"), sem("b_c_gate"), sem("a_product"), sem("b_product")
        b_done, a_conv, a_biased, a_mean = sem("b_done"), sem("a_convolved"), sem("a_biased"), sem("a_mean")
        a_centred, a_sqd, a_var, a_root, a_norm = (sem(n) for n in ("a_centred", "a_squared", "a_var", "a_root", "a_normed"))

        def conv_pe(pe):
            first = FIRST_UNIT["conv_in"]
            for c in range(C):
                pe.wait_ge(u_ready, u_count(5, c))
            for n in range(20):
                b = n % 8
                if n >= 16:
                    pe.wait_ge(b_done, (n - 16) // 3 + 1)
                elif n >= 8:
                    pe.wait_ge(a_prod, (n - 8) // 2 + 1)
                s = take_unit(pe, first, n)
                for k in range(C):
                    last = nc.tensor.matmul(ps[:, b, 0:T], ring[:, s, k], u[:, k], start=(k == 0), stop=(k == C - 1))
                last.then_inc(unit_done[s], 1)
            flat = lambda x, n: x[:, 2 * n:2 * n + 2].rearrange("p a b -> p (a b)")
            pe.wait_ge(a_biased, 1)
            pe.wait_ge(b_done, 4)
            for n in range(2):
                last = nc.tensor.matmul(ps[:, n], const("block_ones"), flat(a_x, n), start=True, stop=True)
            last.then_inc(a_mean, 1)
            pe.wait_ge(a_sqd, 1)
            for n in range(2):
                last = nc.tensor.matmul(ps[:, 2 + n], const("block_ones"), flat(a_sq, n), start=True, stop=True)
            last.then_inc(a_var, 1)

        def conv_act(act):
            first = FIRST_UNIT["conv_in"]
            for j in range(4):
                unit_products(act, first, 2 * j + 1)
                nc.scalar.activation(gate_t[:, j], ps[:, 2 * j + 1, 0:T], ACT.Sigmoid).then_inc(a_sig, 1)
            for j in range(4):
                unit_products(act, first, 8 + 3 * j)
                nc.scalar.activation(cg_t[:, j], ps[:, (8 + 3 * j) % 8, 0:T], ACT.Copy).then_inc(b_cg, 1)
            act.wait_ge(a_conv, 1)
            for j in range(4):
                last = nc.scalar.activation(a_x[:, j], a_acc[:, j], ACT.Identity, bias=col("conv_a_b", j))
            last.then_inc(a_biased, 1)
            act.wait_ge(a_centred, 1)
            nc.scalar.activation(a_sq, a_x, ACT.Square).then_inc(a_sqd, 1)
            act.wait_ge(a_var, 1)
            nc.scalar.activation(a_rt.rearrange("p a b -> p (a b)"), ps[:, 2:4].rearrange("p a b -> p (a b)"), ACT.Sqrt, bias=col("eps"),
                                 scale=1.0 / 64).then_inc(a_root, 1)
            act.wait_ge(a_norm, 1)
            for j in range(4):
                nc.scalar.activation(mix[:, j], a_x[:, j], ACT.Silu, bias=col("ln_b", j)).then_inc(mix_ready, 1)

        def conv_dve(dve, steps):
            m, w = steps.mark, steps.wait
            first = FIRST_UNIT["conv_in"]
            m(nc.vector.memset(a_pad, 0.0))
            m(nc.vector.memset(b_pad, 0.0))
            w()
            for j in range(4):
                dve.wait_ge(a_sig, j + 1)
                nc.vector.tensor_tensor(a_pad[:, j, PAD_A:PAD_A + T], ps[:, 2 * j, 0:T], gate_t[:, j], ALU.mult).then_inc(a_prod, 1)
            dve.wait_ge(a_prod, 4)
            wa = COL["conv_a_w"]
            for j in range(4):
                m(nc.vector.tensor_scalar(a_acc[:, j], a_pad[:, j, 0:T], col("conv_a_w", j), None, ALU.mult))

            def a_taps(turns):
                with dve.Fori(0, turns) as i:
                    steps.start_loop(i, 12)
                    for q in range(3):
                        for j in range(4):
                            steps.wait(3)
                            m(nc.vector.scalar_tensor_tensor(a_acc[:, j], a_pad[:, j, bass.ds(1 + q + 3 * i, T)],
                                                             cols[:, bass.ds(wa + 4 * (1 + q) + j + 12 * i, 1)], a_acc[:, j], ALU.mult, ALU.add))
                    steps.end_loop(turns)

            a_taps((TAPS_A - 1) // 3)
            w()
            nc.vector.tensor_copy(a_rt[:, 0, 0:1], a_acc[:, 3, T - 1:T]).then_inc(a_conv, 1)
            for j in range(4):
                n = 8 + 3 * j
                dve.wait_ge(b_cg, j + 1)
                unit_products(dve, first, n + 1)
                unit_products(dve, first, n + 2)
                m(nc.vector.tensor_tensor(b_pad[:, j, 2:2 + T], ps[:, (n + 1) % 8, 0:T], cg_t[:, j], ALU.mult))
                w()
                m(nc.vector.tensor_scalar(b_acc[:, j], b_pad[:, j, 0:T], col("conv_b_w", 3 * j), None, ALU.mult))
                for q in (1, 2):
                    w()
                    m(nc.vector.scalar_tensor_tensor(b_acc[:, j], b_pad[:, j, q:q + T], col("conv_b_w", 3 * j + q), b_acc[:, j], ALU.mult, ALU.add))
                w()
                m(nc.vector.tensor_tensor(mix[:, 4 + j], b_acc[:, j], ps[:, (n + 2) % 8, 0:T], ALU.mult))
                w()
                nc.vector.tensor_copy(b_acc[:, j, 0:1], b_acc[:, j, 1:2]).then_inc(b_done, 1)
            dve.wait_ge(a_mean, 1)
            flat2 = lambda x: x.rearrange("p a b -> p (a b)")
            nc.vector.scalar_tensor_tensor(flat2(a_x), flat2(ps[:, 0:2]), -1.0 / 64, flat2(a_x), ALU.mult, ALU.add).then_inc(a_centred, 1)
            dve.wait_ge(a_root, 1)
            m(nc.vector.reciprocal(a_rt, a_rt))
            w()
            for j in range(4):
                ins = nc.vector.scalar_tensor_tensor(a_x[:, j], a_x[:, j], col("ln_g", j), a_rt[:, j], ALU.mult, ALU.mult)
            ins.then_inc(a_norm, 1)

        PADP = 16
        at_.at = max(at_.at, reuse_at)
        px, pb1 = at_.cut(4, PADP + T), at_.cut(4, PADP + T)
        at_.at, end = reuse_at, at_.at
        pb2 = at_.cut(4, PADP + T)
        at_.at = end
        pooled = at_.cut(4, T)
        pool_w = at_.cut(4, P)
        moba_loaded, p_copied, p_pooled, p_mixed = sem("moba_loaded"), sem("p_copied"), sem("p_pooled"), sem("p_mixed")

        def moba_pe(pe):
            first = FIRST_UNIT["pm_in"]
            for c in range(C):
                pe.wait_ge(u_ready, u_count(8, c))
            for n in range(12):
                if n >= 8:
                    pe.wait_ge(p_copied, n - 7)
                s = take_unit(pe, first, n)
                for k in range(C):
                    last = nc.tensor.matmul(ps[:, n % 8, 0:T], ring[:, s, k], u[:, k], start=(k == 0), stop=(k == C - 1))
                last.then_inc(unit_done[s], 1)
            pe.wait_ge(qk1_ready, 4)
            for n in range(4):
                s = take_unit(pe, first, 12 + n)
                for tb in range(2):
                    for k in range(C):
                        last = nc.tensor.matmul(ps[:, 4 + tb, n * P:(n + 1) * P], u[:, k, tb * P:(tb + 1) * P], ring[:, s, k],
                                                start=(n == 0 and k == 0), stop=(k == C - 1), skip_group_check=True)
                last.then_inc(unit_done[s], 1)
            pe.wait_ge(p_pooled, 1)
            pe.wait_ge(moba_loaded, 32)
            for g in range(4):
                last = nc.tensor.matmul(ps[:, 6 + g // 2, (g % 2) * T:(g % 2 + 1) * T], pool_w[:, g], pooled[:, g], start=True, stop=True)
            last.then_inc(p_mixed, 1)
            pe.wait_ge(mix_ready, 16)

        def moba_act(act):
            first = FIRST_UNIT["pm_in"]
            for n in range(12):
                unit_products(act, first, n)
                if n < 4:
                    nc.scalar.activation(px[:, n, PADP:PADP + T], ps[:, n, 0:T], ACT.Copy).then_inc(p_copied, 1)
                else:
                    nc.scalar.activation(qk[:, n - 4], ps[:, n % 8, 0:T], ACT.Copy).then_inc(qk1_ready, 1)
            for n in range(4):
                unit_products(act, first, 12 + n)
            nc.scalar.activation(vtok, ps[:, 4:6], ACT.Copy).then_inc(v_copied, 1)

        def moba_dve(dve, steps):
            m, w = steps.mark, steps.wait
            for b in (px, pb1, pb2):
                m(nc.vector.memset(b[:, :, 0:PADP], 0.0))
            w()
            dve.wait_ge(p_copied, 4)
            src = px
            for lv in range(4):
                dst, d = (pb1, pb2)[lv % 2], 1 << lv
                m(nc.vector.tensor_tensor(dst[:, lv:, PADP:], src[:, lv:, PADP:], src[:, lv:, PADP - d:PADP + T - d], ALU.add))
                w()
                src = dst
            inv = const("pool_inv").rearrange("p (g t) -> p g t", g=4)
            for g in range(4):
                m(nc.vector.tensor_tensor(pooled[:, g], (pb1, pb2)[g % 2][:, g, PADP:], inv[:, g], ALU.mult))
            w()
            nc.vector.tensor_tensor(pooled, pooled, px[:, :, PADP:], ALU.subtract).then_inc(p_pooled, 1)
            dve.wait_ge(p_mixed, 1)
            for g in range(4):
                nc.vector.tensor_scalar(mix[:, g], ps[:, 6 + g // 2, (g % 2) * T:(g % 2 + 1) * T], col("pool_b", g), col("pool_scale", g),
                                        ALU.add, ALU.mult).then_inc(mix_ready, 1)
            dve.wait_ge(moba_loaded, 32)

        def moba_pool(pool):
            pool.wait_ge(h_ready, 8 * 8)
            pool.dma_start(alibi, dram["alibi"]).then_inc(moba_loaded, 16)
            pool.dma_start(pool_w, dram["pool_w"]).then_inc(moba_loaded, 16)


        def pe_program(pe):
            pe.wait_ge(small_loaded, 16 * N_SMALL)
            norm_pe(pe, 0)
            attn_in_pe(pe)
            core_pe(pe, 0)
            lin_pe(pe, 0, "attn_out", C)
            norm_pe(pe, 1)
            ffn_pe(pe, 0)
            norm_pe(pe, 2)
            gdn_pe(pe)
            lin_pe(pe, 2, "gdn_out", 2 * C)
            norm_pe(pe, 3)
            ffn_pe(pe, 1)
            norm_pe(pe, 4)
            ffn_pe(pe, 2)
            norm_pe(pe, 5)
            conv_pe(pe)
            lin_pe(pe, 5, "conv_out", C)
            norm_pe(pe, 6)
            ffn_pe(pe, 3)
            norm_pe(pe, 7)
            ffn_pe(pe, 4)
            norm_pe(pe, 8)
            moba_pe(pe)
            core_pe(pe, 1)
            lin_pe(pe, 8, "pm_out", C)
            norm_pe(pe, 9)
            ffn_pe(pe, 5)
            norm_pe(pe, 10)

        def act_program(act):
            steps = Steps(act, act_steps)
            act.wait_ge(small_loaded, 16 * N_SMALL)
            nc.scalar.activation(cond[:], cols[:, COL["cond"]:COL["cond"] + 8], ACT.Silu).then_inc(cond_ready, 1)
            norm_act(act, 0)
            angles_act(act)
            attn_in_act(act)
            core_act(act, 0)
            split_first_act(act, 0)
            norm_act(act, 1)
            split_u_act(act, 0)
            ffn_act(act, 0)
            norm_act(act, 2)
            gdn_act(act, steps)
            split_first_act(act, 1)
            norm_act(act, 3)
            split_u_act(act, 1)
            ffn_act(act, 1)
            split_first_act(act, 2)
            norm_act(act, 4)
            split_u_act(act, 2)
            ffn_act(act, 2)
            norm_act(act, 5)
            conv_act(act)
            split_first_act(act, 3)
            norm_act(act, 6)
            split_u_act(act, 3)
            ffn_act(act, 3)
            split_first_act(act, 4)
            norm_act(act, 7)
            split_u_act(act, 4)
            ffn_act(act, 4)
            norm_act(act, 8)
            moba_act(act)
            core_act(act, 1)
            split_first_act(act, 5)
            norm_act(act, 9)
            split_u_act(act, 5)
            ffn_act(act, 5)
            norm_act(act, 10)

        def dve_program(dve):
            steps = Steps(dve, dve_steps)
            nc.vector.memset(cvb[:, 0, 0:1], 0.0).then_inc(act_ready, CREDIT)
            angles_dve(dve, steps)
            norm_dve(dve, steps, 0)
            attn_in_dve(dve, steps)
            core_dve(dve, steps, 0)
            residual_dve(dve, steps, 0, False, "lin", 0)
            norm_dve(dve, steps, 1)
            split_u_dve(dve, 0)
            dve.wait_ge(cond_ready, 1)
            ffn_dve(dve, steps, 0)
            norm_dve(dve, steps, 2)
            gdn_dve(dve, steps)
            residual_dve(dve, steps, 2, False, "lin", 1)
            norm_dve(dve, steps, 3)
            split_u_dve(dve, 1)
            ffn_dve(dve, steps, 1, 2)
            norm_dve(dve, steps, 4)
            split_u_dve(dve, 2)
            ffn_dve(dve, steps, 2)
            norm_dve(dve, steps, 5)
            conv_dve(dve, steps)
            residual_dve(dve, steps, 5, True, "lin", 3)
            norm_dve(dve, steps, 6)
            split_u_dve(dve, 3)
            ffn_dve(dve, steps, 3, 4)
            norm_dve(dve, steps, 7)
            split_u_dve(dve, 4)
            ffn_dve(dve, steps, 4)
            norm_dve(dve, steps, 8)
            moba_dve(dve, steps)
            core_dve(dve, steps, 1)
            residual_dve(dve, steps, 8, True, "lin", 5)
            norm_dve(dve, steps, 9)
            split_u_dve(dve, 5)
            ffn_dve(dve, steps, 5)
            norm_dve(dve, steps, 10)

        def pool_program(pool):
            ffn_pool(pool, 0)
            gdn_pool(pool)
            for q in (1, 2, 3):
                ffn_pool(pool, q)
            ffn_pool(pool, 4)
            moba_pool(pool)
            ffn_pool(pool, 5)

        SMALL = [(cols[:], dram["cols"]), (consts[:], dram["consts"]), (positions[:], dram["positions"])]
        N_SMALL = len(SMALL)
        block = ctx.enter_context(nc.Block())

        @block.sync
        def _(sp):
            for dst, src in SMALL:
                sp.dma_start(dst, src).then_inc(small_loaded, 16)
            sp.dma_start(h[:], dram["x"]).then_inc(h_loaded, 16)
            for s in range(RING):
                sp.dma_start(ring[:, s], dram["w"][s]).then_inc(raw_ready[s], 16)
            def refill(n, turn=None):
                s, at = n % RING, n + RING
                q = next((q for q in range(len(FFN)) if 0 <= n - FIRST_UNIT[f"ffn{q}"] < 3 * FFN[q][1]), None)
                free, need = (unit_done, n // RING + 1) if q is None else (split_done, split_count(q, n - FIRST_UNIT[f"ffn{q}"]))
                if turn is not None:
                    need, at = need + turn, at + RING * turn
                sp.wait_ge(free[s], need)
                sp.dma_start(ring[:, s], dram["w"][at]).then_inc(raw_ready[s], 16)

            runs, at = [], 0
            for name, n in UNITS:
                kind = name.startswith("ffn")
                if runs and runs[-1][2] == kind:
                    runs[-1][1] += n
                else:
                    runs.append([at, n, kind])
                at += n
            for first, n, _ in runs:
                n = min(n, N_UNITS - RING - first)
                if n >= RING:
                    with sp.Fori(0, n // RING) as i:
                        for s in range(RING):
                            refill(first + s, i)
                for m in range(n - n % RING, n):
                    refill(first + m)
            sp.wait_ge(out_ready, 8)
            sp.dma_start(out_dram, u[:]).then_inc(out_done, 16)
            sp.wait_ge(out_done, 16)

        @block.gpsimd
        def _(pool):
            pool_program(pool)

        @block.tensor
        def _(pe):
            pe_program(pe)

        @block.scalar
        def _(act):
            act_program(act)

        @block.vector
        def _(dve):
            dve_program(dve)


def columns(a):
    a = np.ascontiguousarray(a).reshape(-1, P)
    return a.T


def by_output(w):
    k, n = w.shape
    return w.reshape(k // D, C, P, n // P, P).transpose(3, 0, 2, 1, 4).reshape(-1, P, D)


def by_row(w):
    return w.reshape(-1, P, D)


def ffn_units(gate, up, down):
    g, u, d = by_output(gate), by_output(up), by_row(down)
    nf = d.shape[0]
    order = [g[0], u[0]]
    for f in range(1, nf):
        order += [g[f], u[f], d[f - 1]]
    return order + [d[nf - 1]]


def weight_stream(x):
    heads = np.array([attn_tile_heads(j) for j in range(C)]).reshape(-1)
    q_cols = (heads[:, None] * HD + np.arange(HD)).reshape(-1)
    w = x["attn_w_in"][0]
    units = list(by_output(w[:, D:D + 256])) + list(by_output(w[:, :D][:, q_cols])) + list(by_output(w[:, D + 256:]))
    units += list(by_output(x["attn_w_out"][0][q_cols]))
    up = x["ffn_w_up"][0]
    units += ffn_units(up[:, :3072], up[:, 3072:], x["ffn_w_down"][0])
    w = x["gdn_w_in"][0]
    gates = np.zeros((D, P), w.dtype)
    gates[:, 0:16] = w[:, 6144:6160]
    gates[:, 32:48] = w[:, 6160:6176]
    units += list(by_output(gates))
    tiles = by_output(w[:, :6144])
    for i in range(GH // GB):
        units += [tiles[t] for t in gdn_turn_tiles(i)] + [tiles[32 + 4 * i + j] for j in range(4)]
    units += list(by_output(x["gdn_w_out"][0]))
    up = x["ffn_w_up"][1]
    units += ffn_units(up[:, :3072], up[:, 3072:], x["ffn_w_down"][1])
    f2 = lambda l, s: ffn_units(x["ffn_w_gate_2"][l, s], x["ffn_w_up_2"][l, s], x["ffn_w_down_2"][l, s])
    units += f2(0, 0)
    t = by_output(x["conv_w_in_2"][0])
    units += [t[n] for j in range(4) for n in (j, 4 + j)] + [t[n] for j in range(4) for n in (12 + j, 16 + j, 8 + j)]
    units += list(by_output(x["conv_w_out_2"][0]))
    units += f2(0, 1) + f2(1, 0)
    units += list(by_output(x["pm_w_in_2"][0])) + list(by_output(x["pm_w_out_2"][0]))
    units += f2(1, 1)
    assert len(units) == N_UNITS
    return np.stack(units).reshape(N_UNITS, P, C, P)


def gdn_turn_tiles(i):
    return [2 * i, 2 * i + 1, 8 + 2 * i, 9 + 2 * i] + [16 + 4 * i + j for j in range(4)]


def packed_columns(x):
    out = np.zeros((P, N_COLS), np.float32)

    def put(name, a):
        out[:, COL[name]:COL[name] + a.shape[1]] = a

    put("mixer_norm", columns(x["mixer_norm"]))
    put("ffn_norm", columns(x["ffn_norm"]))
    put("q_gain", np.tile(x["attn_q_gain"][0], 2)[:, None])
    put("k_gain", np.tile(x["attn_k_gain"][0], 2)[:, None])
    taps = x["gdn_conv"][0].reshape(4, 32, P)
    order = [t for i in range(GH // GB) for t in gdn_turn_tiles(i)]
    put("gdn_conv", taps[:, order].transpose(2, 1, 0).reshape(P, 128))
    out[32:48, COL["a_log"]] = x["gdn_a_log"][0]
    out[32:48, COL["dt_bias"]] = x["gdn_dt_bias"][0]
    put("gdn_norm", x["gdn_norm"][0][:, None])
    fc = np.concatenate([x["ffn_conv"], x["ffn_conv_b"][:, None]], axis=1).reshape(2, 4, FF1, P)
    put("ffn_conv", fc.transpose(3, 0, 2, 1).reshape(P, -1))
    put("cond", columns(x["c_2"]))
    put("ada_b", columns(x["ada_b_2"]))
    put("ffn_norm_2", columns(x["ffn_norm_2"]))
    put("mix_norm", columns(x["mix_norm_2"]))
    put("conv_a_w", x["conv_a_w_2"][0].reshape(TAPS_A, 4, P).transpose(2, 0, 1).reshape(P, -1))
    put("conv_a_b", columns(x["conv_a_b_2"]))
    put("ln_g", columns(x["conv_a_ln_g_2"]))
    put("ln_b", columns(x["conv_a_ln_b_2"]))
    put("conv_b_w", x["conv_b_w_2"][0].reshape(3, 4, P).transpose(2, 1, 0).reshape(P, -1))
    put("pool_b", x["pool_b_2"][0].T)
    put("pool_scale", columns(x["pool_scale_2"]))
    put("final_norm", columns(x["final_norm_2"]))
    half = ROPE // 2
    freq = (np.float32(500000.0) ** (-np.arange(0, ROPE, 2, dtype=np.float32) / np.float32(ROPE))).astype(np.float32)
    for b in range(2):
        out[64 * b:64 * b + half, COL["inv_freq"]] = freq
        out[64 * b + half:64 * b + ROPE, COL["inv_freq"]] = freq
    sinks = x["attn_sinks"][0]
    put("sinks", np.broadcast_to(sinks[[hd for j in range(C) for hd in attn_tile_heads(j)]], (P, 16)))
    out[:, COL["eps"]] = EPS
    out[:, COL["half_pi"]] = np.pi / 2
    out[:, COL["one"]] = 1.0
    return out


def constant_matrices():
    out = np.zeros((P, N_CONST), np.float32)

    def put(name, a):
        out[:, CONST[name][0]:CONST[name][0] + a.shape[1]] = a

    i, j = np.arange(P)[:, None], np.arange(P)[None, :]
    put("ident", (i == j) * 1.0)
    put("ones", np.ones((P, P)))
    put("block_ones", (i // 64 == j // 64) * 1.0)
    rot = np.zeros((P, P))
    half = ROPE // 2
    for b in (0, 64):
        for m in range(half):
            rot[b + m + half, b + m] = -1.0
            rot[b + m, b + m + half] = 1.0
    put("rotate", rot)
    q = np.arange(P)[:, None]
    k = np.arange(T)[None, :]
    dist1 = P + q - k
    mask = np.concatenate([np.where(k[:, :P] <= q, 0.0, NEG), np.where((dist1 >= 0) & (dist1 < 128), 0.0, NEG)], axis=1)
    put("window_mask", mask)
    p, s = np.arange(P)[:, None] % 64, np.arange(64)[None, :]
    put("stack_ident", (p == s) * 1.0)
    put("level_lo", ((p // 2 == s // 2) & (p > s)) * 1.0)
    for lv in range(6):
        z = 2 ** lv
        a = CONST["level_up"][0] + 64 * lv
        out[:, a:a + 64] = (p // (2 * z) == s // (2 * z)) & (p // z % 2 == 0) & (s // z % 2 == 1)
    put("strict_lo_neg", np.where(s < p, 0.0, NEG))
    put("incl_up_neg", np.where(s >= p, 0.0, NEG))
    put("strict_up", (s > p) * 1.0)
    put("reset", np.broadcast_to((np.arange(T) % CH != 0) * 1.0, (P, T)))
    inv = np.stack([1.0 / np.minimum(np.arange(1, T + 1), w) for w in (2, 4, 8, 16)]).reshape(1, -1)
    put("pool_inv", np.broadcast_to(inv, (P, 4 * T)))
    return out


def alibi_matrices():
    q, k = np.arange(P)[:, None], np.arange(T)[None, :]
    slopes = 2.0 ** -(np.arange(8) + 1.0)
    out = np.zeros((P, 8, 384), np.float32)
    for n, slope in enumerate(slopes):
        d0, d1 = q - k[:, :P], P + q - k
        out[:, n, :P] = np.where(d0 >= 0, -slope * d0, NEG)
        out[:, n, P:] = np.where(d1 >= 0, -slope * d1, NEG)
    return out


def kernel(**inputs):
    import concourse.bacc as bacc
    from concourse.bass_utils import run_bass_kernel_spmd

    x = {k: np.asarray(v) for k, v in inputs.items()}
    ada = x["ada_w_2"].reshape(2, C, P, 18, PIECE).transpose(0, 3, 2, 1, 4).reshape(PIECES, P, C, PIECE)
    arrays = {
        "x": np.ascontiguousarray(x["x"][0].T.reshape(C, P, T).transpose(1, 0, 2)),
        "w": weight_stream(x),
        "ada": np.ascontiguousarray(ada),
        "cols": packed_columns(x),
        "consts": constant_matrices(),
        "alibi": alibi_matrices(),
        "pool_w": np.ascontiguousarray(x["pool_w_2"][0].transpose(1, 0, 2)),
        "positions": np.ascontiguousarray(np.broadcast_to(x["positions"], (P, T))),
    }
    nc = bacc.Bacc("TRN2", target_bir_lowering=False, num_devices=1)
    dram = {name: nc.dram_tensor(f"in_{name}", a.shape, mybir.dt.from_np(a.dtype), kind="ExternalInput").ap()
            for name, a in arrays.items()}
    out = nc.dram_tensor("out", (P, C, T), F32, kind="ExternalOutput").ap()
    build(nc, dram, out)
    r = run_bass_kernel_spmd(nc, [{f"in_{name}": a for name, a in arrays.items()}], core_ids=[0])
    got = r.results[0]["out"]
    return got.transpose(1, 0, 2).reshape(D, T).T.reshape(1, T, D)
```

```python
from contextlib import ExitStack

import concourse.bass as bass
import numpy as np
from concourse import mybir

F32 = mybir.dt.float32
FR = mybir.dt.float32r
I32 = mybir.dt.int32
ALU = mybir.AluOpType
ACT = mybir.ActivationFunctionType
AX_X = mybir.AxisListType.X

P = 128
D = 1024
T = 256
C = D // P
HD = 64
RING = 4
SPLIT = 3
EPS = 1e-6
NEG = -3.0e38
FF1, FF2 = 3072 // P, 2816 // P
GH, GB = 16, 4
CH = 64
TAPS_A = 31
ROPE = HD // 4
MAGIC = 12582912.0
PIECE = 512
PIECES = 2 * 9 * D // PIECE

UNITS = [("attn_in", 12), ("attn_out", 8), ("ffn0", 3 * FF1), ("gdn_gates", 1), ("gdn_in", 48), ("gdn_out", 16),
         ("ffn1", 3 * FF1), ("ffn2", 3 * FF2), ("conv_in", 20), ("conv_out", 8), ("ffn3", 3 * FF2),
         ("ffn4", 3 * FF2), ("pm_in", 16), ("pm_out", 8), ("ffn5", 3 * FF2)]
FIRST_UNIT = {}
N_UNITS = 0
for _name, _n in UNITS:
    FIRST_UNIT[_name] = N_UNITS
    N_UNITS += _n

COLS = [("mixer_norm", 16), ("ffn_norm", 16), ("q_gain", 1), ("k_gain", 1), ("gdn_conv", 128), ("a_log", 1),
        ("dt_bias", 1), ("gdn_norm", 1), ("ffn_conv", 8 * FF1), ("cond", 8), ("ada_b", 144), ("ffn_norm_2", 32),
        ("mix_norm", 16), ("conv_a_w", 4 * TAPS_A), ("conv_a_b", 4), ("ln_g", 4), ("ln_b", 4), ("conv_b_w", 12),
        ("pool_b", 4), ("pool_scale", 4), ("final_norm", 8), ("inv_freq", 1), ("sinks", 16), ("eps", 1),
        ("half_pi", 1), ("one", 1), ("zero", 1)]
COL = {}
N_COLS = 0
for _name, _n in COLS:
    COL[_name] = N_COLS
    N_COLS += _n

CONSTS = [("ident", 128), ("ones", 128), ("block_ones", 128), ("rotate", 128), ("window_mask", 384),
          ("stack_ident", 64), ("level_lo", 64), ("level_up", 6 * 64), ("strict_lo_neg", 64), ("incl_up_neg", 64),
          ("strict_up", 64), ("reset", T), ("pool_inv", 4 * T)]
CONST = {}
N_CONST = 0
for _name, _n in CONSTS:
    CONST[_name] = (N_CONST, _n)
    N_CONST += _n


def attn_tile_heads(j):
    return (j, 4 + j) if j < 4 else (4 + j, 8 + j)



class Steps:

    def __init__(self, eng, sem):
        self.eng, self.sem, self.n, self.turns = eng, sem, 0, 0

    def mark(self, ins):
        ins.then_inc(self.sem, 1)
        self.n += 1
        return ins

    def wait(self, back=0):
        self.eng.wait_ge(self.sem, self.n - back + self.turns)

    def start_loop(self, turn, per):
        self.n0, self.per, self.turns = self.n, per, per * turn

    def end_loop(self, count):
        assert self.n - self.n0 == self.per, (self.n - self.n0, self.per)
        self.n, self.turns = self.n0 + self.per * count, 0


class Carver:

    def __init__(self, tile, size):
        self.tile, self.size, self.at = tile, size, 0

    def cut(self, *dims):
        n = int(np.prod(dims))
        assert self.at + n <= self.size, (self.at + n, self.size)
        ap = self.tile[:, self.at:self.at + n]
        self.at += n
        names = "abcd"[:len(dims)]
        if len(dims) > 1:
            ap = ap.rearrange(f"p ({' '.join(names)}) -> p {' '.join(names)}", **dict(zip(names, dims)))
        return ap


def build(nc, dram, out_dram):
    with ExitStack() as ctx:
        def sb(name, shape, dt=F32):
            return ctx.enter_context(nc.sbuf_tensor(name, shape, dt))

        def sem(name):
            return ctx.enter_context(nc.semaphore(name))

        ring = sb("weight_ring", [P, RING, C, P])
        h = sb("h", [P, C, T])
        u = sb("u", [P, C, T])
        mix = sb("mix", [P, 2 * C, T])
        cols = sb("cols", [P, N_COLS])
        consts = sb("consts", [P, N_CONST])
        squares = sb("squares", [P, C, T])
        scaled = sb("scaled", [P, C, T])
        root = sb("root", [P, T])
        rstd = sb("rstd", [P, T])
        mods = sb("mods", [P, 144])
        cond = sb("cond", [P, 8])
        gain = sb("gain", [P, 8])
        half_gate = sb("half_gate", [P, 8])
        positions = sb("positions", [P, T], I32)
        AR = 20 * 1024 + 256
        arena = sb("arena", [P, AR])
        with nc.sbuf_tensor("gdn_tiles", [P, 10 * 1024], F32) as gdn_tiles:
            pass
        w_hi, w_lo = sb("weights_hi", [P, SPLIT, C, P], FR), sb("weights_lo", [P, SPLIT, C, P], FR)
        u_hi, u_lo = sb("u_hi", [P, C, T], FR), sb("u_lo", [P, C, T], FR)
        act_hi, act_lo = sb("act_hi", [P, 2, T], FR), sb("act_lo", [P, 2, T], FR)
        ps = ctx.enter_context(nc.psum_tensor("ps", [P, 8, 512], F32))
        gates_dram = nc.dram_tensor("gates_scratch", (2, GH, T), F32, kind="Internal").ap()

        def col(name, k=0):
            at = COL[name] + k
            return cols[:, bass.ds(at, 1)]

        def const(name, k=None, n=None):
            at, size = CONST[name]
            if k is not None:
                at, size = at + k * n, n
            return consts[:, at:at + size]

        ident, ones = const("ident"), const("ones")

        raw_ready = [sem(f"raw_ready{s}") for s in range(RING)]
        unit_done = [sem(f"unit_done{s}") for s in range(RING)]
        small_loaded = sem("small_loaded")
        cond_ready = sem("cond_ready")
        h_loaded, h_ready = sem("h_loaded"), sem("h_ready")
        sq_ready, ss_ready, root_ready = sem("sq_ready"), sem("ss_ready"), sem("root_ready")
        scaled_ready, u_ready = sem("scaled_ready"), sem("u_ready")
        dve_steps, act_steps = sem("dve_steps"), sem("act_steps")
        out_done, out_ready = sem("out_done"), sem("out_ready")
        mix_ready = sem("mix_ready")
        cv0_ready, cv_ready = sem("conv_tap_ready"), sem("conv_ready")
        sg_ready, act_ready = sem("silu_ready"), sem("act_ready")
        hi_ready, split_done = sem("hi_ready"), [sem(f"split_done{s}") for s in range(RING)]
        u_hi_ready, u_lo_ready = sem("u_hi_ready"), sem("u_lo_ready")
        act_hi_ready, act_lo_ready = sem("act_hi_ready"), sem("act_lo_ready")
        ada_loaded = [sem("ada_loaded0"), sem("ada_loaded1")]
        ada_summed, ada_cols, mods_ready = sem("ada_summed"), sem("ada_cols"), sem("mods_ready")
        pjsq_ready, pjss_ready, pjroot_ready = sem("pjsq_ready"), sem("pjss_ready"), sem("pjroot_ready")
        qn_ready, rot_ready, rope_ready = sem("qn_ready"), sem("rot_ready"), sem("rope_ready")
        angle_ready, sine_ready = sem("angle_ready"), sem("sine_ready")
        v_copied, sc_read = sem("v_copied"), sem("scores_read")
        sc_ready, max_ready, exp_ready, p_ready = sem("scores_ready"), sem("max_ready"), sem("exp_ready"), sem("probs_ready")
        pt_ready, ptc_ready, pv_ready = sem("pt_ready"), sem("pt_copied"), sem("pv_ready")

        MODS = {}
        for n, (l, s) in enumerate([(0, 0), (0, 1), (0, 2), (1, 0), (1, 1), (1, 2)]):
            MODS[4 + n] = (l, s)

        def mod_col(l, s, which):
            return 72 * l + (3 * s + which) * 8

        NORM_AT = {0: ("mixer_norm", 0), 2: ("mixer_norm", 8), 1: ("ffn_norm", 0), 3: ("ffn_norm", 8),
                   4: ("ffn_norm_2", 0), 5: ("mix_norm", 0), 6: ("ffn_norm_2", 8),
                   7: ("ffn_norm_2", 16), 8: ("mix_norm", 8), 9: ("ffn_norm_2", 24), 10: ("final_norm", 0)}

        def take_unit(pe, first, j, turn_units=0, turn=None):
            n = first + j
            need = 16 * (n // RING + 1)
            if turn is not None:
                assert turn_units % RING == 0
                need = need + 16 * (turn_units // RING) * turn
            pe.wait_ge(raw_ready[n % RING], need)
            return n % RING

        def unit_products(eng, first, j, turn_units=0, turn=None):
            n = first + j
            need = n // RING + 1
            if turn is not None:
                need = need + turn_units // RING * turn
            eng.wait_ge(unit_done[n % RING], need)

        def norm_bank(k):
            return 0 if k in (1, 6, 9) else 7

        def norm_act(act, k, q=None):
            for c in range(C):
                if k == 0:
                    act.wait_ge(h_loaded, 16)
                else:
                    act.wait_ge(h_ready, 8 * (k - 1) + c + 1)
                nc.scalar.activation(squares[:, c], h[:, c], ACT.Square).then_inc(sq_ready, 1)
            act.wait_ge(ss_ready, k + 1)
            nc.scalar.activation(root[:], ps[:, norm_bank(k), 0:T], ACT.Sqrt, bias=col("eps"), scale=1.0 / D).then_inc(root_ready, 1)
            if k in MODS:
                l, s = MODS[k]
                for c in range(C):
                    act.wait_ge(scaled_ready, 8 * (k - 4) + c + 1)
                    sh = mod_col(l, s, 0) + c
                    nc.scalar.activation(u[:, c], scaled[:, c], ACT.Identity, bias=mods[:, sh:sh + 1]).then_inc(u_ready, 1)
                    if q is not None and c:
                        split_u_act(act, q, c - 1)

        def norm_pe(pe, k):
            for c in range(C):
                pe.wait_ge(sq_ready, 8 * k + c + 1)
                last = nc.tensor.matmul(ps[:, norm_bank(k), 0:T], ones, squares[:, c], start=(c == 0), stop=(c == C - 1))
            last.then_inc(ss_ready, 1)

        def norm_dve(dve, steps, k, q=None):
            if k in MODS:
                l, s = MODS[k]
                name, at = NORM_AT[k]
                dve.wait_ge(h_ready, 8 * k)
                sc, ga = mod_col(l, s, 1), mod_col(l, s, 2)
                a = COL[name] + at
                steps.mark(nc.vector.scalar_tensor_tensor(gain[:], mods[:, sc:sc + 8], 1.0, cols[:, a:a + 8], ALU.add, ALU.mult))
                steps.mark(nc.vector.tensor_scalar(half_gate[:], mods[:, ga:ga + 8], 1.0 if s == 1 else 0.5, None, ALU.mult))
            dve.wait_ge(root_ready, k + 1)
            steps.mark(nc.vector.reciprocal(rstd[:], root[:]))
            steps.wait()
            for c in range(C):
                if k in MODS:
                    nc.vector.scalar_tensor_tensor(scaled[:, c], h[:, c], gain[:, c:c + 1], rstd[:], ALU.mult, ALU.mult).then_inc(scaled_ready, 1)
                    if q is not None and c >= 4:
                        split_u_dve(dve, q, c - 4, c - 3)
                else:
                    name, at = NORM_AT[k]
                    nc.vector.scalar_tensor_tensor(u[:, c], h[:, c], col(name, at + c), rstd[:], ALU.mult, ALU.mult).then_inc(
                        out_ready if k == 10 else u_ready, 1)

        def u_count(k, c):
            return 8 * k + c + 1

        def residual_dve(dve, steps, k, gated, banks, next_ffn=None):
            for c in range(C):
                if k == 2:
                    unit_products(dve, FIRST_UNIT["gdn_out"], C + (c | 1))
                if banks == "lin":
                    unit_products(dve, FIRST_UNIT[LIN[k]], c)
                    src = ps[:, c, 0:T]
                else:
                    src = ps[:, c // 2, (c % 2) * T:(c % 2 + 1) * T]
                g = half_gate[:, c:c + 1] if gated else 1.0
                nc.vector.scalar_tensor_tensor(h[:, c], src, g, h[:, c], ALU.mult, ALU.add).then_inc(h_ready, 1)
            if next_ffn is not None:
                split_lo(dve, nc.vector, next_ffn, 0)

        LIN = {0: "attn_out", 5: "conv_out", 8: "pm_out"}
        MIX_COUNT = {0: 4, 2: 8, 5: 12, 8: 18}

        def lin_pe(pe, k):
            pe.wait_ge(mix_ready, MIX_COUNT[k])
            for n in range(C):
                s = take_unit(pe, FIRST_UNIT[LIN[k]], n)
                for kk in range(C):
                    last = nc.tensor.matmul(ps[:, n, 0:T], ring[:, s, kk], mix[:, kk], start=(kk == 0), stop=(kk == C - 1))
                last.then_inc(unit_done[s], 1)

        ffn = Carver(arena, AR)
        ada_ring = ffn.cut(2, C, PIECE)
        ada_acc = ffn.cut(10, PIECE)
        cvb = ffn.cut(4, T)
        sgb = ffn.cut(4, T)
        actb = ffn.cut(4, T)
        FFN = [(1, FF1, 1, [(5, 2)]), (3, FF1, 1, [(5, 2)]), (4, FF2, 2, [(4, 2)]), (6, FF2, 2, [(4, 2)]),
               (7, FF2, 2, [(4, 0)]), (9, FF2, 2, [(4, 0)])]
        F_BASE = [0, FF1, 2 * FF1, 2 * FF1 + FF2, 2 * FF1 + 2 * FF2, 2 * FF1 + 3 * FF2, 2 * FF1 + 4 * FF2]
        PIECE_BASE = [0, 10, 20, 28, 36, 36, 36]
        CREDIT = 4

        def gate_at(f):
            return 3 * f - 1 if f else 0

        def up_at(f):
            return 3 * f if f else 1

        def down_at(q, f):
            return 3 * f + 4 if f < FFN[q][1] - 1 else 3 * f + 2

        def ffn_unit_done(eng, q, j, turn=None):
            unit_products(eng, FIRST_UNIT[f"ffn{q}"], j, 12, turn)

        def split_count(q, j):
            s = (FIRST_UNIT[f"ffn{q}"] + j) % RING
            return sum((FIRST_UNIT[f"ffn{p_}"] + i) % RING == s for p_ in range(q + 1)
                       for i in range(3 * FFN[p_][1] if p_ < q else j + 1))

        def split_wait(eng, q, j, turn=None):
            need = split_count(q, j)
            if turn is not None:
                need = need + 12 // RING * turn
            eng.wait_ge(split_done[(FIRST_UNIT[f"ffn{q}"] + j) % RING], need)
            return j % SPLIT

        def split_hi(act, q, j, turn=None):
            n = FIRST_UNIT[f"ffn{q}"] + j
            take_unit(act, FIRST_UNIT[f"ffn{q}"], j, 12, turn)
            if j >= SPLIT:
                ffn_unit_done(act, q, j - SPLIT, turn)
            elif q:
                ffn_unit_done(act, q - 1, 3 * FFN[q - 1][1] - SPLIT + j)
            nc.scalar.activation(w_hi[:, j % SPLIT], ring[:, n % RING], ACT.Copy).then_inc(hi_ready, 1)

        def split_lo(eng, vec, q, j, turn=None):
            n = FIRST_UNIT[f"ffn{q}"] + j
            need = 3 * F_BASE[q] + j + 1
            if turn is not None:
                need = need + 12 * turn
            eng.wait_ge(hi_ready, need)
            vec.tensor_tensor(w_lo[:, j % SPLIT], ring[:, n % RING], w_hi[:, j % SPLIT].bitcast(F32), ALU.subtract).then_inc(
                split_done[n % RING], 1)

        def split_first_act(act, q):
            for j in range(SPLIT):
                split_hi(act, q, j)

        def split_u_act(act, q, c):
            act.wait_ge(u_ready, u_count(FFN[q][0], c))
            nc.scalar.activation(u_hi[:, c], u[:, c], ACT.Copy).then_inc(u_hi_ready, 1)

        def split_u_dve(dve, q, first, end):
            for c in range(first, end):
                dve.wait_ge(u_hi_ready, 8 * q + c + 1)
                nc.vector.tensor_tensor(u_lo[:, c], u[:, c], u_hi[:, c].bitcast(F32), ALU.subtract).then_inc(u_lo_ready, 1)

        def split_product(out, hi, lo, x_hi, x_lo, start, stop):
            nc.tensor.matmul(out, hi, x_hi, start=start, stop=False, skip_group_check=True)
            nc.tensor.matmul(out, hi, x_lo, start=False, stop=False, skip_group_check=True)
            return nc.tensor.matmul(out, lo, x_hi, start=False, stop=stop, skip_group_check=True)

        def gate_up(pe, q, f, turn=None):
            need = F_BASE[q] + f - 3 + CREDIT
            if turn is not None:
                need = need + 4 * turn
            pe.wait_ge(act_ready, need)
            b = 4 + f % 4
            for half in range(2):
                j = up_at(f) if half else gate_at(f)
                s = split_wait(pe, q, j, turn)
                for k in range(C):
                    if f == 0 and half == 0:
                        pe.wait_ge(u_lo_ready, 8 * q + k + 1)
                    last = split_product(ps[:, b, half * T:(half + 1) * T], w_hi[:, s, k], w_lo[:, s, k], u_hi[:, k], u_lo[:, k],
                                         half == 0 and k == 0, k == C - 1)
                last.then_inc(unit_done[(FIRST_UNIT[f"ffn{q}"] + j) % RING], 1)

        def down(pe, q, f, start, turn=None):
            need = F_BASE[q] + f + 1
            if turn is not None:
                need = need + 4 * turn
            if start and q in (2, 4):
                pe.wait_ge(mods_ready, q)
            pe.wait_ge(act_lo_ready, need)
            j = down_at(q, f)
            s = split_wait(pe, q, j, turn)
            for c in range(C):
                last = split_product(ps[:, c // 2, (c % 2) * T:(c % 2 + 1) * T], w_hi[:, s, c], w_lo[:, s, c],
                                     act_hi[:, f % 2], act_lo[:, f % 2], start and c % 2 == 0, True)
            last.then_inc(unit_done[(FIRST_UNIT[f"ffn{q}"] + j) % RING], 1)

        def ffn_pe(pe, q):
            k, nf, kind, loops = FFN[q]
            gate_up(pe, q, 0)
            gate_up(pe, q, 1)
            down(pe, q, 0, True)
            f0 = 2
            for turns, _ in loops:
                with pe.Fori(0, turns) as i:
                    for j in range(4):
                        gate_up(pe, q, f0 + j, i)
                        down(pe, q, f0 + j - 1, False, i)
                f0 += 4 * turns
            for f in range(f0, nf):
                gate_up(pe, q, f)
                down(pe, q, f - 1, False)
            down(pe, q, nf - 1, False)

        def mods_pe(pe, q):
            n0, n1 = PIECE_BASE[q], PIECE_BASE[q + 1]
            pe.wait_ge(ada_summed, n1)
            for n in range(4 * (n1 - n0)):
                last = nc.tensor.matmul(ps[:, 3, n:n + 1], ada_acc[:, n // 4, (n % 4) * P:(n % 4 + 1) * P],
                                        ones[:, 0:1], start=True, stop=True)
            last.then_inc(ada_cols, 1)

        def mods_dve(dve, q):
            n0, n1 = PIECE_BASE[q], PIECE_BASE[q + 1]
            dve.wait_ge(ada_cols, q + 1)
            a = COL["ada_b"]
            nc.vector.tensor_tensor(mods[:, 4 * n0:4 * n1], ps[:, 3, 0:4 * (n1 - n0)],
                                    cols[:, a + 4 * n0:a + 4 * n1], ALU.add).then_inc(mods_ready, 1)
            dve.wait_ge(mods_ready, q + 1)

        def ffn_tile_act(act, q, f, turn=None):
            k, nf, kind, loops = FFN[q]
            n = F_BASE[q] + f + 1
            at = 0
            if turn is not None:
                n, at = n + 4 * turn, 16 * turn
            b, r = 4 + f % 4, f % 4
            ffn_unit_done(act, q, up_at(f), turn)
            if kind == 1:
                w = COL["ffn_conv"] + 4 * FF1 * q + 4 * f + at
                nc.scalar.activation(cvb[:, r], ps[:, b, 0:T], ACT.Identity, scale=cols[:, bass.ds(w + 2, 1)],
                                     bias=cols[:, bass.ds(w + 3, 1)]).then_inc(cv0_ready, 1)
                if f < nf - 1:
                    split_hi(act, q, 3 * f + 3, turn)
                act.wait_ge(cv_ready, n)
                nc.scalar.activation(sgb[:, r], cvb[:, r], ACT.Silu).then_inc(sg_ready, 1)
            else:
                nc.scalar.activation(sgb[:, r], ps[:, b, 0:T], ACT.Silu).then_inc(sg_ready, 1)
                if f < nf - 1:
                    split_hi(act, q, 3 * f + 3, turn)
            if f < nf - 1:
                split_hi(act, q, 3 * f + 4, turn)
            act.wait_ge(act_ready, n + CREDIT)
            nc.scalar.activation(act_hi[:, f % 2], actb[:, r], ACT.Copy).then_inc(act_hi_ready, 1)
            if f < nf - 1:
                split_hi(act, q, 3 * f + 5, turn)

        def ffn_tile_dve(dve, steps, q, f, turn=None, ada=None):
            k, nf, kind, loops = FFN[q]
            n = F_BASE[q] + f + 1
            at = 0
            if turn is not None:
                n, at = n + 4 * turn, 16 * turn
            b, r = 4 + f % 4, f % 4
            if kind == 1:
                w = COL["ffn_conv"] + 4 * FF1 * q + 4 * f + at
                dve.wait_ge(cv0_ready, n)
                steps.mark(nc.vector.scalar_tensor_tensor(cvb[:, r, 1:T], ps[:, b, 0:T - 1], cols[:, bass.ds(w + 1, 1)],
                                                          cvb[:, r, 1:T], ALU.mult, ALU.add))
                steps.wait()
                nc.vector.scalar_tensor_tensor(cvb[:, r, 2:T], ps[:, b, 0:T - 2], cols[:, bass.ds(w, 1)],
                                               cvb[:, r, 2:T], ALU.mult, ALU.add).then_inc(cv_ready, 1)
                if f < nf - 1:
                    split_lo(dve, nc.vector, q, 3 * f + 3, turn)
            dve.wait_ge(sg_ready, n)
            nc.vector.tensor_tensor(actb[:, r], sgb[:, r], ps[:, b, T:2 * T], ALU.mult).then_inc(act_ready, 1)
            if kind == 2 and f < nf - 1:
                split_lo(dve, nc.vector, q, 3 * f + 3, turn)
            if ada:
                ada()
            dve.wait_ge(act_hi_ready, n)
            nc.vector.tensor_tensor(act_lo[:, f % 2], actb[:, r], act_hi[:, f % 2].bitcast(F32), ALU.subtract).then_inc(act_lo_ready, 1)
            if f < nf - 1:
                split_lo(dve, nc.vector, q, 3 * f + 5, turn)

        def ada_dve(dve, steps, q, piece, part, turn, per):
            slot = piece % 2
            base = PIECE_BASE[q]
            acc = ada_acc[:, bass.ds(piece - base + per * turn, 1), :].rearrange("p a b -> p (a b)")
            if part == 0:
                dve.wait_ge(ada_loaded[slot], 16 * (piece // 2 + 1) + 16 * (per // 2) * turn)
            for kb in range(4 * part, 4 * part + 4):
                src = ada_ring[:, slot, kb]
                if kb == 0:
                    steps.mark(nc.vector.tensor_scalar(acc, src, cond[:, 0:1], None, ALU.mult))
                else:
                    steps.wait()
                    ins = nc.vector.scalar_tensor_tensor(acc, src, cond[:, kb:kb + 1], acc, ALU.mult, ALU.add)
                    if kb == C - 1:
                        ins.then_inc(ada_summed, 1)
                    else:
                        steps.mark(ins)

        def ffn_act(act, q):
            k, nf, kind, loops = FFN[q]
            for f in range(2):
                ffn_tile_act(act, q, f)
            f0 = 2
            for turns, _ in loops:
                with act.Fori(0, turns) as i:
                    for j in range(4):
                        ffn_tile_act(act, q, f0 + j, i)
                f0 += 4 * turns
            for f in range(f0, nf):
                ffn_tile_act(act, q, f)

        def ffn_dve(dve, steps, q, next_ffn=None):
            k, nf, kind, loops = FFN[q]
            for f in range(2):
                ffn_tile_dve(dve, steps, q, f)
            f0, piece = 2, PIECE_BASE[q]
            for turns, pieces in loops:
                with dve.Fori(0, turns) as i:
                    steps.start_loop(i, (4 if kind == 1 else 0) + 7 * pieces)
                    for j in range(4):
                        part = (lambda: ada_dve(dve, steps, q, piece + j // 2, j % 2, i, pieces)) if pieces else None
                        ffn_tile_dve(dve, steps, q, f0 + j, i, part)
                    steps.end_loop(turns)
                f0, piece = f0 + 4 * turns, piece + pieces * turns
            for f in range(f0, nf):
                ffn_tile_dve(dve, steps, q, f)
            unit_products(dve, FIRST_UNIT[f"ffn{q}"], 3 * nf - 1)
            residual_dve(dve, steps, k, kind == 2, "acc", next_ffn)

        def ffn_pool(pool, q):
            k, nf, kind, loops = FFN[q]
            piece = PIECE_BASE[q]
            has_ada = PIECE_BASE[q + 1] > piece
            for j in range(1, SPLIT):
                split_lo(pool, nc.gpsimd, q, j)

            def load(slot, n, need):
                if need is not None:
                    pool.wait_ge(ada_summed, need)
                pool.dma_start(ada_ring[:, slot], dram["ada"][n]).then_inc(ada_loaded[slot], 16)

            if has_ada:
                pool.wait_ge(h_ready, 8 * k)
                for s in range(2):
                    load(s, piece + s, piece + s - 1 if piece else None)
            for f in range(2):
                split_lo(pool, nc.gpsimd, q, 3 * f + 4)
            f0 = 2
            for turns, pieces in loops:
                with pool.Fori(0, turns - 1 if pieces else turns) as i:
                    for j in range(4):
                        split_lo(pool, nc.gpsimd, q, 3 * (f0 + j) + 4, i)
                        if pieces and j % 2:
                            load(j // 2, piece + j // 2 + 2 + 2 * i, piece + 2 * i + j // 2 + 1)
                f0 += 4 * turns
                if pieces:
                    for f in range(f0 - 4, f0):
                        split_lo(pool, nc.gpsimd, q, 3 * f + 4)
                piece += pieces * turns
            for f in range(f0, nf - 1):
                split_lo(pool, nc.gpsimd, q, 3 * f + 4)

        at_ = Carver(arena, AR)
        qk = at_.cut(10, T)
        vtok = at_.cut(2, 512)
        ax = Carver(gdn_tiles, 10 * 1024)
        sco2 = [ax.cut(4, 384) for _ in range(2)]
        prb2 = [ax.cut(4, 384) for _ in range(2)]
        prT = at_.cut(12, P)
        cosb, sinb = at_.cut(T), at_.cut(T)
        ang, turns_, resid, absr = at_.cut(T), at_.cut(T), at_.cut(T), at_.cut(T)
        reuse_at = at_.at
        pjr, pjs, pjroot, pjn = at_.cut(2, T), at_.cut(2, T), at_.cut(2, T), at_.cut(2, T)
        ropa, ropb = at_.cut(2, T), at_.cut(2, T)
        stats = [[at_.cut(4, 3)] + [at_.cut(4, 2) for _ in range(7)] for _ in range(2)]
        alibi = at_.cut(8, 384)

        TWO_PI = 2 * np.pi
        C1 = 6.28125
        C2 = float(np.round((TWO_PI - C1) * 2**20) / 2**20)
        C3 = float(TWO_PI - C1 - C2)
        PI_IN = float(np.nextafter(np.float32(np.pi), np.float32(0)))

        def angles_dve(dve, steps):
            dve.wait_ge(small_loaded, 16 * N_SMALL)
            m, w = steps.mark, steps.wait
            m(nc.vector.tensor_scalar(ang, positions[:], col("inv_freq"), None, ALU.mult))
            w()
            m(nc.vector.tensor_scalar(turns_, ang, 1.0 / TWO_PI, None, ALU.mult))
            w()
            m(nc.vector.tensor_scalar(turns_, turns_, MAGIC, None, ALU.add))
            w()
            m(nc.vector.tensor_scalar(turns_, turns_, -MAGIC, None, ALU.add))
            w()
            for c_ in (C1, C2, C3):
                m(nc.vector.scalar_tensor_tensor(ang, turns_, -c_, ang, ALU.mult, ALU.add))
                w()
            m(nc.vector.tensor_scalar(resid, ang, PI_IN, -PI_IN, ALU.min, ALU.max))
            w()
            m(nc.vector.tensor_scalar(absr, resid, -1.0, None, ALU.mult))
            w()
            nc.vector.tensor_tensor(absr, absr, resid, ALU.max).then_inc(angle_ready, 1)

        def angles_act(act):
            act.wait_ge(angle_ready, 1)
            nc.scalar.activation(sinb, resid, ACT.Sin)
            nc.scalar.activation(cosb, absr, ACT.Sin, scale=-1.0, bias=col("half_pi")).then_inc(sine_ready, 1)

        def attn_in_pe(pe):
            first = FIRST_UNIT["attn_in"]
            for t in range(12):
                if t < 10:
                    if t == 0:
                        for c in range(C):
                            pe.wait_ge(u_ready, u_count(0, c))
                    if t >= 2:
                        pe.wait_ge(pjsq_ready, t - 1)
                    s = take_unit(pe, first, t)
                    for k in range(C):
                        last = nc.tensor.matmul(ps[:, t % 2, 0:T], ring[:, s, k], u[:, k], start=(k == 0), stop=(k == C - 1))
                    last.then_inc(unit_done[s], 1)
                if 0 <= t - 1 < 10:
                    a = t - 1
                    pe.wait_ge(pjsq_ready, a + 1)
                    if a >= 2:
                        pe.wait_ge(pjroot_ready, a - 1)
                    nc.tensor.matmul(ps[:, 2 + a % 2, 0:T], const("block_ones"), pjs[:, a % 2], start=True, stop=True).then_inc(pjss_ready, 1)
                if 0 <= t - 2 < 10:
                    a = t - 2
                    pe.wait_ge(qn_ready, a + 1)
                    if a >= 2:
                        pe.wait_ge(rope_ready, a - 1)
                    nc.tensor.matmul(ps[:, 4 + a % 2, 0:T], const("rotate"), pjn[:, a % 2], start=True, stop=True).then_inc(rot_ready, 1)
            for n in range(2):
                s = take_unit(pe, first, 10 + n)
                for tb in range(2):
                    for k in range(C):
                        last = nc.tensor.matmul(ps[:, 6, tb * 256 + n * P:tb * 256 + (n + 1) * P], u[:, k, tb * P:(tb + 1) * P],
                                                ring[:, s, k], start=(n == 0 and tb == 0 and k == 0), stop=(k == C - 1),
                                                skip_group_check=True)
                last.then_inc(unit_done[s], 1)

        def attn_in_act(act):
            for t in range(11):
                if t < 10:
                    unit_products(act, FIRST_UNIT["attn_in"], t)
                    if t >= 2:
                        act.wait_ge(qn_ready, t - 1)
                    nc.scalar.activation(pjr[:, t % 2], ps[:, t % 2, 0:T], ACT.Copy)
                    nc.scalar.activation(pjs[:, t % 2], ps[:, t % 2, 0:T], ACT.Square).then_inc(pjsq_ready, 1)
                if t >= 1:
                    a = t - 1
                    act.wait_ge(pjss_ready, a + 1)
                    nc.scalar.activation(pjroot[:, a % 2], ps[:, 2 + a % 2, 0:T], ACT.Sqrt, bias=col("eps"), scale=1.0 / HD).then_inc(pjroot_ready, 1)
            for t in (10, 11):
                unit_products(act, FIRST_UNIT["attn_in"], t)
            nc.scalar.activation(vtok[:, :, 0:256], ps[:, 6, :].rearrange("p (a b) -> p a b", a=2), ACT.Copy).then_inc(v_copied, 1)

        def attn_in_dve(dve, steps):
            m, w = steps.mark, steps.wait
            dve.wait_ge(sine_ready, 1)
            for t in range(11):
                if t < 10:
                    r = t % 2
                    dve.wait_ge(pjroot_ready, t + 1)
                    m(nc.vector.reciprocal(pjroot[:, r], pjroot[:, r]))
                    if t >= 2:
                        dve.wait_ge(rot_ready, t - 1)
                    w()
                    nc.vector.scalar_tensor_tensor(pjn[:, r], pjr[:, r], col("k_gain" if t < 2 else "q_gain"), pjroot[:, r],
                                                   ALU.mult, ALU.mult).then_inc(qn_ready, 1)
                if t >= 1:
                    a, r = t - 1, (t - 1) % 2
                    dve.wait_ge(rot_ready, a + 1)
                    dve.wait_ge(qn_ready, a + 1)
                    m(nc.vector.tensor_tensor(ropa[:, r], pjn[:, r], cosb, ALU.mult))
                    m(nc.vector.tensor_tensor(ropb[:, r], ps[:, 4 + r, 0:T], sinb, ALU.mult))
                    w()
                    nc.vector.tensor_tensor(qk[:, a], ropa[:, r], ropb[:, r], ALU.add).then_inc(rope_ready, 1)

        BATCHES = [4, 2]

        def head_of(which, b, j):
            jt, half = 2 * b + j // 2, j % 2
            if which == 0:
                g = 2 * (jt // 4) + half
                return 2 + jt, half, jt // 4, 64 * g, jt
            return jt, half, 4 + jt, 64 * (2 * jt + half), 4 + jt

        def core_pe(pe, which):
            if which == 0:
                pe.wait_ge(rope_ready, 10)
            else:
                pe.wait_ge(qk1_ready, 8)
            base, count = 4 * which, BATCHES[which]

            def scores(b):
                if b:
                    pe.wait_ge(sc_read, base + b)
                for j in range(4):
                    qt, half, kt, vc, oc = head_of(which, b, j)
                    rows = slice(64 * half, 64 * half + 64)
                    nc.tensor.matmul(ps[:, j, 0:P], qk[rows, qt, 0:P], qk[rows, kt, 0:P], start=True, stop=True)
                    last = nc.tensor.matmul(ps[:, j, P:384], qk[rows, qt, P:T], qk[rows, kt, 0:T], start=True, stop=True)
                last.then_inc(sc_ready, 1)

            scores(0)
            scores(1)
            for b in range(count):
                n, prb = base + b, prb2[b % 2]
                pe.wait_ge(p_ready, n + 1)
                if b:
                    pe.wait_ge(ptc_ready, n)
                for j in range(4):
                    for t in range(3):
                        x = 3 * j + t
                        last = nc.tensor.transpose(ps[:, 4 + x // 4, (x % 4) * P:(x % 4 + 1) * P], prb[:, j, t * P:(t + 1) * P], ident)
                last.then_inc(pt_ready, 1)
                if b + 2 < count:
                    scores(b + 2)
                pe.wait_ge(ptc_ready, n + 1)
                pe.wait_ge(v_copied, which + 1)
                if b:
                    pe.wait_ge(mix_ready, CORE_MIX[which] + b)
                for j in range(4):
                    qt, half, kt, vc, oc = head_of(which, b, j)
                    at = (j // 2) * T
                    o = ps[64 * half:64 * half + 64, 7]
                    nc.tensor.matmul(o[:, at:at + P], vtok[:, 0, vc:vc + 64], prT[:, 3 * j], start=True, stop=True)
                    nc.tensor.matmul(o[:, at + P:at + T], vtok[:, 0, vc:vc + 64], prT[:, 3 * j + 1], start=True, stop=False)
                    last = nc.tensor.matmul(o[:, at + P:at + T], vtok[:, 1, vc:vc + 64], prT[:, 3 * j + 2], start=False, stop=True)
                last.then_inc(pv_ready, 1)

        CORE_MIX = [0, 16]

        def core_act(act, which):
            base, count = 4 * which, BATCHES[which]

            def exponents(b):
                n, sco, prb = base + b, sco2[b % 2], prb2[b % 2]
                mx, mm, nm, sd, sm, es, tot, rec = stats[b % 2]
                act.wait_ge(max_ready, n + 1)
                if b >= 2:
                    act.wait_ge(pt_ready, n - 1)
                for j in range(4):
                    nc.scalar.activation(prb[:, j, 0:P], sco[:, j, 0:P], ACT.Exp, bias=nm[:, j, 0:1], accum_out=sm[:, j, 0:1])
                    last = nc.scalar.activation(prb[:, j, P:384], sco[:, j, P:384], ACT.Exp, bias=nm[:, j, 1:2], accum_out=sm[:, j, 1:2])
                if which == 0:
                    last = nc.scalar.activation(es, sd, ACT.Exp)
                last.then_inc(exp_ready, 1)

            exponents(0)
            for b in range(count):
                n = base + b
                if b + 1 < count:
                    exponents(b + 1)
                act.wait_ge(pt_ready, n + 1)
                if b:
                    act.wait_ge(pv_ready, n)
                for x in range(3):
                    last = nc.scalar.activation(prT[:, 4 * x:4 * x + 4].rearrange("p a b -> p (a b)"), ps[:, 4 + x, :], ACT.Copy)
                last.then_inc(ptc_ready, 1)
                act.wait_ge(pv_ready, n + 1)
                oc = head_of(which, b, 0)[4]
                nc.scalar.activation(mix[:, oc:oc + 2].rearrange("p a b -> p (a b)"), ps[:, 7, :], ACT.Copy).then_inc(mix_ready, 1)

        def core_dve(dve, steps, which):
            m, w = steps.mark, steps.wait
            base, count = 4 * which, BATCHES[which]

            def maxima(b):
                n, sco = base + b, sco2[b % 2]
                mx, mm, nm, sd, sm, es, tot, rec = stats[b % 2]
                dve.wait_ge(sc_ready, n + 1)
                if b >= 2:
                    dve.wait_ge(exp_ready, n - 1)
                for j in range(4):
                    bias = const("window_mask") if which == 0 else alibi[:, 4 * b + j]
                    ins = nc.vector.scalar_tensor_tensor(sco[:, j], ps[:, j, 0:384], HD ** -0.5, bias, ALU.mult, ALU.add)
                    if j < 3:
                        m(ins)
                ins.then_inc(sc_read, 1)
                w()
                dve.wait_ge(sc_read, n + 1)
                m(nc.vector.tensor_reduce(mx.rearrange("p a b -> p (a b)"), sco.rearrange("p j (t k) -> p (j t) k", t=3), AX_X, ALU.max))
                w()
                m(nc.vector.tensor_copy(mm[:, :, 0], mx[:, :, 0]))
                m(nc.vector.tensor_tensor(mm[:, :, 1], mx[:, :, 1], mx[:, :, 2], ALU.max))
                w()
                if which == 0:
                    sk = cols[:, COL["sinks"] + 4 * b:COL["sinks"] + 4 * b + 4].unsqueeze(2).to_broadcast([P, 4, 2])
                    m(nc.vector.tensor_tensor(mm, mm, sk, ALU.max))
                    w()
                    m(nc.vector.tensor_tensor(sd, sk, mm, ALU.subtract))
                    w()
                nc.vector.tensor_scalar(nm, mm, -1.0, None, ALU.mult).then_inc(max_ready, 1)

            maxima(0)
            for b in range(count):
                n, prb = base + b, prb2[b % 2]
                mx, mm, nm, sd, sm, es, tot, rec = stats[b % 2]
                if b + 1 < count:
                    maxima(b + 1)
                dve.wait_ge(exp_ready, n + 1)
                if which == 0:
                    m(nc.vector.tensor_tensor(tot, sm, es, ALU.add))
                    w()
                    m(nc.vector.reciprocal(rec, tot))
                else:
                    m(nc.vector.reciprocal(rec, sm))
                w()
                for j in range(4):
                    m(nc.vector.tensor_scalar(prb[:, j, 0:P], prb[:, j, 0:P], rec[:, j, 0:1], None, ALU.mult))
                    ins = nc.vector.tensor_scalar(prb[:, j, P:384], prb[:, j, P:384], rec[:, j, 1:2], None, ALU.mult)
                    if j < 3:
                        m(ins)
                ins.then_inc(p_ready, 1)

        qk1_ready = sem("moba_qk_ready")

        g_gates, g_rows_out, g_rows, g_cols, g_colsx = (sem(n) for n in (
            "gates_ready", "gates_stored", "gate_rows_loaded", "gate_cols_ready", "gate_cols_exp"))
        g_soft, g_texp, g_tabs = sem("softplus_ready"), sem("table_arg_ready"), sem("tables_exp")
        g_tap, g_conv, g_silu, g_z = sem("g_tap"), sem("g_conv"), sem("g_silu"), sem("g_z")
        g_sq, g_ss, g_root, g_qkn = sem("g_squares"), sem("g_sums"), sem("g_root"), sem("g_qk_normed")
        g_vt, g_vb, g_kt, g_kk, g_ktok, g_kb = (sem(n) for n in (
            "g_v_turned", "g_v_scaled", "g_k_turned", "g_kk", "g_k_copied", "g_k_scaled"))
        g_egr_in, g_egr, g_mt, g_qkm, g_bt, g_x, g_p, g_pc, g_dx = (sem(n) for n in (
            "g_rows_loaded", "g_rows_exp", "g_mt", "g_qk_masked", "g_level_masked", "g_inverse", "g_bx", "g_bx_copied", "g_xbx"))
        g_uw, g_u, g_wt, g_qd, g_s = (sem(n) for n in ("g_uw", "g_u_copied", "g_w_copied", "g_q_decayed", "g_state"))
        pe_waited = sem("pe_waited")
        g_zc, g_ln = sem("g_z_copied"), sem("g_ln")
        qk_squared, qk_summed, qk_ln, qk_root = sem("g_qk_squared"), sem("g_qk_summed"), sem("g_qk_ln"), sem("g_qk_root")
        g_ws, g_vn, g_op, g_kv, g_o = (sem(n) for n in ("g_ws", "g_v_new", "g_out", "g_kv", "g_out_copied"))

        gd, gx = Carver(arena, AR), Carver(gdn_tiles, 10 * 1024)
        cbuf = squares[:]
        m_tab = scaled[:].rearrange("p a b -> p (a b)").rearrange("p (h t s) -> p h t s", h=GH, t=2)
        mt_tab, qk_tab = gd.cut(GH, 2, CH), gd.cut(GH, 2, CH)
        qkv, zs, egr = gd.cut(8, T), gd.cut(4, T), gd.cut(4, T)
        kb_at = gd.at
        kb, kd, vb = gd.cut(4, 2, P), gd.cut(4, 2, P), gd.cut(4, 2, P)
        m_, mt_, qk_ = gd.cut(4, 2, CH), gd.cut(4, 2, CH), gd.cut(4, 2, CH)
        bt, x_, xt_ = gd.cut(5, 8, CH), gd.cut(8, CH), gd.cut(8, CH)
        p1, vnew = gd.cut(8, CH), gd.cut(4, P)
        ktok, qd, state, ot = gd.cut(4, P), gd.cut(4, T), gd.cut(4, P), gd.cut(4, T)
        uu, wt = gx.cut(8, P), gx.cut(4, T)
        qkn, zs_now, gsq, grt = gx.cut(4, T), gx.cut(4, T), gx.cut(4, T), gx.cut(4, T)
        qk_sq, qk_rt = gx.cut(4, T), gx.cut(4, T)
        bcol, gcol, ecol, kbcol, nea = gd.cut(2, GH), gd.cut(2, GH), gd.cut(2, GH), gd.cut(2, GH), gd.cut(1)
        gates, xa, ta, tb_ = ot[:, 0], ot[:, 1], ot[:, 2], ot[:, 3]
        g_row = gdn_tiles[:, 0:2 * GH * CH].rearrange("p (h t s) -> p h t s", h=GH, t=2)
        b_row = arena[:, kb_at:kb_at + 2 * 4 * T].rearrange("p (h t s) -> p h t s", h=GH, t=2)
        N_TURNS = GH // GB

        def gdn_gates_pe(pe):
            first = FIRST_UNIT["gdn_gates"]
            for c in range(C):
                pe.wait_ge(u_ready, u_count(2, c))
            s = take_unit(pe, first, 0)
            for k in range(C):
                last = nc.tensor.matmul(ps[:, 4, 0:T], ring[:, s, k], u[:, k], start=(k == 0), stop=(k == C - 1))
            last.then_inc(unit_done[s], 1)
            for j in range(4):
                gdn_unit_pe(pe, j)
            pe.wait_ge(g_gates, 1)
            for t in range(2):
                last = nc.tensor.matmul(ps[:, 7, 64 * t:64 * t + 48], gates[0:48, t * P:(t + 1) * P], ident[0:48, 0:48],
                                        start=True, stop=True)
            last.then_inc(g_cols, 1)

        def gdn_gates_act(act, steps):
            m, w = steps.mark, steps.wait
            unit_products(act, FIRST_UNIT["gdn_gates"], 0)
            act.wait_ge(g_soft, 1)
            m(nc.scalar.activation(gates[0:16], ps[0:16, 4, 0:T], ACT.Sigmoid))
            a = slice(32, 48)
            m(nc.scalar.activation(xa[a], ps[a, 4, 0:T], ACT.Identity, bias=cols[a, COL["dt_bias"]:COL["dt_bias"] + 1]))
            w()
            m(nc.scalar.activation(ta[a], xa[a], ACT.Abs))
            w()
            m(nc.scalar.activation(ta[a], ta[a], ACT.Exp, scale=-1.0))
            m(nc.scalar.activation(nea[a], cols[a, COL["a_log"]:COL["a_log"] + 1], ACT.Exp))
            w()
            nc.scalar.activation(ta[a], ta[a], ACT.Ln, bias=cols[a, COL["one"]:COL["one"] + 1]).then_inc(g_soft, 1)
            act.wait_ge(g_colsx, 1)
            nc.scalar.activation(ecol, gcol, ACT.Exp).then_inc(g_colsx, 1)
            for j in range(8):
                gdn_tile_act(act, j)
            act.wait_ge(g_texp, 2)
            nc.scalar.activation(qk_tab, qk_tab, ACT.Exp).then_inc(g_tabs, 1)
            nc.scalar.activation(m_tab, m_tab, ACT.Exp).then_inc(g_tabs, 1)

        def gdn_gates_dve(dve, steps):
            m, w = steps.mark, steps.wait
            a = slice(32, 48)
            nc.vector.memset(gates[0:64], 0.0).then_inc(g_soft, 1)
            dve.wait_ge(g_soft, 2)
            m(nc.vector.tensor_scalar(tb_[a], xa[a], 0.0, None, ALU.max))
            m(nc.vector.tensor_scalar(nea[a], nea[a], -1.0, None, ALU.mult))
            w()
            m(nc.vector.tensor_tensor(tb_[a], tb_[a], ta[a], ALU.add))
            w()
            m(nc.vector.tensor_scalar(tb_[a], tb_[a], nea[a], None, ALU.mult))
            w()
            at, _ = CONST["reset"]
            nc.vector.tensor_tensor_scan(gates[a], consts[a, at:at + T], tb_[a], 0.0, ALU.mult, ALU.add).then_inc(g_gates, 1)
            dve.wait_ge(g_cols, 1)
            cols_ = ps[:, 7, 0:2 * 64].rearrange("p (t n) -> p t n", t=2)
            m(nc.vector.tensor_copy(bcol, cols_[:, :, 0:16]))
            nc.vector.tensor_copy(gcol, cols_[:, :, 32:48]).then_inc(g_colsx, 1)
            dve.wait_ge(g_colsx, 2)
            m(nc.vector.tensor_tensor(kbcol, bcol, ecol, ALU.mult))
            for j in range(8):
                gdn_tile_dve(dve, steps, j)
            dve.wait_ge(g_rows, 64)
            gc4 = gcol.rearrange("p t h -> p h t").unsqueeze(3).to_broadcast([P, GH, 2, CH])
            bc4 = bcol.rearrange("p t h -> p h t").unsqueeze(3).to_broadcast([P, GH, 2, CH])
            flat = lambda x: x.rearrange("p h t s -> p (h t) s")
            each = lambda name: const(name).unsqueeze(1).to_broadcast([P, GH * 2, CH])
            m(nc.vector.tensor_tensor(mt_tab, g_row, gc4, ALU.subtract))
            w()
            nc.vector.tensor_tensor(flat(qk_tab), flat(mt_tab), each("incl_up_neg"), ALU.add).then_inc(g_texp, 1)
            nc.vector.scalar_tensor_tensor(flat(m_tab), flat(mt_tab), -1.0, each("strict_lo_neg"), ALU.mult, ALU.add).then_inc(g_texp, 1)
            dve.wait_ge(g_tabs, 1)
            m(nc.vector.tensor_tensor(mt_tab, qk_tab, b_row, ALU.mult))
            w()
            m(nc.vector.tensor_tensor(flat(mt_tab), flat(mt_tab), each("strict_up"), ALU.mult))
            dve.wait_ge(g_tabs, 2)
            m(nc.vector.tensor_tensor(m_tab, m_tab, bc4, ALU.mult))
            w()

        def gdn_gates_pool(pool):
            pool.wait_ge(g_gates, 1)
            pool.dma_start(gates_dram[0], gates[0:16]).then_inc(g_rows_out, 16)
            pool.dma_start(gates_dram[1], gates[32:48]).then_inc(g_rows_out, 16)
            pool.wait_ge(g_rows_out, 32)
            for n, dst in ((0, b_row), (1, g_row)):
                for half in range(2):
                    src = gates_dram[n].rearrange("h (t f s) -> f h t s", t=2, f=2)[half].partition_broadcast(64)
                    pool.dma_start(dst[64 * half:64 * half + 64], src).then_inc(g_rows, 16)

        def gdn_turn_pool(pool, i):
            pool.wait_ge(g_z, 4 * i + 4)
            pool.wait_ge(mix_ready, 4 + i)
            gain_ = col("gdn_norm").unsqueeze(2).to_broadcast([P, 4, T])
            nc.gpsimd.tensor_tensor(zs_now, zs, gain_, ALU.mult).then_inc(g_zc, 1)
            pool.wait_ge(g_s, 5 * i + 1)
            pool.dma_start(egr, gates_dram[1][bass.ds(4 * i, 4), :].partition_broadcast(P)).then_inc(g_egr_in, 16)
            pool.wait_ge(g_mt, i + 1)
            for lv in range(1, 6):
                up = const("level_up", lv, CH).unsqueeze(1).to_broadcast([P, 8, CH])
                nc.gpsimd.tensor_tensor(bt[:, lv - 1], mt_.rearrange("p h t s -> p (h t) s"), up, ALU.mult).then_inc(g_bt, 1)

        def small_tiles(pe):
            pe.sem_inc(pe_waited, 1)

        def gdn_unit_pe(pe, j, i=None):
            first, ahead = FIRST_UNIT["gdn_in"], 0 if i is None else 1
            if j >= 4:
                pe.wait_ge(g_conv, 8 * ahead + j - 3 + (8 * i if ahead else 0))
            elif ahead:
                pe.wait_ge(g_z, 4 * i + j + 1)
            if j == 3 and not ahead:
                pe.wait_ge(mods_ready, 1)
            s = take_unit(pe, first + 12 * ahead, j, 12, i)
            for k in range(C):
                last = nc.tensor.matmul(ps[:, j % 4, 0:T], ring[:, s, k], u[:, k], start=(k == 0), stop=(k == C - 1))
            last.then_inc(unit_done[s], 1)

        def qk_sums_pe(pe, half, i, ahead):
            pe.wait_ge(qk_squared, i + ahead + 1)
            if half:
                pe.wait_ge(qk_ln, 2 * i + 2 * ahead + 1)
            nc.tensor.matmul(ps[:, 7], ones, qk_sq[:, 2 * half:2 * half + 2], start=True, stop=True).then_inc(qk_summed, 1)

        def qk_squares_act(act, i, ahead):
            act.wait_ge(g_silu, 8 * i + 8 * ahead + 4)
            nc.scalar.activation(qk_sq, qkv[:, 0:4], ACT.Square).then_inc(qk_squared, 1)

        def qk_root_act(act, half, i, ahead):
            act.wait_ge(qk_summed, 2 * i + 2 * ahead + half + 1)
            nc.scalar.activation(qk_rt[:, 2 * half:2 * half + 2].rearrange("p a b -> p (a b)"), ps[:, 7], ACT.Ln,
                                 bias=col("eps")).then_inc(qk_ln, 1)
            if half:
                act.wait_ge(qk_ln, 2 * i + 2 * ahead + 2)
                nc.scalar.activation(qk_rt, qk_rt, ACT.Exp, scale=-0.5).then_inc(qk_root, 1)

        def qk_norm_dve(dve, steps, i, ahead):
            dve.wait_ge(qk_root, i + ahead + 1)
            steps.mark(nc.vector.scalar_tensor_tensor(qkn[:, 0:2], qkv[:, 0:2], P ** -0.5, qk_rt[:, 0:2], ALU.mult, ALU.mult))
            steps.wait()
            nc.vector.tensor_tensor(qkn[:, 2:4], qkv[:, 2:4], qk_rt[:, 2:4], ALU.mult).then_inc(g_qkn, 1)

        def gdn_out_pe(pe, n, half):
            if half == 0:
                pe.wait_ge(mix_ready, MIX_COUNT[2] - 2)
                if n == 0:
                    pe.wait_ge(g_z, 4 * N_TURNS)
            s = take_unit(pe, FIRST_UNIT["gdn_out"], C * half + n)
            for kk in range(C):
                last = nc.tensor.matmul(ps[:, n // 2, (n % 2) * T:(n % 2 + 1) * T], ring[:, s, kk], mix[:, half * C + kk],
                                        start=(half == 0 and n % 2 == 0 and kk == 0), stop=(kk == C - 1), skip_group_check=True)
            last.then_inc(unit_done[s], 1)

        def gdn_turn_pe(pe, i, more):
            def projections(*tiles):
                for j in tiles:
                    if more:
                        gdn_unit_pe(pe, j, i)
                    elif j < C:
                        gdn_out_pe(pe, j, 0)

            pe.wait_ge(g_silu, 8 * i + 8)
            for n in range(4):
                for t in range(2):
                    x = 2 * n + t
                    last = nc.tensor.transpose(ps[:, 6 + x // 4, (x % 4) * P:(x % 4 + 1) * P], qkv[:, 4 + n, t * P:(t + 1) * P], ident)
            last.then_inc(g_vt, 1)
            pe.wait_ge(g_ln, i + 1)
            pe.wait_ge(g_qkn, i + 1)
            for n in range(2):
                for t in range(2):
                    last = nc.tensor.transpose(ps[:, 4, (2 * n + t) * P:(2 * n + t + 1) * P], qkn[:, 2 + n, t * P:(t + 1) * P], ident)
            last.then_inc(g_kt, 1)
            for q in range(2):
                for n in range(2):
                    for c in range(4):
                        tk = slice(c * CH, (c + 1) * CH)
                        at = 256 * q + 128 * n + 64 * (c // 2)
                        rhs = qkn[:, 2 + n, tk] if q == 0 else qkn[:, n, tk]
                        last = nc.tensor.matmul(ps[64 * (c % 2):64 * (c % 2) + 64, 5, at:at + 64], qkn[:, 2 + n, tk], rhs, start=True, stop=True)
            last.then_inc(g_kk, 1)
            projections(0, 1, 2)
            for lv in range(1, 6):
                pe.wait_ge(g_x, 6 * i + lv)
                pe.wait_ge(g_bt, 5 * i + lv)
                if lv == 1:
                    pe.wait_ge(g_ktok, i + 1)
                    pe.wait_ge(g_vb, i + 1)
                if lv >= 4 and more:
                    qk_sums_pe(pe, lv - 4, i, 1)
                small_tiles(pe)
                for n in range(8):
                    for f in range(2):
                        r = slice(64 * f, 64 * f + 64)
                        last = nc.tensor.matmul(ps[r, 4, 64 * n:64 * n + 64], bt[r, lv - 1, n], x_[r, n], start=True, stop=True)
                last.then_inc(g_p, 1)
                pe.wait_ge(g_pc, 5 * i + lv)
                small_tiles(pe)
                for which in range(2):
                    if which == 0 and lv == 5:
                        continue
                    for n in range(8):
                        for f in range(2):
                            r = slice(64 * f, 64 * f + 64)
                            o = ps[r, 5 + which, 64 * n:64 * n + 64]
                            if which == 0:
                                last = nc.tensor.matmul(o, xt_[r, n], p1[r, n], start=True, stop=True)
                            else:
                                last = nc.tensor.matmul(o, p1[r, n], xt_[r, n], start=True, stop=True)
                last.then_inc(g_dx, 1)
                projections(2 + lv)
            pe.wait_ge(g_x, 6 * i + 6)
            pe.wait_ge(g_vb, i + 1)
            pe.wait_ge(g_kb, i + 1)
            if more:
                pe.wait_ge(qk_ln, 2 * i + 4)
            small_tiles(pe)
            for n in range(8):
                for f in range(2):
                    r = slice(64 * f, 64 * f + 64)
                    nc.tensor.matmul(ps[r, 4 + n // 4, (n % 4) * P:(n % 4 + 1) * P], xt_[r, n], vb[r, n // 2, n % 2], start=True, stop=True)
                    last = nc.tensor.matmul(ps[:, 6 + f, 64 * n:64 * n + 64], kb[r, n // 2, n % 2], xt_[r, n], start=True, stop=True)
            last.then_inc(g_uw, 1)
            projections(8)
            pe.wait_ge(g_u, i + 1)
            pe.wait_ge(g_wt, i + 1)
            pe.wait_ge(g_qd, i + 1)
            for c in range(4):
                f, t = c % 2, c // 2
                r, tk = slice(64 * f, 64 * f + 64), slice(c * CH, (c + 1) * CH)
                pe.wait_ge(g_s, 5 * i + c + 1)
                for n in range(4):
                    last = nc.tensor.matmul(ps[r, 4, n * P:(n + 1) * P], wt[:, n, tk], state[:, n], start=True, stop=True)
                last.then_inc(g_ws, 1)
                if c:
                    pe.wait_ge(g_o, 4 * i + c)
                for n in range(4):
                    nc.tensor.matmul(ps[:, 5, n * CH:(n + 1) * CH], state[:, n], qd[:, n, tk], start=(n == 0), stop=False, skip_group_check=True)
                pe.wait_ge(g_vn, 4 * i + c + 1)
                for n in range(4):
                    last = nc.tensor.matmul(ps[:, 6, n * P:(n + 1) * P], kd[r, n, t], vnew[r, n], start=True, stop=True)
                last.then_inc(g_kv, 1)
                for n in range(4):
                    last = nc.tensor.matmul(ps[:, 5, n * CH:(n + 1) * CH], vnew[r, n], qk_[r, n, t], start=False, stop=True, skip_group_check=True)
                last.then_inc(g_op, 1)
                if c < 3:
                    projections(9 + c)
            pe.wait_ge(g_sq, i + 1)
            pe.wait_ge(g_s, 5 * i + 5)
            for n in range(2):
                last = nc.tensor.matmul(ps[:, 4 + n], ones, gsq[:, 2 * n:2 * n + 2], start=True, stop=True)
            last.then_inc(g_ss, 1)

        def gdn_tile_act(act, j, i=None):
            first, ahead = FIRST_UNIT["gdn_in"], 0 if i is None else 1
            turns = 0 if i is None else i
            wc = COL["gdn_conv"] + 32 * ahead
            unit_products(act, first + 12 * ahead, j, 12, i)
            if j < 8:
                nc.scalar.activation(cbuf[:, j], ps[:, j % 4, 0:T], ACT.Identity,
                                     scale=cols[:, bass.ds(wc + 4 * j + 3 + 32 * turns, 1)]).then_inc(g_tap, 1)
            if 1 <= j <= 8:
                act.wait_ge(g_conv, 8 * (turns + ahead) + j)
                if ahead and j == 1:
                    act.wait_ge(g_qkn, turns + 1)
                nc.scalar.activation(qkv[:, j - 1], cbuf[:, j - 1], ACT.Silu).then_inc(g_silu, 1)
            if j >= 8:
                if ahead and j == 8:
                    act.wait_ge(g_zc, turns + 1)
                nc.scalar.activation(zs[:, j - 8], ps[:, j % 4, 0:T], ACT.Silu).then_inc(g_z, 1)

        def gdn_turn_act(act, steps, i, more):
            def projections(*tiles):
                if more:
                    for j in tiles:
                        gdn_tile_act(act, j, i)

            act.wait_ge(g_vt, i + 1)
            for n in range(4):
                for t in range(2):
                    x = 2 * n + t
                    last = nc.scalar.activation(vb[:, n, t], ps[:, 6 + x // 4, (x % 4) * P:(x % 4 + 1) * P], ACT.Copy,
                                                scale=bcol[:, t, bass.ds(4 * i + n, 1)])
            last.then_inc(g_vb, 1)
            act.wait_ge(g_egr_in, 16 * i + 16)
            nc.scalar.activation(egr, egr, ACT.Exp).then_inc(g_egr, 1)
            act.wait_ge(g_kt, i + 1)
            nc.scalar.activation(ktok.rearrange("p a b -> p (a b)"), ps[:, 4], ACT.Copy).then_inc(g_ktok, 1)
            act.wait_ge(g_ktok, i + 1)
            for n in range(4):
                for t in range(2):
                    last = nc.scalar.activation(kb[:, n, t], ktok[:, 2 * (n // 2) + t], ACT.Copy, scale=kbcol[:, t, bass.ds(4 * i + n, 1)])
            last.then_inc(g_kb, 1)
            projections(0, 1, 2)
            for lv in range(1, 6):
                act.wait_ge(g_p, 5 * i + lv)
                nc.scalar.activation(p1.rearrange("p a b -> p (a b)"), ps[:, 4], ACT.Copy).then_inc(g_pc, 1)
                if lv == 3 and more:
                    qk_squares_act(act, i, 1)
                if lv >= 4 and more:
                    qk_root_act(act, lv - 4, i, 1)
                projections(2 + lv)
            act.wait_ge(g_uw, i + 1)
            nc.scalar.activation(uu.rearrange("p a b -> p (a b)"), ps[:, 4:6].rearrange("p a b -> p (a b)"), ACT.Copy).then_inc(g_u, 1)
            projections(8)
            for c in range(4):
                act.wait_ge(g_op, 4 * i + c + 1)
                nc.scalar.activation(ot[:, :, c * CH:(c + 1) * CH], ps[:, 5, 0:256].rearrange("p (a b) -> p a b", a=4), ACT.Copy).then_inc(g_o, 1)
                if c < 3:
                    projections(9 + c)
            act.wait_ge(g_o, 4 * i + 4)
            nc.scalar.activation(gsq, ot, ACT.Square).then_inc(g_sq, 1)
            act.wait_ge(g_ss, i + 1)
            nc.scalar.activation(grt.rearrange("p a b -> p (a b)"), ps[:, 4:6].rearrange("p a b -> p (a b)"), ACT.Ln, bias=col("eps"),
                                 scale=1.0 / P).then_inc(g_ln, 1)
            act.wait_ge(g_ln, i + 2)
            nc.scalar.activation(grt, grt, ACT.Exp, scale=-0.5).then_inc(g_root, 1)

        def gdn_tile_dve(dve, steps, j, i=None):
            ahead, turns = 0 if i is None else 1, 0 if i is None else i
            wc = COL["gdn_conv"] + 32 * ahead
            dve.wait_ge(g_tap, 8 * (turns + ahead) + j + 1)
            for tap in range(3):
                d = 3 - tap
                ins = nc.vector.scalar_tensor_tensor(cbuf[:, j, d:T], ps[:, j % 4, 0:T - d],
                                                     cols[:, bass.ds(wc + 4 * j + tap + 32 * turns, 1)], cbuf[:, j, d:T], ALU.mult, ALU.add)
                if tap < 2:
                    steps.mark(ins)
                    steps.wait()
                else:
                    ins.then_inc(g_conv, 1)

        def gdn_turn_dve(dve, steps, i, more):
            m, w = steps.mark, steps.wait

            def projections(*tiles):
                if more:
                    for j in tiles:
                        gdn_tile_dve(dve, steps, j, i)

            nc.vector.memset(state, 0.0).then_inc(g_s, 1)
            dve.wait_ge(g_kk, i + 1)
            for q, (dst, tab) in enumerate(((m_, m_tab), (mt_, mt_tab), (qk_, qk_tab))):
                for n in range(2):
                    at = 128 * n + (256 if q == 2 else 0)
                    kk = ps[:, 5, at:at + 128].unsqueeze(1).to_broadcast([P, 2, 128])
                    ins = nc.vector.tensor_tensor(dst[:, 2 * n:2 * n + 2].rearrange("p a b c -> p a (b c)"), kk,
                                                  tab[:, bass.ds(4 * i + 2 * n, 2)].rearrange("p a b c -> p a (b c)"), ALU.mult)
                    if q == 1 and n == 1:
                        ins.then_inc(g_mt, 1)
                    elif q == 2 and n == 1:
                        ins.then_inc(g_qkm, 1)
                    else:
                        m(ins)
            w()
            dve.wait_ge(g_mt, i + 1)
            eye = const("stack_ident").unsqueeze(1).to_broadcast([P, 8, CH])
            lo = const("level_lo").unsqueeze(1).to_broadcast([P, 8, CH])
            up = const("level_up", 0, CH).unsqueeze(1).to_broadcast([P, 8, CH])
            m(nc.vector.tensor_tensor(x_, m_.rearrange("p a b c -> p (a b) c"), lo, ALU.mult))
            m(nc.vector.tensor_tensor(xt_, mt_.rearrange("p a b c -> p (a b) c"), up, ALU.mult))
            w()
            m(nc.vector.tensor_tensor(x_, eye, x_, ALU.subtract))
            nc.vector.tensor_tensor(xt_, eye, xt_, ALU.subtract).then_inc(g_x, 1)
            dve.wait_ge(g_ktok, i + 1)
            for n in range(4):
                for t in range(2):
                    dcol = qk_tab[:, bass.ds(4 * i + n, 1), t, CH - 1]
                    ins = nc.vector.tensor_scalar(kd[:, n, t], ktok[:, 2 * (n // 2) + t], dcol, None, ALU.mult)
                    m(ins)
            dve.wait_ge(g_egr, i + 1)
            for n in range(2):
                ins = nc.vector.tensor_tensor(qd[:, 2 * n:2 * n + 2], qkn[:, n].unsqueeze(1).to_broadcast([P, 2, T]), egr[:, 2 * n:2 * n + 2], ALU.mult)
                if n == 0:
                    m(ins)
                else:
                    ins.then_inc(g_qd, 1)
            projections(0, 1, 2)
            for lv in range(1, 6):
                dve.wait_ge(g_dx, 5 * i + lv)
                flat = lambda x: x.rearrange("p a b -> p (a b)")
                if lv < 5:
                    m(nc.vector.tensor_tensor(flat(x_), flat(x_), ps[:, 5], ALU.subtract))
                nc.vector.tensor_tensor(flat(xt_), flat(xt_), ps[:, 6], ALU.subtract).then_inc(g_x, 1)
                projections(2 + lv)
            if more:
                qk_norm_dve(dve, steps, i, 1)
            dve.wait_ge(g_uw, i + 1)
            nc.vector.tensor_copy(wt.rearrange("p h (t f s) -> p (h t) f s", t=2, f=2),
                                  ps[:, 6:8].rearrange("p f (n s) -> p n f s", n=8)).then_inc(g_wt, 1)
            dve.wait_ge(g_u, i + 1)
            for c in range(4):
                f, t = c % 2, c // 2
                r = slice(64 * f, 64 * f + 64)
                dve.wait_ge(g_ws, 4 * i + c + 1)
                ut = uu[r].rearrange("p (a b) c -> p a b c", b=2)[:, :, t]
                nc.vector.tensor_tensor(vnew[r], ut, ps[r, 4].rearrange("p (a b) -> p a b", a=4), ALU.subtract).then_inc(g_vn, 1)
                dve.wait_ge(g_kv, 4 * i + c + 1)
                for n in range(4):
                    ins = nc.vector.scalar_tensor_tensor(state[:, n], state[:, n], egr[:, n, c * CH + CH - 1:c * CH + CH],
                                                         ps[:, 6, n * P:(n + 1) * P], ALU.mult, ALU.add)
                    if n < 3:
                        m(ins)
                ins.then_inc(g_s, 1)
            dve.wait_ge(g_root, i + 1)
            m(nc.vector.tensor_tensor(ot, ot, grt, ALU.mult))
            w()
            dve.wait_ge(g_zc, i + 1)
            nc.vector.tensor_tensor(mix[:, bass.ds(4 * i, 4)], ot, zs_now, ALU.mult).then_inc(mix_ready, 1)

        def gdn_pe(pe):
            gdn_gates_pe(pe)
            for j in range(4, 12):
                gdn_unit_pe(pe, j)
            pe.wait_ge(g_colsx, 1)
            for half in range(2):
                qk_sums_pe(pe, half, 0, 0)
            pe.wait_ge(qk_ln, 2)
            with pe.Fori(0, N_TURNS - 1) as i:
                gdn_turn_pe(pe, i, True)
            gdn_turn_pe(pe, N_TURNS - 1, False)
            pe.wait_ge(mix_ready, MIX_COUNT[2])
            for n in range(C):
                gdn_out_pe(pe, n, 1)

        def gdn_act(act, steps):
            gdn_gates_act(act, steps)
            for j in range(8, 12):
                gdn_tile_act(act, j)
            qk_squares_act(act, 0, 0)
            for half in range(2):
                qk_root_act(act, half, 0, 0)
            with act.Fori(0, N_TURNS - 1) as i:
                gdn_turn_act(act, steps, i, True)
            gdn_turn_act(act, steps, N_TURNS - 1, False)

        def gdn_dve(dve, steps):
            gdn_gates_dve(dve, steps)
            nc.vector.memset(nea[0:1], 0.0).then_inc(g_ln, 1)
            qk_norm_dve(dve, steps, 0, 0)
            with dve.Fori(0, N_TURNS - 1) as i:
                steps.start_loop(i, 16 + 1 + 4 + 3 + 8 + 1 + 4 + 12 + 1)
                gdn_turn_dve(dve, steps, i, True)
                steps.end_loop(N_TURNS - 1)
            gdn_turn_dve(dve, steps, N_TURNS - 1, False)

        def gdn_pool(pool):
            gdn_gates_pool(pool)
            with pool.Fori(0, N_TURNS) as i:
                gdn_turn_pool(pool, i)

        cm = Carver(arena, AR)
        PAD_A = TAPS_A - 1
        a_pad, a_acc, a_x, a_sq, a_rt = cm.cut(4, PAD_A + T), cm.cut(4, T), cm.cut(4, T), cm.cut(4, T), cm.cut(4, T)
        b_pad, b_acc, gate_t, cg_t = cm.cut(4, 2 + T), cm.cut(4, T), cm.cut(4, T), cm.cut(4, T)
        a_sig, b_cg, a_prod = sem("a_sigmoid"), sem("b_c_gate"), sem("a_product")
        b_done, a_conv, a_biased, a_mean = sem("b_done"), sem("a_convolved"), sem("a_biased"), sem("a_mean")
        a_ln = sem("a_ln")
        a_centred, a_sqd, a_var, a_root, a_norm = (sem(n) for n in ("a_centred", "a_squared", "a_var", "a_root", "a_normed"))

        def conv_pe(pe):
            first = FIRST_UNIT["conv_in"]
            for c in range(C):
                pe.wait_ge(u_ready, u_count(5, c))
            for n in range(20):
                b = n % 8
                if n >= 16:
                    pe.wait_ge(b_done, (n - 16) // 3 + 1)
                elif n >= 8:
                    pe.wait_ge(a_prod, (n - 8) // 2 + 1)
                elif n == 3:
                    pe.wait_ge(mods_ready, 3)
                s = take_unit(pe, first, n)
                for k in range(C):
                    last = nc.tensor.matmul(ps[:, b, 0:T], ring[:, s, k], u[:, k], start=(k == 0), stop=(k == C - 1))
                last.then_inc(unit_done[s], 1)
            flat = lambda x, n: x[:, 2 * n:2 * n + 2].rearrange("p a b -> p (a b)")
            pe.wait_ge(a_biased, 1)
            pe.wait_ge(b_done, 4)
            for n in range(2):
                last = nc.tensor.matmul(ps[:, n], const("block_ones"), flat(a_x, n), start=True, stop=True)
            last.then_inc(a_mean, 1)
            pe.wait_ge(a_sqd, 1)
            for n in range(2):
                last = nc.tensor.matmul(ps[:, 2 + n], const("block_ones"), flat(a_sq, n), start=True, stop=True)
            last.then_inc(a_var, 1)

        def conv_act(act):
            first = FIRST_UNIT["conv_in"]
            for j in range(4):
                unit_products(act, first, 2 * j + 1)
                nc.scalar.activation(gate_t[:, j], ps[:, 2 * j + 1, 0:T], ACT.Sigmoid).then_inc(a_sig, 1)
            for j in range(4):
                unit_products(act, first, 8 + 3 * j)
                nc.scalar.activation(cg_t[:, j], ps[:, (8 + 3 * j) % 8, 0:T], ACT.Copy).then_inc(b_cg, 1)
            act.wait_ge(a_conv, 1)
            for j in range(4):
                last = nc.scalar.activation(a_x[:, j], a_acc[:, j], ACT.Identity, bias=col("conv_a_b", j))
            last.then_inc(a_biased, 1)
            act.wait_ge(a_centred, 1)
            nc.scalar.activation(a_sq, a_x, ACT.Square).then_inc(a_sqd, 1)
            act.wait_ge(a_var, 1)
            nc.scalar.activation(a_rt.rearrange("p a b -> p (a b)"), ps[:, 2:4].rearrange("p a b -> p (a b)"), ACT.Ln, bias=col("eps"),
                                 scale=1.0 / 64).then_inc(a_ln, 1)
            act.wait_ge(a_ln, 1)
            nc.scalar.activation(a_rt, a_rt, ACT.Exp, scale=-0.5).then_inc(a_root, 1)
            act.wait_ge(a_norm, 1)
            for j in range(4):
                nc.scalar.activation(mix[:, j], a_x[:, j], ACT.Silu, bias=col("ln_b", j)).then_inc(mix_ready, 1)

        def conv_dve(dve, steps):
            m, w = steps.mark, steps.wait
            first = FIRST_UNIT["conv_in"]
            m(nc.vector.memset(a_pad, 0.0))
            m(nc.vector.memset(b_pad, 0.0))
            w()
            wa = COL["conv_a_w"]

            def a_product(j):
                dve.wait_ge(a_sig, j + 1)
                nc.vector.tensor_tensor(a_pad[:, j, PAD_A:PAD_A + T], ps[:, 2 * j, 0:T], gate_t[:, j], ALU.mult).then_inc(a_prod, 1)

            def a_taps(tiles, first_tap, turns):
                with dve.Fori(0, turns) as i:
                    steps.start_loop(i, 6)
                    for q in range(3):
                        for j in tiles:
                            steps.wait(1)
                            m(nc.vector.scalar_tensor_tensor(a_acc[:, j], a_pad[:, j, bass.ds(first_tap + q + 3 * i, T)],
                                                             cols[:, bass.ds(wa + 4 * (first_tap + q) + j + 12 * i, 1)], a_acc[:, j], ALU.mult, ALU.add))
                    steps.end_loop(turns)

            def a_first_tap(tiles):
                for j in tiles:
                    dve.wait_ge(a_prod, j + 1)
                    m(nc.vector.tensor_scalar(a_acc[:, j], a_pad[:, j, 0:T], col("conv_a_w", j), None, ALU.mult))

            a_product(0)
            a_product(1)
            a_first_tap((0, 1))
            a_taps((0, 1), 1, 4)
            a_product(2)
            a_product(3)
            a_taps((0, 1), 13, 6)
            a_first_tap((2, 3))
            tap = 1
            for j in range(4):
                turns = (2, 3, 3, 2)[j]
                a_taps((2, 3), tap, turns)
                tap += 3 * turns
                n = 8 + 3 * j
                dve.wait_ge(b_cg, j + 1)
                unit_products(dve, first, n + 1)
                unit_products(dve, first, n + 2)
                m(nc.vector.tensor_tensor(b_pad[:, j, 2:2 + T], ps[:, (n + 1) % 8, 0:T], cg_t[:, j], ALU.mult))
                w()
                m(nc.vector.tensor_scalar(b_acc[:, j], b_pad[:, j, 0:T], col("conv_b_w", 3 * j), None, ALU.mult))
                for q in (1, 2):
                    w()
                    m(nc.vector.scalar_tensor_tensor(b_acc[:, j], b_pad[:, j, q:q + T], col("conv_b_w", 3 * j + q), b_acc[:, j], ALU.mult, ALU.add))
                w()
                m(nc.vector.tensor_tensor(mix[:, 4 + j], b_acc[:, j], ps[:, (n + 2) % 8, 0:T], ALU.mult))
                w()
                nc.vector.tensor_copy(b_acc[:, j, 0:1], b_acc[:, j, 1:2]).then_inc(b_done, 1)
                if j == 3:
                    nc.vector.tensor_copy(a_rt[:, 0, 0:1], a_acc[:, 3, T - 1:T]).then_inc(a_conv, 1)
            dve.wait_ge(a_mean, 1)
            flat2 = lambda x: x.rearrange("p a b -> p (a b)")
            nc.vector.scalar_tensor_tensor(flat2(a_x), flat2(ps[:, 0:2]), -1.0 / 64, flat2(a_x), ALU.mult, ALU.add).then_inc(a_centred, 1)
            dve.wait_ge(a_root, 1)
            for j in range(4):
                ins = nc.vector.scalar_tensor_tensor(a_x[:, j], a_x[:, j], col("ln_g", j), a_rt[:, j], ALU.mult, ALU.mult)
            ins.then_inc(a_norm, 1)

        PADP = 16
        px, pb1 = at_.cut(4, PADP + T), at_.cut(4, PADP + T)
        at_.at, end = reuse_at, at_.at
        pb2 = at_.cut(4, PADP + T)
        at_.at = end
        pooled = at_.cut(4, T)
        pool_w = at_.cut(4, P)
        moba_loaded, p_copied, p_pooled, p_mixed = sem("moba_loaded"), sem("p_copied"), sem("p_pooled"), sem("p_mixed")

        def moba_pe(pe):
            first = FIRST_UNIT["pm_in"]
            for c in range(C):
                pe.wait_ge(u_ready, u_count(8, c))
            for n in range(12):
                if n >= 8:
                    pe.wait_ge(p_copied, n - 7)
                s = take_unit(pe, first, n)
                for k in range(C):
                    last = nc.tensor.matmul(ps[:, n % 8, 0:T], ring[:, s, k], u[:, k], start=(k == 0), stop=(k == C - 1))
                last.then_inc(unit_done[s], 1)
            pe.wait_ge(qk1_ready, 4)
            for n in range(4):
                s = take_unit(pe, first, 12 + n)
                for tb in range(2):
                    for k in range(C):
                        last = nc.tensor.matmul(ps[:, 4 + tb, n * P:(n + 1) * P], u[:, k, tb * P:(tb + 1) * P], ring[:, s, k],
                                                start=(n == 0 and k == 0), stop=(k == C - 1), skip_group_check=True)
                last.then_inc(unit_done[s], 1)
            pe.wait_ge(p_pooled, 1)
            pe.wait_ge(moba_loaded, 32)
            for g in range(4):
                last = nc.tensor.matmul(ps[:, 6 + g // 2, (g % 2) * T:(g % 2 + 1) * T], pool_w[:, g], pooled[:, g], start=True, stop=True)
            last.then_inc(p_mixed, 1)
            pe.wait_ge(mix_ready, 16)

        def moba_act(act):
            first = FIRST_UNIT["pm_in"]
            for n in range(12):
                unit_products(act, first, n)
                if n < 4:
                    nc.scalar.activation(px[:, n, PADP:PADP + T], ps[:, n, 0:T], ACT.Copy).then_inc(p_copied, 1)
                else:
                    nc.scalar.activation(qk[:, n - 4], ps[:, n % 8, 0:T], ACT.Copy).then_inc(qk1_ready, 1)
            for n in range(4):
                unit_products(act, first, 12 + n)
            nc.scalar.activation(vtok, ps[:, 4:6], ACT.Copy).then_inc(v_copied, 1)

        def moba_dve(dve, steps):
            m, w = steps.mark, steps.wait
            for b in (px, pb1, pb2):
                m(nc.vector.memset(b[:, :, 0:PADP], 0.0))
            w()
            dve.wait_ge(p_copied, 4)
            src = px
            for lv in range(4):
                dst, d = (pb1, pb2)[lv % 2], 1 << lv
                m(nc.vector.tensor_tensor(dst[:, lv:, PADP:], src[:, lv:, PADP:], src[:, lv:, PADP - d:PADP + T - d], ALU.add))
                w()
                src = dst
            inv = const("pool_inv").rearrange("p (g t) -> p g t", g=4)
            for g in range(4):
                m(nc.vector.tensor_tensor(pooled[:, g], (pb1, pb2)[g % 2][:, g, PADP:], inv[:, g], ALU.mult))
            w()
            nc.vector.tensor_tensor(pooled, pooled, px[:, :, PADP:], ALU.subtract).then_inc(p_pooled, 1)
            dve.wait_ge(p_mixed, 1)
            for g in range(4):
                nc.vector.tensor_scalar(mix[:, g], ps[:, 6 + g // 2, (g % 2) * T:(g % 2 + 1) * T], col("pool_b", g), col("pool_scale", g),
                                        ALU.add, ALU.mult).then_inc(mix_ready, 1)
            dve.wait_ge(moba_loaded, 32)

        def moba_pool(pool):
            pool.wait_ge(h_ready, 8 * 8)
            pool.dma_start(alibi, dram["alibi"]).then_inc(moba_loaded, 16)
            pool.dma_start(pool_w, dram["pool_w"]).then_inc(moba_loaded, 16)


        def pe_program(pe):
            pe.wait_ge(small_loaded, 16 * N_SMALL)
            norm_pe(pe, 0)
            attn_in_pe(pe)
            core_pe(pe, 0)
            lin_pe(pe, 0)
            norm_pe(pe, 1)
            ffn_pe(pe, 0)
            norm_pe(pe, 2)
            mods_pe(pe, 0)
            gdn_pe(pe)
            norm_pe(pe, 3)
            ffn_pe(pe, 1)
            norm_pe(pe, 4)
            mods_pe(pe, 1)
            ffn_pe(pe, 2)
            norm_pe(pe, 5)
            mods_pe(pe, 2)
            conv_pe(pe)
            lin_pe(pe, 5)
            norm_pe(pe, 6)
            ffn_pe(pe, 3)
            norm_pe(pe, 7)
            mods_pe(pe, 3)
            ffn_pe(pe, 4)
            norm_pe(pe, 8)
            moba_pe(pe)
            core_pe(pe, 1)
            lin_pe(pe, 8)
            norm_pe(pe, 9)
            ffn_pe(pe, 5)
            norm_pe(pe, 10)

        def act_program(act):
            steps = Steps(act, act_steps)
            act.wait_ge(small_loaded, 16 * N_SMALL)
            nc.scalar.activation(cond[:], cols[:, COL["cond"]:COL["cond"] + 8], ACT.Silu).then_inc(cond_ready, 1)
            norm_act(act, 0)
            angles_act(act)
            attn_in_act(act)
            core_act(act, 0)
            split_first_act(act, 0)
            norm_act(act, 1)
            for c in range(C):
                split_u_act(act, 0, c)
            ffn_act(act, 0)
            norm_act(act, 2)
            gdn_act(act, steps)
            split_first_act(act, 1)
            norm_act(act, 3)
            for c in range(C):
                split_u_act(act, 1, c)
            ffn_act(act, 1)
            split_first_act(act, 2)
            norm_act(act, 4, 2)
            split_u_act(act, 2, C - 1)
            ffn_act(act, 2)
            norm_act(act, 5)
            conv_act(act)
            split_first_act(act, 3)
            norm_act(act, 6, 3)
            split_u_act(act, 3, C - 1)
            ffn_act(act, 3)
            split_first_act(act, 4)
            norm_act(act, 7, 4)
            split_u_act(act, 4, C - 1)
            ffn_act(act, 4)
            norm_act(act, 8)
            moba_act(act)
            core_act(act, 1)
            split_first_act(act, 5)
            norm_act(act, 9, 5)
            split_u_act(act, 5, C - 1)
            ffn_act(act, 5)
            norm_act(act, 10)

        def dve_program(dve):
            steps = Steps(dve, dve_steps)
            nc.vector.memset(cvb[:, 0, 0:1], 0.0).then_inc(act_ready, CREDIT)
            angles_dve(dve, steps)
            norm_dve(dve, steps, 0)
            attn_in_dve(dve, steps)
            core_dve(dve, steps, 0)
            residual_dve(dve, steps, 0, False, "lin", 0)
            norm_dve(dve, steps, 1)
            split_u_dve(dve, 0, 0, C)
            dve.wait_ge(cond_ready, 1)
            ffn_dve(dve, steps, 0)
            norm_dve(dve, steps, 2)
            mods_dve(dve, 0)
            gdn_dve(dve, steps)
            residual_dve(dve, steps, 2, False, "acc", 1)
            norm_dve(dve, steps, 3)
            split_u_dve(dve, 1, 0, C)
            ffn_dve(dve, steps, 1, 2)
            norm_dve(dve, steps, 4, 2)
            split_u_dve(dve, 2, 4, C)
            mods_dve(dve, 1)
            ffn_dve(dve, steps, 2)
            norm_dve(dve, steps, 5)
            mods_dve(dve, 2)
            conv_dve(dve, steps)
            residual_dve(dve, steps, 5, True, "lin", 3)
            norm_dve(dve, steps, 6, 3)
            split_u_dve(dve, 3, 4, C)
            ffn_dve(dve, steps, 3, 4)
            norm_dve(dve, steps, 7, 4)
            split_u_dve(dve, 4, 4, C)
            mods_dve(dve, 3)
            ffn_dve(dve, steps, 4)
            norm_dve(dve, steps, 8)
            moba_dve(dve, steps)
            core_dve(dve, steps, 1)
            residual_dve(dve, steps, 8, True, "lin", 5)
            norm_dve(dve, steps, 9, 5)
            split_u_dve(dve, 5, 4, C)
            ffn_dve(dve, steps, 5)
            norm_dve(dve, steps, 10)

        def pool_program(pool):
            ffn_pool(pool, 0)
            gdn_pool(pool)
            for q in (1, 2, 3):
                ffn_pool(pool, q)
            ffn_pool(pool, 4)
            moba_pool(pool)
            ffn_pool(pool, 5)

        SMALL = [(cols[:], dram["cols"]), (consts[:], dram["consts"]), (positions[:], dram["positions"])]
        N_SMALL = len(SMALL)
        block = ctx.enter_context(nc.Block())

        @block.sync
        def _(sp):
            for dst, src in SMALL:
                sp.dma_start(dst, src).then_inc(small_loaded, 16)
            sp.dma_start(h[:], dram["x"]).then_inc(h_loaded, 16)
            for s in range(RING):
                sp.dma_start(ring[:, s], dram["w"][s]).then_inc(raw_ready[s], 16)
            def refill(n, turn=None):
                s, at = n % RING, n + RING
                q = next((q for q in range(len(FFN)) if 0 <= n - FIRST_UNIT[f"ffn{q}"] < 3 * FFN[q][1]), None)
                free, need = (unit_done, n // RING + 1) if q is None else (split_done, split_count(q, n - FIRST_UNIT[f"ffn{q}"]))
                if turn is not None:
                    need, at = need + turn, at + RING * turn
                sp.wait_ge(free[s], need)
                sp.dma_start(ring[:, s], dram["w"][at]).then_inc(raw_ready[s], 16)

            runs, at = [], 0
            for name, n in UNITS:
                kind = name.startswith("ffn")
                if runs and runs[-1][2] == kind:
                    runs[-1][1] += n
                else:
                    runs.append([at, n, kind])
                at += n
            for first, n, _ in runs:
                n = min(n, N_UNITS - RING - first)
                if n >= RING:
                    with sp.Fori(0, n // RING) as i:
                        for s in range(RING):
                            refill(first + s, i)
                for m in range(n - n % RING, n):
                    refill(first + m)
            sp.wait_ge(out_ready, 8)
            sp.dma_start(out_dram, u[:]).then_inc(out_done, 16)
            sp.wait_ge(out_done, 16)

        @block.gpsimd
        def _(pool):
            pool_program(pool)

        @block.tensor
        def _(pe):
            pe_program(pe)

        @block.scalar
        def _(act):
            act_program(act)

        @block.vector
        def _(dve):
            dve_program(dve)


def columns(a):
    a = np.ascontiguousarray(a).reshape(-1, P)
    return a.T


def by_output(w):
    k, n = w.shape
    return w.reshape(k // D, C, P, n // P, P).transpose(3, 0, 2, 1, 4).reshape(-1, P, D)


def by_row(w):
    return w.reshape(-1, P, D)


def ffn_units(gate, up, down):
    g, u, d = by_output(gate), by_output(up), by_row(down)
    nf = d.shape[0]
    order = [g[0], u[0]]
    for f in range(1, nf):
        order += [g[f], u[f], d[f - 1]]
    return order + [d[nf - 1]]


def weight_stream(x):
    heads = np.array([attn_tile_heads(j) for j in range(C)]).reshape(-1)
    q_cols = (heads[:, None] * HD + np.arange(HD)).reshape(-1)
    w = x["attn_w_in"][0]
    units = list(by_output(w[:, D:D + 256])) + list(by_output(w[:, :D][:, q_cols])) + list(by_output(w[:, D + 256:]))
    units += list(by_output(x["attn_w_out"][0][q_cols]))
    up = x["ffn_w_up"][0]
    units += ffn_units(up[:, :3072], up[:, 3072:], x["ffn_w_down"][0])
    w = x["gdn_w_in"][0]
    gates = np.zeros((D, P), w.dtype)
    gates[:, 0:16] = w[:, 6144:6160]
    gates[:, 32:48] = w[:, 6160:6176]
    units += list(by_output(gates))
    tiles = by_output(w[:, :6144])
    for i in range(GH // GB):
        units += [tiles[t] for t in gdn_turn_tiles(i)] + [tiles[32 + 4 * i + j] for j in range(4)]
    units += [w_ for half in (0, 1) for w_ in by_output(x["gdn_w_out"][0])[half::2]]
    up = x["ffn_w_up"][1]
    units += ffn_units(up[:, :3072], up[:, 3072:], x["ffn_w_down"][1])
    f2 = lambda l, s: ffn_units(x["ffn_w_gate_2"][l, s], x["ffn_w_up_2"][l, s], x["ffn_w_down_2"][l, s])
    units += f2(0, 0)
    t = by_output(x["conv_w_in_2"][0])
    units += [t[n] for j in range(4) for n in (j, 4 + j)] + [t[n] for j in range(4) for n in (12 + j, 16 + j, 8 + j)]
    units += list(by_output(x["conv_w_out_2"][0]))
    units += f2(0, 1) + f2(1, 0)
    units += list(by_output(x["pm_w_in_2"][0])) + list(by_output(x["pm_w_out_2"][0]))
    units += f2(1, 1)
    assert len(units) == N_UNITS
    return np.stack(units).reshape(N_UNITS, P, C, P)


def gdn_turn_tiles(i):
    return [2 * i, 2 * i + 1, 8 + 2 * i, 9 + 2 * i] + [16 + 4 * i + j for j in range(4)]


def packed_columns(x):
    out = np.zeros((P, N_COLS), np.float32)

    def put(name, a):
        out[:, COL[name]:COL[name] + a.shape[1]] = a

    put("mixer_norm", columns(x["mixer_norm"]))
    put("ffn_norm", columns(x["ffn_norm"]))
    put("q_gain", np.tile(x["attn_q_gain"][0], 2)[:, None])
    put("k_gain", np.tile(x["attn_k_gain"][0], 2)[:, None])
    taps = x["gdn_conv"][0].reshape(4, 32, P)
    order = [t for i in range(GH // GB) for t in gdn_turn_tiles(i)]
    put("gdn_conv", taps[:, order].transpose(2, 1, 0).reshape(P, 128))
    out[32:48, COL["a_log"]] = x["gdn_a_log"][0]
    out[32:48, COL["dt_bias"]] = x["gdn_dt_bias"][0]
    put("gdn_norm", x["gdn_norm"][0][:, None])
    fc = np.concatenate([x["ffn_conv"], x["ffn_conv_b"][:, None]], axis=1).reshape(2, 4, FF1, P)
    put("ffn_conv", fc.transpose(3, 0, 2, 1).reshape(P, -1))
    put("cond", columns(x["c_2"]))
    put("ada_b", columns(x["ada_b_2"]))
    put("ffn_norm_2", columns(x["ffn_norm_2"]))
    put("mix_norm", columns(x["mix_norm_2"]))
    put("conv_a_w", x["conv_a_w_2"][0].reshape(TAPS_A, 4, P).transpose(2, 0, 1).reshape(P, -1))
    put("conv_a_b", columns(x["conv_a_b_2"]))
    put("ln_g", columns(x["conv_a_ln_g_2"]))
    put("ln_b", columns(x["conv_a_ln_b_2"]))
    put("conv_b_w", x["conv_b_w_2"][0].reshape(3, 4, P).transpose(2, 1, 0).reshape(P, -1))
    put("pool_b", x["pool_b_2"][0].T)
    put("pool_scale", columns(x["pool_scale_2"]))
    put("final_norm", columns(x["final_norm_2"]))
    half = ROPE // 2
    freq = (np.float32(500000.0) ** (-np.arange(0, ROPE, 2, dtype=np.float32) / np.float32(ROPE))).astype(np.float32)
    for b in range(2):
        out[64 * b:64 * b + half, COL["inv_freq"]] = freq
        out[64 * b + half:64 * b + ROPE, COL["inv_freq"]] = freq
    sinks = x["attn_sinks"][0]
    put("sinks", np.broadcast_to(sinks[[hd for j in range(C) for hd in attn_tile_heads(j)]], (P, 16)))
    out[:, COL["eps"]] = EPS
    out[:, COL["half_pi"]] = np.pi / 2
    out[:, COL["one"]] = 1.0
    return out


def constant_matrices():
    out = np.zeros((P, N_CONST), np.float32)

    def put(name, a):
        out[:, CONST[name][0]:CONST[name][0] + a.shape[1]] = a

    i, j = np.arange(P)[:, None], np.arange(P)[None, :]
    put("ident", (i == j) * 1.0)
    put("ones", np.ones((P, P)))
    put("block_ones", (i // 64 == j // 64) * 1.0)
    rot = np.zeros((P, P))
    half = ROPE // 2
    for b in (0, 64):
        for m in range(half):
            rot[b + m + half, b + m] = -1.0
            rot[b + m, b + m + half] = 1.0
    put("rotate", rot)
    q = np.arange(P)[:, None]
    k = np.arange(T)[None, :]
    dist1 = P + q - k
    mask = np.concatenate([np.where(k[:, :P] <= q, 0.0, NEG), np.where((dist1 >= 0) & (dist1 < 128), 0.0, NEG)], axis=1)
    put("window_mask", mask)
    p, s = np.arange(P)[:, None] % 64, np.arange(64)[None, :]
    put("stack_ident", (p == s) * 1.0)
    put("level_lo", ((p // 2 == s // 2) & (p > s)) * 1.0)
    for lv in range(6):
        z = 2 ** lv
        a = CONST["level_up"][0] + 64 * lv
        out[:, a:a + 64] = (p // (2 * z) == s // (2 * z)) & (p // z % 2 == 0) & (s // z % 2 == 1)
    put("strict_lo_neg", np.where(s < p, 0.0, NEG))
    put("incl_up_neg", np.where(s >= p, 0.0, NEG))
    put("strict_up", (s > p) * 1.0)
    put("reset", np.broadcast_to((np.arange(T) % CH != 0) * 1.0, (P, T)))
    inv = np.stack([1.0 / np.minimum(np.arange(1, T + 1), w) for w in (2, 4, 8, 16)]).reshape(1, -1)
    put("pool_inv", np.broadcast_to(inv, (P, 4 * T)))
    return out


def alibi_matrices():
    q, k = np.arange(P)[:, None], np.arange(T)[None, :]
    slopes = 2.0 ** -(np.arange(8) + 1.0)
    out = np.zeros((P, 8, 384), np.float32)
    for n, slope in enumerate(slopes):
        d0, d1 = q - k[:, :P], P + q - k
        out[:, n, :P] = np.where(d0 >= 0, -slope * d0, NEG)
        out[:, n, P:] = np.where(d1 >= 0, -slope * d1, NEG)
    return out


def kernel(**inputs):
    import concourse.bacc as bacc
    from concourse.bass_utils import run_bass_kernel_spmd

    x = {k: np.asarray(v) for k, v in inputs.items()}
    ada = x["ada_w_2"].reshape(2, C, P, 18, PIECE).transpose(0, 3, 2, 1, 4).reshape(PIECES, P, C, PIECE)
    arrays = {
        "x": np.ascontiguousarray(x["x"][0].T.reshape(C, P, T).transpose(1, 0, 2)),
        "w": weight_stream(x),
        "ada": np.ascontiguousarray(ada),
        "cols": packed_columns(x),
        "consts": constant_matrices(),
        "alibi": alibi_matrices(),
        "pool_w": np.ascontiguousarray(x["pool_w_2"][0].transpose(1, 0, 2)),
        "positions": np.ascontiguousarray(np.broadcast_to(x["positions"], (P, T))),
    }
    nc = bacc.Bacc("TRN2", target_bir_lowering=False, num_devices=1)
    dram = {name: nc.dram_tensor(f"in_{name}", a.shape, mybir.dt.from_np(a.dtype), kind="ExternalInput").ap()
            for name, a in arrays.items()}
    out = nc.dram_tensor("out", (P, C, T), F32, kind="ExternalOutput").ap()
    build(nc, dram, out)
    r = run_bass_kernel_spmd(nc, [{f"in_{name}": a for name, a in arrays.items()}], core_ids=[0])
    got = r.results[0]["out"]
    return got.transpose(1, 0, 2).reshape(D, T).T.reshape(1, T, D)
```
